# Optimizing a Trainium2 kernel written in Bass

```python
import jax, jax.numpy as jnp
from jax import lax
import numpy as np
import math

D_MODEL = 1024
BATCH = 1
SEQ = 256
DEPTH = 2

GRID_W = 64
CTX_LEN = 256
N_EVEN = (DEPTH + 1) // 2
N_ODD = DEPTH // 2
HEAD_DIM = 64
ATTN_HEADS = 8
KV_HEADS = 2
GQA_GROUP = ATTN_HEADS // KV_HEADS
WINDOW = 128
ATTN_BLOCK = 128
ROPE_BASE = 10000.0
GMLP_GROUPS = 8
GMLP_DIM = 64
CHUNK = 128
Q_W = ATTN_HEADS * HEAD_DIM
KV_W = KV_HEADS * HEAD_DIM
A_W = GMLP_GROUPS * GMLP_DIM
IN_W = Q_W + 2 * KV_W + 2 * A_W
MIX_W = Q_W + A_W
POOL_WINDOWS = (2, 4, 8, 16)
POOL_GROUPS = 4
POOL_DIM = D_MODEL // POOL_GROUPS
PEER_HEADS = 8
PEER_NKEYS = 128
PEER_EXPERTS = PEER_NKEYS * PEER_NKEYS
PEER_TOPK = 16
PEER_DKEY = 256
PEER_DHALF = PEER_DKEY // 2
PEER_BLOCK = 128
N_MOD = 6
EPS = 1e-6


def rms_norm(x, g):
    xf = x.astype(jnp.float32)
    y = xf * lax.rsqrt(jnp.mean(jnp.square(xf), axis=-1, keepdims=True) + EPS)
    return (y * g).astype(x.dtype)

def axial_rope(t, row, col):
    half = HEAD_DIM // 2
    quarter = half // 2
    inv = jnp.power(ROPE_BASE, -jnp.arange(quarter, dtype=jnp.float32) / quarter)

    def rot(xa, pos):
        ang = pos[:, None] * inv[None, :]
        cos = jnp.cos(ang)[None, :, None, :]
        sin = jnp.sin(ang)[None, :, None, :]
        x1, x2 = xa[..., :quarter], xa[..., quarter:]
        return jnp.concatenate([x1 * cos - x2 * sin, x1 * sin + x2 * cos], axis=-1)

    tf = t.astype(jnp.float32)
    return jnp.concatenate([rot(tf[..., :half], row), rot(tf[..., half:], col)], axis=-1).astype(t.dtype)

def sink_softmax(logits, sink):
    sk = jnp.broadcast_to(sink.astype(jnp.float32).reshape(1, KV_HEADS, GQA_GROUP, 1, 1), logits.shape[:-1] + (1,))
    return jax.nn.softmax(jnp.concatenate([logits, sk], axis=-1), axis=-1)[..., :-1]

def window_attention(q, k, v, k_ctx, v_ctx, sink):
    B_, L_ = q.shape[0], q.shape[1]
    nb = L_ // ATTN_BLOCK
    span = ATTN_BLOCK + 2 * WINDOW
    scale = HEAD_DIM ** -0.5
    pad = ((0, 0), (WINDOW, WINDOW), (0, 0), (0, 0))
    kp = jnp.pad(k, pad)
    vp = jnp.pad(v, pad)
    qb = q.reshape(B_, nb, ATTN_BLOCK, KV_HEADS, GQA_GROUP, HEAD_DIM).swapaxes(0, 1)

    def one_block(args):
        n, qn = args
        start = n * ATTN_BLOCK
        kn = lax.dynamic_slice_in_dim(kp, start, span, axis=1)
        vn = lax.dynamic_slice_in_dim(vp, start, span, axis=1)
        qpos = start + jnp.arange(ATTN_BLOCK)
        kpos = start - WINDOW + jnp.arange(span)
        valid = (jnp.abs(qpos[:, None] - kpos[None, :]) <= WINDOW) & (kpos >= 0)[None, :] & (kpos < L_)[None, :]
        s_loc = jnp.einsum('bqhgd,bkhd->bhgqk', qn, kn).astype(jnp.float32) * scale
        s_loc = jnp.where(valid, s_loc, -jnp.inf)
        s_ctx = jnp.einsum('bqhgd,bkhd->bhgqk', qn, k_ctx).astype(jnp.float32) * scale
        p = sink_softmax(jnp.concatenate([s_loc, s_ctx], axis=-1), sink)
        o = (jnp.einsum('bhgqk,bkhd->bqhgd', p[..., :span], vn.astype(jnp.float32))
             + jnp.einsum('bhgqk,bkhd->bqhgd', p[..., span:], v_ctx.astype(jnp.float32)))
        return o.astype(q.dtype)

    out = lax.map(one_block, (jnp.arange(nb), qb))
    return out.swapaxes(0, 1).reshape(B_, L_, Q_W)

def context_attention(qc, kc, vc, sink):
    B_, C_ = qc.shape[0], qc.shape[1]
    qg = qc.reshape(B_, C_, KV_HEADS, GQA_GROUP, HEAD_DIM)
    s = jnp.einsum('bqhgd,bkhd->bhgqk', qg, kc).astype(jnp.float32) * (HEAD_DIM ** -0.5)
    p = sink_softmax(s, sink)
    o = jnp.einsum('bhgqk,bkhd->bqhgd', p, vc.astype(jnp.float32))
    return o.astype(qc.dtype).reshape(B_, C_, Q_W)

def chunk_gmlp(ua, va, w_s, b_s):
    B_, L_ = ua.shape[0], ua.shape[1]
    u = jax.nn.gelu(ua).reshape(B_, L_, GMLP_GROUPS, GMLP_DIM)
    vf = jax.nn.gelu(va).reshape(B_, L_, GMLP_GROUPS, GMLP_DIM).astype(jnp.float32)
    mu = jnp.mean(vf, axis=-1, keepdims=True)
    var = jnp.mean(jnp.square(vf - mu), axis=-1, keepdims=True)
    v = ((vf - mu) * lax.rsqrt(var + EPS)).astype(ua.dtype)
    vc = v.reshape(B_, L_ // CHUNK, CHUNK, GMLP_GROUPS, GMLP_DIM)
    mixed = jnp.einsum('gpq,bcqgd->bcpgd', w_s, vc) + b_s.T[:, :, None]
    return (u * mixed.reshape(B_, L_, GMLP_GROUPS, GMLP_DIM)).reshape(B_, L_, A_W)

def split_proj(p):
    return jnp.split(p, [Q_W, Q_W + KV_W, Q_W + 2 * KV_W, Q_W + 2 * KV_W + A_W], axis=-1)

def attn_gmlp_mixer(h, hc, w_in, w_out, sink, w_s, b_s, row, col, need_ctx_out):
    B_, L_ = h.shape[0], h.shape[1]
    C_ = hc.shape[1]
    q, k, v, ua, va = split_proj(h @ w_in)
    q = axial_rope(q.reshape(B_, L_, ATTN_HEADS, HEAD_DIM), row, col)
    k = axial_rope(k.reshape(B_, L_, KV_HEADS, HEAD_DIM), row, col)
    v = v.reshape(B_, L_, KV_HEADS, HEAD_DIM)
    if need_ctx_out:
        qc, kc, vc, uac, vac = split_proj(hc @ w_in)
    else:
        kc, vc = jnp.split(hc @ w_in[:, Q_W:Q_W + 2 * KV_W], 2, axis=-1)
    kc = kc.reshape(B_, C_, KV_HEADS, HEAD_DIM)
    vc = vc.reshape(B_, C_, KV_HEADS, HEAD_DIM)
    attn = window_attention(q, k, v, kc, vc, sink)
    mix = chunk_gmlp(ua, va, w_s, b_s)
    y = jnp.concatenate([attn, mix], axis=-1) @ w_out
    yc = None
    if need_ctx_out:
        attn_c = context_attention(qc.reshape(B_, C_, ATTN_HEADS, HEAD_DIM), kc, vc, sink)
        mix_c = chunk_gmlp(uac, vac, w_s, b_s)
        yc = jnp.concatenate([attn_c, mix_c], axis=-1) @ w_out
    return y, yc

def multiscale_pool(h, w_pool, scale):
    B_, L_ = h.shape[0], h.shape[1]
    hf = h.reshape(B_, L_, POOL_GROUPS, POOL_DIM).astype(jnp.float32)
    cs = jnp.pad(lax.cumsum(hf, axis=1), ((0, 0), (1, 0), (0, 0), (0, 0)))
    t = jnp.arange(L_)
    diffs = []
    for g, w in enumerate(POOL_WINDOWS):
        lo = jnp.clip(t - w // 2, 0, L_)
        hi = jnp.clip(t + w // 2, 0, L_)
        mean = (cs[:, hi, g] - cs[:, lo, g]) / (hi - lo).astype(jnp.float32)[None, :, None]
        diffs.append(mean - hf[:, :, g])
    pooled = jnp.stack(diffs, axis=2).astype(h.dtype)
    y = jnp.einsum('blgc,gce->blge', pooled, w_pool).reshape(B_, L_, D_MODEL)
    return y * scale

def peer_ffn(h, w_q, sub_keys, down, up):
    shape = h.shape
    blocks = h.reshape(-1, PEER_BLOCK, D_MODEL)

    def one_block(xb):
        n = xb.shape[0]
        q = (xb @ w_q).reshape(n, PEER_HEADS, 2, PEER_DHALF)
        s = jnp.einsum('thpk,pnk->thpn', q, sub_keys).astype(jnp.float32)
        s_top, i_top = lax.top_k(s, PEER_TOPK)
        cand_s = s_top[:, :, 0, :, None] + s_top[:, :, 1, None, :]
        cand_i = i_top[:, :, 0, :, None] * PEER_NKEYS + i_top[:, :, 1, None, :]
        best_s, best_pos = lax.top_k(cand_s.reshape(n, PEER_HEADS, -1), PEER_TOPK)
        idx = jnp.take_along_axis(cand_i.reshape(n, PEER_HEADS, -1), best_pos, axis=-1)
        gate = jax.nn.softmax(best_s, axis=-1)
        u = jnp.take(down, idx, axis=0)
        act = jax.nn.gelu(jnp.einsum('thkd,td->thk', u, xb))
        v = jnp.take(up, idx, axis=0)
        return jnp.einsum('thk,thkd->td', (gate * act).astype(v.dtype), v)

    return lax.map(one_block, blocks).reshape(shape)

def first_inputs(seed: int = 0) -> dict:
    key = jax.random.key(seed)
    ks = jax.random.split(key, 20)
    D = D_MODEL

    def nrm(k, shape, s):
        return jax.random.normal(k, shape, jnp.float32) * s

    return {
        'x': nrm(ks[0], (BATCH, SEQ, D), 1.0),
        'c': nrm(ks[1], (BATCH, D), 1.0),
        'ctx': nrm(ks[2], (BATCH, CTX_LEN, D), 1.0),
        'c_ctx': nrm(ks[3], (D,), 1.0),
        'mod_w': nrm(ks[4], (DEPTH, D, N_MOD * D), 0.5 * D ** -0.5),
        'mod_b': nrm(ks[5], (DEPTH, N_MOD * D), 0.02),
        'norm1_g': 1.0 + nrm(ks[6], (DEPTH, D), 0.02),
        'norm2_g': 1.0 + nrm(ks[7], (DEPTH, D), 0.02),
        'attn_in_w': nrm(ks[8], (N_EVEN, D, IN_W), D ** -0.5),
        'attn_out_w': nrm(ks[9], (N_EVEN, MIX_W, D), MIX_W ** -0.5),
        'attn_sink': nrm(ks[10], (N_EVEN, ATTN_HEADS), 0.5),
        'gmlp_w_s': nrm(ks[11], (N_EVEN, GMLP_GROUPS, CHUNK, CHUNK), CHUNK ** -0.5),
        'gmlp_b_s': 1.0 + nrm(ks[12], (N_EVEN, GMLP_GROUPS, CHUNK), 0.02),
        'pool_w': nrm(ks[13], (N_ODD, POOL_GROUPS, POOL_DIM, POOL_DIM), POOL_DIM ** -0.5),
        'pool_scale': 1.0 + nrm(ks[14], (N_ODD, D), 0.02),
        'peer_w_q': nrm(ks[15], (DEPTH, D, PEER_HEADS * PEER_DKEY), D ** -0.5),
        'peer_sub_keys': nrm(ks[16], (DEPTH, 2, PEER_NKEYS, PEER_DHALF), PEER_DHALF ** -0.5),
        'peer_down': nrm(ks[17], (DEPTH, PEER_EXPERTS, D), D ** -0.5),
        'peer_up': nrm(ks[18], (DEPTH, PEER_EXPERTS, D), 0.5),
        'final_g': 1.0 + nrm(ks[19], (D,), 0.02),
    }

def first_block(x, c, ctx, c_ctx, mod_w, mod_b, norm1_g, norm2_g, attn_in_w, attn_out_w, attn_sink,
              gmlp_w_s, gmlp_b_s, pool_w, pool_scale, peer_w_q, peer_sub_keys, peer_down, peer_up, final_g):
    L_ = x.shape[1]
    ROWS = L_ // GRID_W
    t = jnp.arange(ROWS * GRID_W)
    row = (t // GRID_W).astype(jnp.float32)
    col = (t % GRID_W).astype(jnp.float32)
    last_reader = ((DEPTH - 1) // 2) * 2
    xc = ctx
    for l in range(DEPTH):
        has_ctx = l <= last_reader
        keep_ctx = l < last_reader
        m = jax.nn.silu(c) @ mod_w[l] + mod_b[l]
        sh1, sc1, g1, sh2, sc2, g2 = jnp.split(m[:, None, :], N_MOD, axis=-1)
        h = rms_norm(x, norm1_g[l]) * (1.0 + sc1) + sh1
        hc = None
        if has_ctx:
            mc = jax.nn.silu(c_ctx) @ mod_w[l] + mod_b[l]
            csh1, csc1, cg1, csh2, csc2, cg2 = jnp.split(mc, N_MOD, axis=-1)
            hc = rms_norm(xc, norm1_g[l]) * (1.0 + csc1) + csh1
        if l % 2 == 0:
            e = l // 2
            y, yc = attn_gmlp_mixer(h, hc, attn_in_w[e], attn_out_w[e], attn_sink[e],
                                    gmlp_w_s[e], gmlp_b_s[e], row, col, keep_ctx)
        else:
            o = l // 2
            y = multiscale_pool(h, pool_w[o], pool_scale[o])
            yc = multiscale_pool(hc, pool_w[o], pool_scale[o]) if keep_ctx else None
        x = x + g1 * y
        h2 = rms_norm(x, norm2_g[l]) * (1.0 + sc2) + sh2
        x = x + g2 * peer_ffn(h2, peer_w_q[l], peer_sub_keys[l], peer_down[l], peer_up[l])
        if keep_ctx:
            xc = xc + cg1 * yc
            hc2 = rms_norm(xc, norm2_g[l]) * (1.0 + csc2) + csh2
            xc = xc + cg2 * peer_ffn(hc2, peer_w_q[l], peer_sub_keys[l], peer_down[l], peer_up[l])
    return rms_norm(x, final_g)


N_HEADS = D_MODEL // HEAD_DIM
SB_HEADS = N_HEADS // 4
DIL_HEADS = N_HEADS - SB_HEADS
DIL_PATTERNS = ((128, 1), (512, 4), (2048, 16))
DIL_GROUP_HEADS = DIL_HEADS // len(DIL_PATTERNS)
OUT_WIDTH = (SB_HEADS + DIL_GROUP_HEADS) * HEAD_DIM
BLOCK = 128
N_BUCKETS = 32
MAX_DISTANCE = 2048
D_FF = 2816
RWKV_HEAD = 64
RWKV_HEADS = D_MODEL // RWKV_HEAD
D_DECAY_LORA = 64
D_AAA_LORA = 64
D_GATE_LORA = 160
NORM_EPS = 1e-6
GN_EPS = 64e-5
NEG_INF = -1e30
N_EVEN_2 = (DEPTH + 1) // 2
N_ODD_2 = DEPTH // 2


def rms_norm_2(x, g, eps=NORM_EPS):
    x32 = x.astype(jnp.float32)
    y = x32 * lax.rsqrt(jnp.mean(x32 * x32, axis=-1, keepdims=True) + eps)
    return (y * g.astype(jnp.float32)).astype(x.dtype)

def swiglu(h, w_gate, w_up, w_down):
    return (jax.nn.silu(h @ w_gate) * (h @ w_up)) @ w_down

def t5_bucket(dist):
    max_exact = N_BUCKETS // 2
    d = jnp.maximum(dist, 1).astype(jnp.float32)
    large = max_exact + (jnp.log(d / max_exact) / math.log(MAX_DISTANCE / max_exact)
                         * (N_BUCKETS - max_exact)).astype(jnp.int32)
    large = jnp.minimum(large, N_BUCKETS - 1)
    return jnp.where(dist < max_exact, dist, large)

def stick_breaking_attention(q, k, v):
    B, S, H, Dh = q.shape
    nb = S // BLOCK
    scale = Dh ** -0.5
    qb = q.reshape(B, nb, BLOCK, H, Dh).transpose(1, 0, 3, 2, 4)
    kpos = jnp.arange(S)

    def one_block(args):
        qi, n = args
        z = jnp.einsum('bhqd,bshd->bhqs', qi, k).astype(jnp.float32) * scale
        qpos = n * BLOCK + jnp.arange(BLOCK)
        strict = kpos[None, :] < qpos[:, None]
        log_keep = jnp.where(strict, jax.nn.log_sigmoid(-z), 0.0)
        after = lax.cumsum(log_keep, axis=3, reverse=True) - log_keep
        weight = jnp.where(strict, jnp.exp(jax.nn.log_sigmoid(z) + after), 0.0)
        return jnp.einsum('bhqs,bshd->bqhd', weight.astype(v.dtype), v)

    out = lax.map(one_block, (qb, jnp.arange(nb)))
    return out.transpose(1, 0, 2, 3, 4).reshape(B, S, H, Dh)

def dilated_window_attention(q, k, v, bias_table, window, dilation):
    B, S, G, Dh = q.shape
    r = dilation
    L = S // r
    span = window // r
    nb = -(-L // BLOCK)
    Lp = nb * BLOCK

    def to_sub(t):
        t = t.reshape(B, L, r, G, Dh).transpose(0, 2, 1, 3, 4)
        t = jnp.pad(t, ((0, 0), (0, 0), (0, Lp - L), (0, 0), (0, 0)))
        return t.reshape(B, r, nb, BLOCK, G, Dh)

    def with_prev(t):
        prev = jnp.pad(t, ((0, 0), (0, 0), (1, 0), (0, 0), (0, 0), (0, 0)))[:, :, :-1]
        return jnp.concatenate([prev, t], axis=3)

    qs = to_sub(q)
    kw, vw = with_prev(to_sub(k)), with_prev(to_sub(v))
    logits = jnp.einsum('brnqgd,brnkgd->brngqk', qs, kw).astype(jnp.float32) * (Dh ** -0.5)
    qi = jnp.arange(BLOCK)[:, None]
    kj = jnp.arange(2 * BLOCK)[None, :] - BLOCK
    dist = qi - kj
    in_window = (dist >= 0) & (dist <= span)
    has_key = (jnp.arange(nb)[:, None, None] > 0) | (kj[None] >= 0)
    mask = (in_window[None] & has_key)[:, None]
    bias = bias_table[t5_bucket(jnp.maximum(dist, 0) * r)].astype(jnp.float32).transpose(2, 0, 1)
    logits = jnp.where(mask, logits + bias, NEG_INF)
    m = jnp.max(logits, axis=-1, keepdims=True)
    p = jnp.exp(logits - m)
    den = jnp.sum(p, axis=-1, keepdims=True)
    o = jnp.einsum('brngqk,brnkgd->brnqgd', (p / den).astype(v.dtype), vw)
    lse = (m + jnp.log(den))[..., 0].transpose(0, 1, 2, 4, 3)

    def from_sub(t):
        t = t.reshape((B, r, Lp) + t.shape[4:])[:, :, :L]
        return jnp.swapaxes(t, 1, 2).reshape((B, S) + t.shape[3:])

    return from_sub(o), from_sub(lse)

def parallel_attention_mixer(h, w_in, q_norm, k_norm, w_out, rel_bias):
    B, S, _ = h.shape
    proj = h @ w_in
    a_cols = 3 * SB_HEADS * HEAD_DIM
    sb = proj[..., :a_cols].reshape(B, S, 3, SB_HEADS, HEAD_DIM)
    dl = proj[..., a_cols:].reshape(B, S, 3, DIL_HEADS, HEAD_DIM)
    out_a = stick_breaking_attention(sb[:, :, 0], sb[:, :, 1], sb[:, :, 2])
    q = rms_norm_2(dl[:, :, 0], q_norm)
    k = rms_norm_2(dl[:, :, 1], k_norm)
    v = dl[:, :, 2]
    outs, lses = [], []
    for g, (window, dilation) in enumerate(DIL_PATTERNS):
        sl = slice(g * DIL_GROUP_HEADS, (g + 1) * DIL_GROUP_HEADS)
        o, l = dilated_window_attention(q[:, :, sl], k[:, :, sl], v[:, :, sl],
                                        rel_bias[:, sl], window, dilation)
        outs.append(o)
        lses.append(l)
    alpha = jax.nn.softmax(jnp.stack(lses, axis=0), axis=0)
    out_b = jnp.sum(alpha[..., None].astype(v.dtype) * jnp.stack(outs, axis=0), axis=0)
    merged = jnp.concatenate([out_a.reshape(B, S, -1), out_b.reshape(B, S, -1)], axis=-1)
    return merged @ w_out

def rwkv7_step(state, inp):
    r_t, w_t, k_t, v_t, a_t, b_t = inp
    sa = jnp.einsum('bhvk,bhk->bhv', state, a_t)
    state = (state * w_t[:, :, None, :] + sa[..., None] * b_t[:, :, None, :]
             + v_t[..., None] * k_t[:, :, None, :])
    return state, jnp.einsum('bhvk,bhk->bhv', state, r_t)

def rwkv7_time_mix(h, mix, w0, w1, w2, a0, a1, a2, g1, g2, k_k, k_a, r_k,
                   w_r, w_k, w_v, w_o, lnx_g, lnx_b):
    B, S, D = h.shape
    H, N = RWKV_HEADS, RWKV_HEAD
    f32 = jnp.float32
    xx = jnp.pad(h, ((0, 0), (1, 0), (0, 0)))[:, :-1] - h
    xr, xw, xk, xv, xa, xg = [h + xx * mix[i] for i in range(6)]
    r = (xr @ w_r).astype(f32)
    k = (xk @ w_k).astype(f32)
    v = (xv @ w_v).astype(f32)
    w_log = -jax.nn.softplus(-(w0 + jnp.tanh(xw @ w1) @ w2).astype(f32)) - 0.5
    decay = jnp.exp(-jnp.exp(w_log))
    a = jax.nn.sigmoid((a0 + (xa @ a1) @ a2).astype(f32))
    g = jax.nn.sigmoid(xg @ g1) @ g2
    heads = lambda t: t.reshape(B, S, H, N)
    kk = heads(k * k_k.astype(f32))
    kk = kk / jnp.maximum(jnp.sqrt(jnp.sum(kk * kk, axis=-1, keepdims=True)), 1e-12)
    k = k * (1.0 + (a - 1.0) * k_a.astype(f32))
    r_h, k_h, v_h, a_h, w_h = heads(r), heads(k), heads(v), heads(a), heads(decay)
    tm = lambda t: jnp.swapaxes(t, 0, 1)
    seqs = (tm(r_h), tm(w_h), tm(k_h), tm(v_h), tm(-kk), tm(kk * a_h))
    _, y = lax.scan(rwkv7_step, jnp.zeros((B, H, N, N), f32), seqs)
    y = jnp.swapaxes(y, 0, 1)
    mu = jnp.mean(y, axis=-1, keepdims=True)
    var = jnp.mean(jnp.square(y - mu), axis=-1, keepdims=True)
    y = ((y - mu) * lax.rsqrt(var + GN_EPS)).reshape(B, S, D)
    y = y * lnx_g.astype(f32) + lnx_b.astype(f32)
    y = y + (jnp.sum(r_h * k_h * r_k.astype(f32), axis=-1, keepdims=True) * v_h).reshape(B, S, D)
    return (y.astype(h.dtype) * g) @ w_o

def second_inputs(seed: int = 0) -> dict:
    key = jax.random.key(seed)
    ks = iter(jax.random.split(key, 48))
    D = D_MODEL
    nrm = lambda shape, scale: jax.random.normal(next(ks), shape, jnp.float32) * scale
    uni = lambda shape, lo, hi: jax.random.uniform(next(ks), shape, jnp.float32, lo, hi)
    return {
        "x": nrm((BATCH, SEQ, D), 1.0),
        "ffn_norm": 1.0 + nrm((DEPTH, 2, D), 0.05),
        "ffn_w_gate": nrm((DEPTH, 2, D, D_FF), D ** -0.5),
        "ffn_w_up": nrm((DEPTH, 2, D, D_FF), D ** -0.5),
        "ffn_w_down": nrm((DEPTH, 2, D_FF, D), D_FF ** -0.5),
        "mix_norm": 1.0 + nrm((DEPTH, D), 0.05),
        "rel_bias": nrm((N_BUCKETS, DIL_HEADS), 0.3),
        "attn_w_in": nrm((N_EVEN_2, D, 3 * N_HEADS * HEAD_DIM), D ** -0.5),
        "attn_q_norm": 1.0 + nrm((N_EVEN_2, HEAD_DIM), 0.05),
        "attn_k_norm": 1.0 + nrm((N_EVEN_2, HEAD_DIM), 0.05),
        "attn_w_out": nrm((N_EVEN_2, OUT_WIDTH, D), OUT_WIDTH ** -0.5),
        "rw_mix": uni((N_ODD_2, 6, D), 0.0, 1.0),
        "rw_w0": uni((N_ODD_2, D), -4.0, 0.0),
        "rw_w1": nrm((N_ODD_2, D, D_DECAY_LORA), D ** -0.5),
        "rw_w2": nrm((N_ODD_2, D_DECAY_LORA, D), 0.1 * D_DECAY_LORA ** -0.5),
        "rw_a0": nrm((N_ODD_2, D), 0.1),
        "rw_a1": nrm((N_ODD_2, D, D_AAA_LORA), D ** -0.5),
        "rw_a2": nrm((N_ODD_2, D_AAA_LORA, D), 0.1 * D_AAA_LORA ** -0.5),
        "rw_g1": nrm((N_ODD_2, D, D_GATE_LORA), D ** -0.5),
        "rw_g2": nrm((N_ODD_2, D_GATE_LORA, D), D_GATE_LORA ** -0.5),
        "rw_kk": 0.85 + nrm((N_ODD_2, D), 0.05),
        "rw_ka": 1.0 + nrm((N_ODD_2, D), 0.05),
        "rw_rk": nrm((N_ODD_2, RWKV_HEADS, RWKV_HEAD), 0.1),
        "rw_wr": nrm((N_ODD_2, D, D), D ** -0.5),
        "rw_wk": nrm((N_ODD_2, D, D), D ** -0.5),
        "rw_wv": nrm((N_ODD_2, D, D), D ** -0.5),
        "rw_wo": nrm((N_ODD_2, D, D), D ** -0.5),
        "rw_lnx_g": 1.0 + nrm((N_ODD_2, D), 0.05),
        "rw_lnx_b": nrm((N_ODD_2, D), 0.01),
    }

def second_block(x, ffn_norm, ffn_w_gate, ffn_w_up, ffn_w_down, mix_norm, rel_bias,
              attn_w_in, attn_q_norm, attn_k_norm, attn_w_out,
              rw_mix, rw_w0, rw_w1, rw_w2, rw_a0, rw_a1, rw_a2, rw_g1, rw_g2,
              rw_kk, rw_ka, rw_rk, rw_wr, rw_wk, rw_wv, rw_wo, rw_lnx_g, rw_lnx_b):
    for layer in range(DEPTH):
        x = x + 0.5 * swiglu(rms_norm_2(x, ffn_norm[layer, 0]), ffn_w_gate[layer, 0],
                             ffn_w_up[layer, 0], ffn_w_down[layer, 0])
        h = rms_norm_2(x, mix_norm[layer])
        if layer % 2 == 0:
            e = layer // 2
            x = x + parallel_attention_mixer(h, attn_w_in[e], attn_q_norm[e], attn_k_norm[e],
                                             attn_w_out[e], rel_bias)
        else:
            o = layer // 2
            x = x + rwkv7_time_mix(h, rw_mix[o], rw_w0[o], rw_w1[o], rw_w2[o], rw_a0[o],
                                   rw_a1[o], rw_a2[o], rw_g1[o], rw_g2[o], rw_kk[o], rw_ka[o],
                                   rw_rk[o], rw_wr[o], rw_wk[o], rw_wv[o], rw_wo[o],
                                   rw_lnx_g[o], rw_lnx_b[o])
        x = x + 0.5 * swiglu(rms_norm_2(x, ffn_norm[layer, 1]), ffn_w_gate[layer, 1],
                             ffn_w_up[layer, 1], ffn_w_down[layer, 1])
    return x


def setup_inputs(seed=0):
    out = dict(first_inputs(seed))
    for name, value in second_inputs(seed + 1).items():
        if name != "x":
            out[name + "_2"] = value
    return out


def reference(
    x, c, ctx, c_ctx, mod_w, mod_b, norm1_g, norm2_g, attn_in_w, attn_out_w, attn_sink,
    gmlp_w_s, gmlp_b_s, pool_w, pool_scale, peer_w_q, peer_sub_keys, peer_down, peer_up,
    final_g, ffn_norm_2, ffn_w_gate_2, ffn_w_up_2, ffn_w_down_2, mix_norm_2, rel_bias_2,
    attn_w_in_2, attn_q_norm_2, attn_k_norm_2, attn_w_out_2, rw_mix_2, rw_w0_2, rw_w1_2,
    rw_w2_2, rw_a0_2, rw_a1_2, rw_a2_2, rw_g1_2, rw_g2_2, rw_kk_2, rw_ka_2, rw_rk_2, rw_wr_2,
    rw_wk_2, rw_wv_2, rw_wo_2, rw_lnx_g_2, rw_lnx_b_2,
):
    x = first_block(
        x, c, ctx, c_ctx, mod_w, mod_b, norm1_g, norm2_g, attn_in_w, attn_out_w, attn_sink,
        gmlp_w_s, gmlp_b_s, pool_w, pool_scale, peer_w_q, peer_sub_keys, peer_down, peer_up,
        final_g,
    )
    return second_block(
        x, ffn_norm_2, ffn_w_gate_2, ffn_w_up_2, ffn_w_down_2, mix_norm_2, rel_bias_2,
        attn_w_in_2, attn_q_norm_2, attn_k_norm_2, attn_w_out_2, rw_mix_2, rw_w0_2, rw_w1_2,
        rw_w2_2, rw_a0_2, rw_a1_2, rw_a2_2, rw_g1_2, rw_g2_2, rw_kk_2, rw_ka_2, rw_rk_2,
        rw_wr_2, rw_wk_2, rw_wv_2, rw_wo_2, rw_lnx_g_2, rw_lnx_b_2,
    )


_drawn_inputs = setup_inputs


def setup_inputs(seed=0):
    import zlib

    import numpy as np

    out = dict(_drawn_inputs(seed))
    spreads = {}
    factors = {'norm1_g': 3.052,
     'attn_sink': 64.0,
     'gmlp_b_s': 4.895,
     'pool_scale': 5.198,
     'attn_q_norm_2': 8.0,
     'attn_k_norm_2': 8.0,
     'rw_w1_2': 8.0,
     'rw_w2_2': 8.0,
     'rw_a0_2': 2.88,
     'rw_a1_2': 3.211,
     'rw_a2_2': 3.201,
     'rw_kk_2': 28.752,
     'rw_lnx_b_2': 23.297,
     'rw_lnx_g_2': 2.943}
    for name, (base, spread) in spreads.items():
        noise = np.random.default_rng([zlib.crc32(name.encode()), seed]).standard_normal(out[name].shape)
        drawn = base * np.exp(spread * noise) if base else spread * noise
        out[name] = __import__('jax').numpy.asarray(drawn.astype(out[name].dtype))
    for name, factor in factors.items():
        out[name] = (out[name] * factor).astype(out[name].dtype)
    return out
```

```python
import numpy as np
import concourse.bass as bass
from concourse import mybir

F32 = mybir.dt.float32
U32 = mybir.dt.uint32
ALU = mybir.AluOpType
ACT = mybir.ActivationFunctionType
AX = mybir.AxisListType.X

P = 128
SEQ = 256
NT = SEQ // P
D = 1024
KD = D // P
EPS = 1e-6
GN_EPS = 64e-5
NEG = -1e30
HD = 64
SCALE = HD ** -0.5

N_MOD = 6
Q_W, KV_W, A_W = 512, 128, 512
HEADS, GQA = 8, 4
GROUPS = 8
POOL_WINDOWS = (2, 4, 8, 16)

PH = 8
NKEYS = 128
TOPK = 16
PICKS = PH * TOPK

D_FF = 2816
BLK = 256
FF_BLOCKS = D_FF // BLK

SB_HEADS, DIL_HEADS, DIL_GROUPS, GROUP_HEADS = 4, 12, 3, 4
DIL_PATTERNS = ((128, 1), (512, 4), (2048, 16))
N_BUCKETS, MAX_DISTANCE = 32, 2048

RH = 16
C = 32
CH = P // C

SLOTS = 6
GRING = 8

CONST_PARTS = [("ident", P), ("after", P), ("lt", P), ("le", P), ("ends", CH), ("iota16", 16),
               ("strict", NT * SEQ), ("window", NT * 512), ("cos", NT * HD), ("sin", NT * HD)]


def layout_constants():
    t = np.arange(SEQ)
    pi = np.arange(P)
    same = (pi[:, None] // C) == (pi[None, :] // C)
    quarter = HD // 4
    inv = np.power(np.float32(10000.0), -np.arange(quarter, dtype=np.float32) / np.float32(quarter))
    row, col = (t // 64).astype(np.float32), (t % 64).astype(np.float32)
    ar, ac = row[:, None] * inv[None, :], col[:, None] * inv[None, :]
    cos = np.concatenate([np.cos(ar), np.cos(ar), np.cos(ac), np.cos(ac)], 1)
    sin = np.concatenate([-np.sin(ar), np.sin(ar), -np.sin(ac), np.sin(ac)], 1)
    window = np.zeros((SEQ, 512), np.float32)
    window[:, :SEQ] = np.where(np.abs(t[:, None] - t[None, :]) <= 128, 0.0, NEG)

    def tiles(a):
        return a.reshape(NT, P, -1).transpose(1, 0, 2).reshape(P, -1)

    parts = {
        "ident": np.eye(P), "after": (pi[:, None] > pi[None, :]),
        "lt": same & (pi[:, None] < pi[None, :]), "le": same & (pi[:, None] <= pi[None, :]),
        "ends": (pi[:, None] // C) == np.arange(CH)[None, :],
        "iota16": np.broadcast_to(np.arange(16), (P, 16)),
        "strict": tiles((t[:, None] < t[None, :]).astype(np.float32)),
        "window": tiles(window), "cos": tiles(cos), "sin": tiles(sin),
    }
    consts = np.concatenate([np.asarray(parts[n], np.float32) for n, _ in CONST_PARTS], 1)
    bands = np.zeros((len(POOL_WINDOWS), SEQ, SEQ), np.float32)
    for g, w in enumerate(POOL_WINDOWS):
        lo, hi = np.clip(t - w // 2, 0, SEQ), np.clip(t + w // 2, 0, SEQ)
        inside = (t[:, None] >= lo[None, :]) & (t[:, None] < hi[None, :])
        bands[g] = inside / (hi - lo).astype(np.float32)[None, :] - np.eye(SEQ)
    dist = np.arange(512) - (SEQ - 1)
    half = N_BUCKETS // 2
    large = half + (np.log(np.maximum(dist, 1).astype(np.float32) / half) / np.log(MAX_DISTANCE / half)
                    * (N_BUCKETS - half)).astype(np.int32)
    bucket = np.where(dist < half, dist, np.minimum(large, N_BUCKETS - 1))
    onehot = np.zeros((N_BUCKETS + 1, DIL_GROUPS, 512), np.float32)
    for g, (w, r) in enumerate(DIL_PATTERNS):
        ok = (dist >= 0) & (dist % r == 0) & (dist <= w)
        for j in range(512):
            if ok[j]:
                onehot[bucket[j], g, j] = 1.0 / SCALE
            else:
                onehot[N_BUCKETS, g, j] = 1.0
    return {"consts": np.ascontiguousarray(consts), "bands": bands, "onehot": onehot}


class Count:

    def __init__(self, nc, name):
        self.sem, self.n = nc.alloc_semaphore(name), 0

    def up(self, ins, by=1):
        ins.then_inc(self.sem, by)
        self.n += by
        return self.n


class Kit:

    def __init__(self, nc, dram):
        self.nc, self.dram, self.counts, self.taken = nc, dram, {}, 0
        self.bank = [nc.alloc_psum_tensor(f"bank{i}", [P, 512], F32) for i in range(8)]
        self.step = {e: Count(nc, f"{e}_step") for e in ("dve", "act", "pool")}

    def count(self, name):
        if name not in self.counts:
            self.counts[name] = Count(self.nc, name)
        return self.counts[name]

    def sb(self, name, shape, dt=F32):
        self.taken += 1
        return self.nc.sbuf_tensor(f"{name}_{self.taken}", shape, dt)

    def dve(self, ins):
        self.nc.vector.wait_ge(self.step["dve"].sem, self.step["dve"].up(ins))

    def act(self, ins):
        self.nc.scalar.wait_ge(self.step["act"].sem, self.step["act"].up(ins))

    def roots(self, act, jobs):
        ready, made = self.count("variance_ready"), self.count("root_made")
        for i, (dst, src) in enumerate(jobs):
            act.wait_ge(ready.sem, made.n + 1)
            made.up(self.nc.scalar.activation(dst, src, ACT.Sqrt))

    def rsqrt(self, dve, ins, dst, src):
        n = self.count("variance_ready").up(ins)
        dve.wait_ge(self.count("root_made").sem, n)
        self.dve(self.nc.vector.reciprocal(dst, src))

    def load(self, eng, dst, src, slow=False):
        self.count("loaded").up(eng.dma_start(dst, src, allow_slow_non_contiguous=slow), 16)


class Weights:

    def __init__(self, kit):
        nc = kit.nc
        self.ring = nc.alloc_sbuf_tensor("weight_ring", [P, SLOTS, 2048], F32)
        self.landed = [nc.alloc_semaphore(f"block_landed{i}") for i in range(SLOTS)]
        self.multiplied = nc.alloc_semaphore("block_multiplied")
        self.blocks, self.issued, self.used = [], 0, 0

    def add(self, srcs):
        self.blocks += srcs

    def tile(self, b, kc):
        return self.ring[:, b % SLOTS, :].rearrange("p (k n) -> p k n", k=kc)

    def issue(self, sp, upto):
        for b in range(self.issued, min(upto, len(self.blocks))):
            if b >= SLOTS:
                sp.wait_ge(self.multiplied, b - SLOTS + 1)
            src = self.blocks[b]
            sp.dma_start(self.tile(b, src.shape[1]), src).then_inc(self.landed[b % SLOTS], 16)
        self.issued = max(self.issued, min(upto, len(self.blocks)))

    def wait(self, pe, b):
        pe.wait_ge(self.landed[b % SLOTS], 16 * (b // SLOTS + 1))


def bcast(row, n):
    return row.partition_broadcast(P).rearrange("p a n -> p (a n)")


def columns(w):
    v = w.rearrange("(k p) n -> p k n", p=P)
    return [v[:, :, b * BLK:(b + 1) * BLK] for b in range(w.shape[1] // BLK)]



def transposes(kit, jobs):
    nc = kit.nc
    turned, freed = kit.count("turned"), [kit.count("turned_out_act"), kit.count("turned_out_dve")]
    b0, f0 = turned.n, [f.n for f in freed]
    with nc.Block() as block:
        @block.tensor
        def _(pe):
            for j, (ins, _) in enumerate(jobs):
                if j >= 4:
                    pe.wait_ge(freed[j % 2].sem, f0[j % 2] + (j - 4) // 2 + 1)
                n = ins[0].shape[0]
                for i, a in enumerate(ins):
                    mm = nc.tensor.transpose(kit.bank[j % 4][:, i * n:(i + 1) * n], a, kit.ident[0:n, 0:n])
                turned.up(mm)

        def source(j):
            n, t = len(jobs[j][0]), jobs[j][0][0].shape[0]
            return kit.bank[j % 4][:, 0:n * t].rearrange("p (n t) -> p n t", n=n)

        @block.scalar
        def _(act):
            for j in range(0, len(jobs), 2):
                act.wait_ge(turned.sem, b0 + j + 1)
                freed[0].up(nc.scalar.copy(jobs[j][1], source(j)))

        @block.vector
        def _(dve):
            for j in range(1, len(jobs), 2):
                dve.wait_ge(turned.sem, b0 + j + 1)
                freed[1].up(nc.vector.tensor_copy(jobs[j][1], source(j)))


def transpose_tokens(kit, src, dstT, kc=KD):
    jobs = []
    for T in range(NT):
        for k in range(0, kc, 4):
            jobs.append(([src[:, T, (k + i) * P:(k + i + 1) * P] for i in range(4)],
                         dstT[:, k:k + 4, T * P:(T + 1) * P]))
    transposes(kit, jobs)


def norm(kit, x, gain, shift, out, load=()):
    nc = kit.nc
    squares, loaded = kit.count("squares_summed"), kit.count("loaded")
    s0, l0 = squares.n, loaded.n
    with kit.sb("ss", [P, 8]) as ss, kit.sb("junk", [P, D]) as junk, nc.Block() as block:
        @block.sync
        def _(sp):
            for dst, src in load:
                kit.load(sp, dst, src)

        @block.scalar
        def _(act):
            for T in range(NT):
                kit.act(nc.scalar.activation(junk[:], x[:, T], ACT.Square, accum_out=ss[:, T:T + 1]))
            squares.up(nc.scalar.activation(ss[:, 4:4 + NT], ss[:, 0:NT], ACT.Sqrt, scale=1.0 / D, bias=kit.eps))

        @block.vector
        def _(dve):
            dve.wait_ge(squares.sem, s0 + 1)
            if load:
                dve.wait_ge(loaded.sem, l0 + 16 * len(load))
            kit.dve(nc.vector.reciprocal(ss[:, 6:6 + NT], ss[:, 4:4 + NT]))
            for T in range(NT):
                ins = nc.vector.scalar_tensor_tensor(out=out[:, T], in0=x[:, T], scalar=ss[:, 6 + T:7 + T],
                                                     in1=gain, op0=ALU.mult, op1=ALU.mult)
                if shift is not None:
                    kit.dve(ins)
                    nc.vector.tensor_tensor(out[:, T], out[:, T], shift, ALU.add)


def norm_modulated(kit, x, g_row, scale, shift, out):
    nc = kit.nc
    loaded = kit.count("loaded")
    l0 = loaded.n
    with kit.sb("gain", [P, D]) as gain:
        with nc.Block() as block:
            @block.sync
            def _(sp):
                kit.load(sp, gain[:], bcast(g_row, D))

            @block.vector
            def _(dve):
                dve.wait_ge(loaded.sem, l0 + 16)
                nc.vector.scalar_tensor_tensor(out=gain[:], in0=scale, scalar=1.0, in1=gain[:],
                                               op0=ALU.add, op1=ALU.mult)
        norm(kit, x, gain[:], shift, out)


def norm_plain(kit, x, g_row, out):
    with kit.sb("gain", [P, D]) as gain:
        norm(kit, x, gain[:], None, out, load=[(gain[:], bcast(g_row, D))])


def linear(kit, xT, nblocks, transposed, evacuate, on_dve=False, kc=KD, extra=None, lhs_of=None, extra_evacuate=None):
    nc, W = kit.nc, kit.weights
    b0 = W.used
    emptied = kit.count("bank_emptied")
    e0 = emptied.n
    extra_done = kit.count("extra_multiplied")
    x0 = extra_done.n
    with nc.Block() as block:
        @block.sync
        def _(sp):
            W.issue(sp, b0 + nblocks + SLOTS)

        @block.tensor
        def _(pe):
            for b in range(nblocks):
                w = W.tile(b0 + b, kc)
                W.wait(pe, b0 + b)
                if b >= 4:
                    pe.wait_ge(emptied.sem, e0 + b - 3)
                if lhs_of is not None:
                    xin = lhs_of(pe, b)
                else:
                    xin = xT
                if extra is not None and extra[0] == b:
                    for T in range(NT):
                        for k in range(kc):
                            mm = nc.tensor.matmul(kit.bank[4][:, T * BLK:(T + 1) * BLK], extra[1][:, k, T * P:(T + 1) * P],
                                                  w[:, k, :], start=(k == 0), stop=(k == kc - 1))
                    extra_done.up(mm)
                for half in range(2):
                    for k in range(kc):
                        o = kit.bank[b % 4][:, half * BLK:(half + 1) * BLK]
                        if transposed:
                            mm = nc.tensor.matmul(o, w[:, k, half * P:(half + 1) * P], xin[:, k, :],
                                                  start=(k == 0), stop=(k == kc - 1))
                        else:
                            mm = nc.tensor.matmul(o, xin[:, k, half * P:(half + 1) * P], w[:, k, :],
                                                  start=(k == 0), stop=(k == kc - 1))
                mm.then_inc(W.multiplied, 1)

        def empty(eng):
            if extra is not None:
                eng.wait_ge(extra_done.sem, x0 + 1)
                extra_evacuate(kit.bank[4][:, :].rearrange("p (t n) -> p t n", t=2))
            for b in range(nblocks):
                eng.wait_ge(W.multiplied, b0 + b + 1)
                if on_dve and b:
                    eng.wait_ge(emptied.sem, e0 + b)
                emptied.up(evacuate(b, kit.bank[b % 4][:, :].rearrange("p (t n) -> p t n", t=2)))

        if on_dve:
            @block.vector
            def _(dve):
                empty(dve)
        else:
            @block.scalar
            def _(act):
                empty(act)
    W.used += nblocks


def add_gated(kit, x, tmp, gate):
    nc = kit.nc

    def evacuate(b, bank):
        cols = slice(b * BLK, (b + 1) * BLK)
        g = gate[:, cols].unsqueeze(1).to_broadcast([P, NT, BLK])
        kit.dve(nc.vector.tensor_tensor(tmp[:], bank, g, ALU.mult))
        return nc.vector.tensor_tensor(x[:, :, cols], x[:, :, cols], tmp[:], ALU.add)
    return evacuate


def copy_out(kit, dst):
    def evacuate(b, bank):
        return kit.nc.scalar.copy(dst[:, :, b * BLK:(b + 1) * BLK], bank)
    return evacuate



def load_constants(kit, dram):
    nc = kit.nc
    loaded = kit.count("loaded")
    with nc.Block() as block:
        @block.sync
        def _(sp):
            kit.load(sp, kit.consts[:], dram["consts"])
            kit.load(sp, kit.x[:], dram["x"].rearrange("a (t p) d -> p (a t) d", p=P))
            kit.weights.issue(sp, SLOTS)
            sp.wait_ge(loaded.sem, 32)

        @block.vector
        def _(dve):
            nc.vector.memset(kit.ones[:], 1.0)
            nc.vector.memset(kit.zeros[:], 0.0)
            nc.vector.memset(kit.eps, EPS)
            for s in range(GRING):
                kit.count("row_slots_freed").up(nc.vector.memset(kit.spare[:, s:s + 1], 0.0))
            dve.wait_ge(kit.count("row_slots_freed").sem, GRING)
            kit.count("dots_copied").up(nc.vector.memset(kit.spare[:, 0:1], 0.0))


def modulation(kit, dram, layer, mod, mod_ctx):
    nc, W = kit.nc, kit.weights
    b0 = W.used
    nb = N_MOD * D // BLK
    ctx_blocks = 2 * D // BLK if mod_ctx is not None else 0
    peeled = 2 * SLOTS if mod_ctx is not None else 0
    rounds = (nb - peeled) // SLOTS
    names = ("c", "c_ctx") if mod_ctx is not None else ("c",)
    loaded, ready = kit.count("loaded"), kit.count("mod_input_ready")
    emptied, ctx_emptied, ctx_done = kit.count("mod_emptied"), kit.count("mod_ctx_emptied"), kit.count("mod_ctx_done")
    l0, r0, e0, c0, d0 = loaded.n, ready.n, emptied.n, ctx_emptied.n, ctx_done.n
    with kit.sb("ccol", [P, 2, KD]) as ccol, kit.sb("cwide", [P, 2, KD, P]) as cwide, \
            kit.sb("mod_b_row", [1, N_MOD * D]) as brow, nc.Block() as block:
        @block.sync
        def _(sp):
            W.issue(sp, b0 + max(peeled, SLOTS))
            done = max(peeled, SLOTS)
            n = (nb - done) // SLOTS
            v = dram["mod_w"][layer].rearrange("(k p) n -> p k n", p=P)
            with sp.Fori(0, n) as i:
                for u in range(SLOTS):
                    b = b0 + done + u
                    sp.wait_ge(W.multiplied, i * SLOTS + (b - SLOTS + 1))
                    sp.dma_start(W.tile(b, KD), v[:, :, bass.ds(i * (SLOTS * BLK) + (done + u) * BLK, BLK)]) \
                        .then_inc(W.landed[b % SLOTS], 16)
            W.issued = b0 + nb
            W.issue(sp, b0 + nb + SLOTS)

        @block.vector
        def _(dve):
            dve.wait_ge(ready.sem, r0 + 1)
            for n in range(len(names)):
                ready.up(nc.vector.tensor_copy(cwide[:, n], ccol[:, n].unsqueeze(2).to_broadcast([P, KD, P])))

        @block.tensor
        def _(pe):
            pe.wait_ge(ready.sem, r0 + 1 + len(names))

            def one(u, slot, bias_cols, ctx=False):
                dst = kit.bank[6 + u % 2] if ctx else kit.bank[u]
                n = 1 if ctx else 0
                nc.tensor.matmul(dst[:, 0:BLK], kit.ones[0:1, :], brow[0:1, bias_cols], start=True, stop=False)
                for k in range(KD):
                    mm = nc.tensor.matmul(dst[:, 0:BLK], cwide[:, n, k, :], W.tile(slot, KD)[:, k, :],
                                          start=False, stop=(k == KD - 1))
                return mm

            for b in range(peeled):
                W.wait(pe, b0 + b)
                if b < ctx_blocks:
                    if b >= 2:
                        pe.wait_ge(ctx_emptied.sem, c0 + b - 1)
                    ctx_done.up(one(b, b0 + b, slice(b * BLK, (b + 1) * BLK), ctx=True))
                if b >= SLOTS:
                    pe.wait_ge(emptied.sem, e0 + b - SLOTS + 1)
                one(b % SLOTS, b0 + b, slice(b * BLK, (b + 1) * BLK)).then_inc(W.multiplied, 1)
            with pe.Fori(0, rounds) as i:
                for u in range(SLOTS):
                    b = b0 + peeled + u
                    pe.wait_ge(W.landed[b % SLOTS], i * 16 + 16 * (b // SLOTS + 1))
                    if peeled:
                        pe.wait_ge(emptied.sem, i * SLOTS + (e0 + peeled + u - SLOTS + 1))
                    else:
                        pe.wait_ge(emptied.sem, i * SLOTS + e0)
                    one(u, b, bass.ds(i * (SLOTS * BLK) + (peeled + u) * BLK, BLK)).then_inc(W.multiplied, 1)

        @block.scalar
        def _(act):
            kit.load(act, ccol[:, 0], dram["c"].rearrange("a (k p) -> p (a k)", p=P), slow=True)
            kit.load(act, ccol[:, 1], dram["c_ctx"].rearrange("(k p) -> p k", p=P), slow=True)
            kit.load(act, brow[:], dram["mod_b"][layer:layer + 1, :])
            act.wait_ge(loaded.sem, l0 + 48)
            ready.up(nc.scalar.activation(ccol[:], ccol[:], ACT.Silu))
            for b in range(peeled):
                if b < ctx_blocks:
                    act.wait_ge(ctx_done.sem, d0 + b + 1)
                    ctx_emptied.up(nc.scalar.copy(mod_ctx[:, b * BLK:(b + 1) * BLK], kit.bank[6 + b % 2][:, 0:BLK]))
                act.wait_ge(W.multiplied, b0 + b + 1)
                nc.scalar.copy(mod[:, b * BLK:(b + 1) * BLK], kit.bank[b % SLOTS][:, 0:BLK]).then_inc(emptied.sem, 1)
            with act.Fori(0, rounds) as i:
                for u in range(SLOTS):
                    act.wait_ge(W.multiplied, i * SLOTS + (b0 + peeled + u + 1))
                    nc.scalar.copy(mod[:, bass.ds(i * (SLOTS * BLK) + (peeled + u) * BLK, BLK)],
                                   kit.bank[u][:, 0:BLK]).then_inc(emptied.sem, 1)
    W.used += nb
    emptied.n = e0 + nb



def attend(kit, units, PT, cat_bank, probs_of, values_of):
    nc = kit.nc
    turned, copied, mixed = kit.count("probs_turned"), kit.count("probs_copied"), kit.count("values_mixed")
    t0, c0, m0 = turned.n, copied.n, mixed.n
    jobs = []
    for u, chunks in enumerate(units):
        for a in range(0, len(chunks), 4):
            jobs.append((u, a, chunks[a:a + 4], a + 4 >= len(chunks)))

    def pe_side(pe, before_unit):
        def turn(j):
            u, a, cs, last = jobs[j]
            if a == 0:
                before_unit(pe, u)
            if j >= 4:
                pe.wait_ge(copied.sem, c0 + j - 3)
            for i, c in enumerate(cs):
                mm = nc.tensor.transpose(kit.bank[j % 4][:, i * P:(i + 1) * P], probs_of(u, c), kit.ident)
            turned.up(mm)

        def mix(j):
            u, a, cs, last = jobs[j]
            pe.wait_ge(copied.sem, c0 + j + 1)
            for i, c in enumerate(cs):
                mm = nc.tensor.matmul(cat_bank(u), PT[:, j % 4, i, :], values_of(u, c),
                                      start=(a == 0 and i == 0), stop=(last and i == len(cs) - 1))
            mixed.up(mm)

        for j in range(len(jobs)):
            turn(j)
            if j >= 2:
                mix(j - 2)
        for j in range(max(0, len(jobs) - 2), len(jobs)):
            mix(j)

    def act_side(act):
        for j, (u, a, cs, last) in enumerate(jobs):
            act.wait_ge(turned.sem, t0 + j + 1)
            if j >= 4:
                act.wait_ge(mixed.sem, m0 + j - 3)
            copied.up(nc.scalar.copy(PT[:, j % 4, 0:len(cs), :], kit.bank[j % 4][:, 0:len(cs) * P].rearrange(
                "p (n t) -> p n t", n=len(cs))))

    return pe_side, act_side, m0 + len(jobs)


def window_attention(kit, dram, proj, kvc, cat):
    nc = kit.nc
    nqk = (Q_W + KV_W) // HD
    loaded = kit.count("loaded")
    l0 = loaded.n
    with kit.sb("qT", [P, GQA, SEQ]) as qT, kit.sb("kT", [P, 2 * SEQ]) as kT, kit.sb("sink", [P, HEADS]) as sink:
        with kit.sb("rot", [P, NT, nqk * HD]) as rot, kit.sb("rot2", [P, NT, nqk * HD]) as rot2, \
                kit.sb("turned", [P, NT, nqk * HD]) as turned:
            with nc.Block() as block:
                @block.sync
                def _(sp):
                    kit.load(sp, sink[:], bcast(dram["attn_sink"], HEADS))

                @block.vector
                def _(dve):
                    for T in range(NT):
                        x = proj[:, T, 0:nqk * HD]
                        cos = kit.cos[:, T].unsqueeze(1).to_broadcast([P, nqk, HD])
                        nc.vector.tensor_tensor(rot[:, T].rearrange("p (h d) -> p h d", d=HD),
                                                x.rearrange("p (h d) -> p h d", d=HD), cos, ALU.mult)
                        xs = x.rearrange("p (h f s c) -> p h f s c", f=2, s=2, c=16)
                        o = rot2[:, T].rearrange("p (h f s c) -> p h f s c", f=2, s=2, c=16)
                        sn = kit.sin[:, T].rearrange("p (f s c) -> p f s c", f=2, s=2)
                        for s in range(2):
                            ins = nc.vector.tensor_tensor(o[:, :, :, s], xs[:, :, :, 1 - s],
                                                          sn[:, :, s].unsqueeze(1).to_broadcast([P, nqk, 2, 16]),
                                                          ALU.mult)
                        kit.dve(ins)
                        by_chunk = lambda a: a[:, T, 0:Q_W].rearrange("p (v c d) -> p c v d", v=2, d=HD)
                        nc.vector.tensor_tensor(turned[:, T, 0:Q_W].rearrange("p (c v d) -> p c v d", v=2, d=HD),
                                                by_chunk(rot), by_chunk(rot2), ALU.add)
                        nc.vector.tensor_tensor(turned[:, T, Q_W:], rot[:, T, Q_W:], rot2[:, T, Q_W:], ALU.add)
                    dve.wait_ge(loaded.sem, l0 + 16)
            jobs = []
            for T in range(NT):
                jobs.append(([turned[:, T, c * P:(c + 1) * P] for c in range(GQA)], qT[:, :, T * P:(T + 1) * P]))
            jobs.append(([turned[:, T, Q_W:Q_W + KV_W] for T in range(NT)] + [kvc[:, T, 0:KV_W] for T in range(NT)],
                         kT[:].rearrange("p (n t) -> p n t", t=P)))
            transposes(kit, jobs)

        units = [(T, h) for T in range(NT) for h in range(HEADS)]
        nu = len(units)
        with kit.sb("probs", [P, nu, 512]) as probs, kit.sb("PT", [P, 4, 4, P]) as PT, \
                kit.sb("rows", [P, 8, nu]) as rows:
            scored, masked = kit.count("scored"), kit.count("score_masked")
            s0, k0 = scored.n, masked.n
            negmax, exped, normed = kit.count("negmax_ready"), kit.count("exped"), kit.count("denominators")
            n0, x0, d0 = negmax.n, exped.n, normed.n
            cat_bank = lambda u: kit.bank[4 + u // HEADS][:, (u % HEADS) * HD:(u % HEADS + 1) * HD]
            values = lambda u, c: (proj[:, c, Q_W + KV_W:][:, (u % HEADS) // GQA * HD:((u % HEADS) // GQA + 1) * HD]
                                   if c < NT else
                                   kvc[:, c - NT, KV_W + (u % HEADS) // GQA * HD:KV_W + ((u % HEADS) // GQA + 1) * HD])
            pe_side, act_side, m_end = attend(kit, [range(4)] * nu, PT, cat_bank,
                                              lambda u, c: probs[:, u, c * P:(c + 1) * P], values)
            mixed = kit.count("values_mixed")
            with nc.Block() as block:
                @block.tensor
                def _(pe):
                    for u, (T, h) in enumerate(units):
                        if u >= 4:
                            pe.wait_ge(masked.sem, k0 + u - 3)
                        v, c = h // GQA, h % GQA
                        scored.up(nc.tensor.matmul(kit.bank[u % 4][:, :], qT[v * HD:(v + 1) * HD, c, T * P:(T + 1) * P],
                                                   kT[v * HD:(v + 1) * HD, :], start=True, stop=True))
                    pe.wait_ge(masked.sem, k0 + nu)
                    pe_side(pe, lambda pe, u: pe.wait_ge(exped.sem, x0 + u + 1))

                @block.vector
                def _(dve):
                    for u, (T, h) in enumerate(units):
                        dve.wait_ge(scored.sem, s0 + u + 1)
                        masked.up(nc.vector.tensor_tensor_reduce(
                            out=probs[:, u], in0=kit.bank[u % 4][:, :], in1=kit.window[:, T], scale=SCALE,
                            scalar=NEG, op0=ALU.add, op1=ALU.max, accum_out=rows[:, 0, u:u + 1]))
                    dve.wait_ge(masked.sem, k0 + nu)
                    sk = sink[:].unsqueeze(1).to_broadcast([P, NT, HEADS])
                    r = lambda i: rows[:, i].rearrange("p (t h) -> p t h", t=NT)
                    kit.dve(nc.vector.tensor_tensor(r(1), r(0), sk, ALU.max))
                    nc.vector.tensor_tensor(r(3), sk, r(1), ALU.subtract).then_inc(negmax.sem, 1)
                    nc.vector.tensor_scalar(rows[:, 2], rows[:, 1], -1.0, None, ALU.mult).then_inc(negmax.sem, 1)
                    negmax.n += 2
                    dve.wait_ge(exped.sem, x0 + nu + 1)
                    kit.dve(nc.vector.tensor_tensor(rows[:, 6], rows[:, 5], rows[:, 4], ALU.add))
                    kit.dve(nc.vector.reciprocal(rows[:, 7], rows[:, 6]))
                    dve.wait_ge(mixed.sem, m_end)
                    for T in range(NT):
                        nc.vector.tensor_tensor(
                            cat[:, T, 0:Q_W].rearrange("p (h d) -> p h d", d=HD),
                            kit.bank[4 + T][:, :].rearrange("p (h d) -> p h d", d=HD),
                            rows[:, 7, T * HEADS:(T + 1) * HEADS].unsqueeze(2).to_broadcast([P, HEADS, HD]), ALU.mult)

                @block.scalar
                def _(act):
                    act.wait_ge(negmax.sem, n0 + 2)
                    for u in range(nu):
                        exped.up(nc.scalar.activation(probs[:, u], probs[:, u], ACT.Exp, bias=rows[:, 2, u:u + 1],
                                                      accum_out=rows[:, 4, u:u + 1]))
                    exped.up(nc.scalar.activation(rows[:, 5], rows[:, 3], ACT.Exp))
                    act_side(act)


def gmlp(kit, dram, proj, cat):
    nc = kit.nc
    loaded = kit.count("loaded")
    l0 = loaded.n
    u0 = Q_W + 2 * KV_W
    with kit.sb("ws", [P, GROUPS, P]) as ws, kit.sb("wsT", [P, GROUPS, P]) as wsT, kit.sb("bs", [P, GROUPS]) as bs, \
            kit.sb("stat", [P, 4, NT * GROUPS]) as stat, kit.sb("sq", [P, NT, A_W]) as sq:
        gelued = kit.count("gelued")
        g0 = gelued.n
        with nc.Block() as block:
            @block.sync
            def _(sp):
                kit.load(sp, ws[:], dram["gmlp_w_s"].rearrange("e g p q -> p (e g) q"))
                kit.load(sp, bs[:], dram["gmlp_b_s"].rearrange("e g p -> p (e g)"), slow=True)
                sp.wait_ge(loaded.sem, l0 + 32)

            @block.scalar
            def _(act):
                for T in range(NT):
                    gelued.up(nc.scalar.activation(proj[:, T, u0:u0 + 2 * A_W], proj[:, T, u0:u0 + 2 * A_W],
                                                   ACT.Gelu_apprx_tanh))
                kit.roots(act, [(stat[:, 3, T * GROUPS:(T + 1) * GROUPS], stat[:, 2, T * GROUPS:(T + 1) * GROUPS])
                                for T in range(NT)])

            @block.vector
            def _(dve):
                for T in range(NT):
                    dve.wait_ge(gelued.sem, g0 + T + 1)
                    v = proj[:, T, u0 + A_W:u0 + 2 * A_W].rearrange("p (g d) -> p g d", d=HD)
                    s = sq[:, T].rearrange("p (g d) -> p g d", d=HD)
                    st = lambda i: stat[:, i, T * GROUPS:(T + 1) * GROUPS]
                    wide = lambda i: st(i).unsqueeze(2).to_broadcast([P, GROUPS, HD])
                    kit.dve(nc.vector.tensor_reduce(st(0), v, AX, ALU.add))
                    kit.dve(nc.vector.tensor_scalar(st(0), st(0), 1.0 / HD, None, ALU.mult))
                    kit.dve(nc.vector.tensor_tensor(v, v, wide(0), ALU.subtract))
                    kit.dve(nc.vector.tensor_tensor(s, v, v, ALU.mult))
                    kit.dve(nc.vector.tensor_reduce(st(1), s, AX, ALU.add))
                    kit.rsqrt(dve, nc.vector.tensor_scalar(st(2), st(1), 1.0 / HD, EPS, ALU.mult, ALU.add), st(3), st(3))
                    kit.dve(nc.vector.tensor_tensor(v, v, wide(3), ALU.mult))
        transposes(kit, [([ws[:, g + i, :] for i in range(4)], wsT[:, g:g + 4, :]) for g in (0, 4)])
        spread = kit.count("tokens_mixed")
        s0 = spread.n
        with nc.Block() as block:
            @block.tensor
            def _(pe):
                for g in range(GROUPS):
                    spread.up(nc.tensor.matmul(kit.bank[g // 4][:, g % 4 * P:(g % 4 + 1) * P], wsT[:, g, :],
                                               proj[:, :, u0 + A_W + g * HD:u0 + A_W + (g + 1) * HD],
                                               start=True, stop=True))

            @block.vector
            def _(dve):
                dve.wait_ge(spread.sem, s0 + GROUPS)
                for g in range(GROUPS):
                    nc.vector.scalar_tensor_tensor(
                        out=cat[:, :, Q_W + g * HD:Q_W + (g + 1) * HD],
                        in0=kit.bank[g // 4][:, g % 4 * P:(g % 4 + 1) * P].rearrange("p (t d) -> p t d", t=NT),
                        scalar=bs[:, g:g + 1], in1=proj[:, :, u0 + g * HD:u0 + (g + 1) * HD],
                        op0=ALU.add, op1=ALU.mult)


def mixer(kit, dram, mod, mod_ctx):
    x, h, hT = kit.x, kit.h, kit.hT
    nc = kit.nc
    with kit.sb("cat", [P, NT, D]) as cat:
        with kit.sb("proj", [P, NT, Q_W + 2 * KV_W + 2 * A_W]) as proj, kit.sb("kvc", [P, NT, 2 * KV_W]) as kvc:
            with kit.sb("hcT", [P, KD, SEQ]) as hcT:
                with kit.sb("xc", [P, NT, D]) as xc:
                    loaded = kit.count("loaded")
                    l0 = loaded.n
                    with nc.Block() as block:
                        @block.sync
                        def _(sp):
                            kit.load(sp, xc[:], dram["ctx"].rearrange("a (t p) d -> p (a t) d", p=P))
                            sp.wait_ge(loaded.sem, l0 + 16)
                    norm_modulated(kit, xc, dram["norm1_g"][0:1, :], mod_ctx[:, D:2 * D], mod_ctx[:, 0:D], h)
                transpose_tokens(kit, h, hcT)
                norm_modulated(kit, x, dram["norm1_g"][0:1, :], mod[:, D:2 * D], mod[:, 0:D], h)
                transpose_tokens(kit, h, hT)
                linear(kit, hT, 7, False, copy_out(kit, proj), extra=(Q_W // BLK, hcT),
                       extra_evacuate=lambda bank: nc.scalar.copy(kvc[:], bank))
            window_attention(kit, dram, proj, kvc, cat)
            gmlp(kit, dram, proj, cat)
        transpose_tokens(kit, cat, hT)
        with kit.sb("tmp", [P, NT, BLK]) as tmp:
            linear(kit, hT, 4, False, add_gated(kit, x, tmp, mod[:, 2 * D:3 * D]), on_dve=True)


def pooling(kit, dram, mod):
    nc, W = kit.nc, kit.weights
    x, h = kit.x, kit.h
    norm_modulated(kit, x, dram["norm1_g"][1:2, :], mod[:, D:2 * D], mod[:, 0:D], h)
    b0 = W.used
    loaded, pooled, copied, done = kit.count("loaded"), kit.count("pooled"), kit.count("pooled_copied"), kit.count("pool_projected")
    l0, p0, c0, d0 = loaded.n, pooled.n, copied.n, done.n
    G = len(POOL_WINDOWS)
    with kit.sb("bands", [P, G, NT, SEQ]) as bands, kit.sb("pooledT", [P, KD, SEQ]) as pT, \
            kit.sb("gs", [P, D]) as gs, kit.sb("tmp", [P, D]) as tmp, nc.Block() as block:
        @block.sync
        def _(sp):
            kit.load(sp, bands[:], dram["bands"].rearrange("g (t p) n -> p g t n", p=P))
            kit.load(sp, gs[:], bcast(dram["pool_scale"], D))
            W.issue(sp, b0 + 1 + SLOTS)

        @block.tensor
        def _(pe):
            pe.wait_ge(loaded.sem, l0 + 32)
            for k in range(KD):
                for t in range(NT):
                    mm = nc.tensor.matmul(kit.bank[k // 2][:, k % 2 * SEQ:(k % 2 + 1) * SEQ], h[:, t, k * P:(k + 1) * P],
                                          bands[:, k // 2, t, :], start=(t == 0), stop=(t == NT - 1))
                pooled.up(mm)
            W.wait(pe, b0)
            w = W.tile(b0, KD)
            for T in range(NT):
                for g in range(G):
                    pe.wait_ge(copied.sem, c0 + g + 1)
                    for cc in range(2):
                        mm = nc.tensor.matmul(kit.bank[4 + 2 * T + g // 2][:, g % 2 * BLK:(g % 2 + 1) * BLK],
                                              pT[:, 2 * g + cc, T * P:(T + 1) * P], w[:, 2 * g + cc, :],
                                              start=(cc == 0), stop=(cc == 1))
                if T == NT - 1:
                    mm.then_inc(W.multiplied, 1)
                else:
                    done.up(mm)

        @block.scalar
        def _(act):
            for g in range(G):
                act.wait_ge(pooled.sem, p0 + 2 * g + 2)
                copied.up(nc.scalar.copy(pT[:, 2 * g:2 * g + 2, :], kit.bank[g][:, :].rearrange("p (a n) -> p a n", a=2)))

        @block.vector
        def _(dve):
            dve.wait_ge(loaded.sem, l0 + 32)
            kit.dve(nc.vector.tensor_tensor(gs[:], gs[:], mod[:, 2 * D:3 * D], ALU.mult))
            for T in range(NT):
                if T == NT - 1:
                    dve.wait_ge(W.multiplied, b0 + 1)
                else:
                    dve.wait_ge(done.sem, d0 + 1)
                for i in range(2):
                    kit.dve(nc.vector.tensor_tensor(tmp[:, i * 512:(i + 1) * 512], kit.bank[4 + 2 * T + i][:, :],
                                                    gs[:, i * 512:(i + 1) * 512], ALU.mult))
                kit.dve(nc.vector.tensor_tensor(x[:, T], x[:, T], tmp[:], ALU.add))
    W.used += 1



def peer(kit, dram, layer, mod):
    nc = kit.nc
    x, h, hT = kit.x, kit.h, kit.hT
    norm_modulated(kit, x, dram["norm2_g"][layer:layer + 1, :], mod[:, 4 * D:5 * D], mod[:, 3 * D:4 * D], h)
    transpose_tokens(kit, h, hT)
    with kit.sb("idx", [P, NT, PICKS], U32) as idx, kit.sb("gate", [P, NT, PICKS]) as gate:
        with kit.sb("peer_q", [P, PH, 2, SEQ]) as qT, kit.sb("keys", [P, 2, P]) as keys, kit.sb("keysT", [P, 2, P]) as keysT:
            linear(kit, hT, 8, True, lambda b, bank: nc.scalar.copy(qT[:, b], bank))
            loaded = kit.count("loaded")
            l0 = loaded.n
            with nc.Block() as block:
                @block.sync
                def _(sp):
                    kit.load(sp, keys[:], dram["peer_sub_keys"][layer].rearrange("s n k -> n s k"))
                    sp.wait_ge(loaded.sem, l0 + 16)
            transposes(kit, [([keys[:, s, :] for s in range(2)], keysT[:])])
            choose(kit, qT, keysT, idx, gate)
        gather_experts(kit, dram, layer, idx, gate, mod)


def top16(kit, values, indices, data, spare):
    nc = kit.nc
    kit.dve(nc.vector.max(values[:, 0:8], data))
    nc.vector.max_index(indices[:, 0:8], values[:, 0:8], data)
    kit.dve(nc.vector.match_replace(spare, values[:, 0:8], data, -3e38))
    kit.dve(nc.vector.max(values[:, 8:16], spare))
    kit.dve(nc.vector.max_index(indices[:, 8:16], values[:, 8:16], spare))


def choose(kit, qT, keysT, idx, gate):
    nc = kit.nc
    nu = 2 * PH
    scored, copied, shifted, exped = (kit.count("keys_scored"), kit.count("key_scores_copied"),
                                      kit.count("best_shifted"), kit.count("best_exped"))
    s0, c0, h0, x0 = scored.n, copied.n, shifted.n, exped.n
    with kit.sb("scores", [P, NT, nu, NKEYS]) as sc, kit.sb("spare", [P, 256]) as spare, \
            kit.sb("top", [P, NT, PH, 2, TOPK]) as top, kit.sb("itop", [P, NT, PH, 2, TOPK], U32) as itop, \
            kit.sb("ftop", [P, PH, 2, TOPK]) as ftop, \
            kit.sb("cand", [P, 16, 16]) as cand, kit.sb("best", [P, NT, PH, TOPK]) as best, \
            kit.sb("pos", [P, PH, TOPK], U32) as pos, kit.sb("part", [P, 2, PICKS], U32) as part, \
            kit.sb("fpart", [P, 2, PICKS]) as fpart, kit.sb("sel", [P, PICKS, 16]) as sel, \
            kit.sb("row", [P, 2, PICKS]) as row, kit.sb("fidx", [P, PICKS]) as fidx, \
            kit.sb("den", [P, 2, NT, PH]) as den, nc.Block() as block:
        @block.tensor
        def _(pe):
            for T in range(NT):
                for q in range(nu // 4):
                    b = T * (nu // 4) + q
                    if b >= 4:
                        pe.wait_ge(copied.sem, c0 + b - 3)
                    for i in range(4):
                        hh, s = (4 * q + i) // 2, i % 2
                        mm = nc.tensor.matmul(kit.bank[b % 4][:, i * P:(i + 1) * P], qT[:, hh, s, T * P:(T + 1) * P],
                                              keysT[:, s, :], start=True, stop=True)
                    scored.up(mm)

        @block.scalar
        def _(act):
            for T in range(NT):
                for q in range(nu // 4):
                    b = T * (nu // 4) + q
                    act.wait_ge(scored.sem, s0 + b + 1)
                    copied.up(nc.scalar.copy(sc[:, T, 4 * q:4 * q + 4, :], kit.bank[b % 4][:, :].rearrange(
                        "p (a n) -> p a n", a=4)))
            for T in range(NT):
                act.wait_ge(shifted.sem, h0 + T + 1)
                exped.up(nc.scalar.activation(gate[:, T], gate[:, T], ACT.Exp))

        @block.vector
        def _(dve):
            for T in range(NT):
                for u in range(nu):
                    dve.wait_ge(copied.sem, c0 + T * (nu // 4) + u // 4 + 1)
                    top16(kit, top[:, T, u // 2, u % 2], itop[:, T, u // 2, u % 2], sc[:, T, u], spare[:, 0:NKEYS])
                for hh in range(PH):
                    kit.dve(nc.vector.tensor_tensor(cand[:], top[:, T, hh, 0].unsqueeze(2).to_broadcast([P, 16, 16]),
                                                    top[:, T, hh, 1].unsqueeze(1).to_broadcast([P, 16, 16]), ALU.add))
                    top16(kit, best[:, T, hh], pos[:, hh], cand[:].rearrange("p a b -> p (a b)"), spare[:])
                g = gate[:, T].rearrange("p (h k) -> p h k", h=PH)
                shifted.up(nc.vector.tensor_tensor(g, best[:, T], best[:, T, :, 0:1].to_broadcast([P, PH, TOPK]),
                                                   ALU.subtract))
                flat = pos[:].rearrange("p h k -> p (h k)")
                nc.vector.tensor_scalar(part[:, 0], flat, 4, None, ALU.logical_shift_right)
                kit.dve(nc.vector.tensor_scalar(part[:, 1], flat, 15, None, ALU.bitwise_and))
                nc.vector.tensor_copy(ftop[:], itop[:, T])
                kit.dve(nc.vector.tensor_copy(fpart[:], part[:]))
                for s in range(2):
                    kit.dve(nc.vector.tensor_tensor(sel[:], fpart[:, s].unsqueeze(2).to_broadcast([P, PICKS, 16]),
                                                    kit.iota16.unsqueeze(1).to_broadcast([P, PICKS, 16]), ALU.is_equal))
                    sv = sel[:].rearrange("p (h k) i -> p h k i", h=PH)
                    kit.dve(nc.vector.tensor_tensor(sv, sv, ftop[:, :, s].unsqueeze(2).to_broadcast([P, PH, TOPK, 16]),
                                                    ALU.mult))
                    kit.dve(nc.vector.tensor_reduce(row[:, s], sel[:], AX, ALU.add))
                kit.dve(nc.vector.scalar_tensor_tensor(out=fidx[:], in0=row[:, 0], scalar=float(NKEYS), in1=row[:, 1],
                                                       op0=ALU.mult, op1=ALU.add))
                nc.vector.tensor_copy(idx[:, T], fidx[:])
            for T in range(NT):
                dve.wait_ge(exped.sem, x0 + T + 1)
                g = gate[:, T].rearrange("p (h k) -> p h k", h=PH)
                kit.dve(nc.vector.tensor_reduce(den[:, 0, T], g, AX, ALU.add))
                kit.dve(nc.vector.reciprocal(den[:, 1, T], den[:, 0, T]))
                nc.vector.tensor_tensor(g, g, den[:, 1, T].unsqueeze(2).to_broadcast([P, PH, TOPK]), ALU.mult)


def gather_experts(kit, dram, layer, idx, gate, mod):
    nc = kit.nc
    x, h = kit.x, kit.h
    UN = 2 * GRING
    rounds = PICKS // UN
    row_landed = [kit.count(f"row_landed{i}") for i in range(GRING)]
    claimed = kit.count("row_slots_claimed")
    free, idx_ready, dots, copied = (kit.count("row_slots_freed"), kit.count("slot_indices"), kit.count("dots_copied"),
                                     kit.count("gelu_done"))
    phases = [("peer_down", T) for T in range(NT)] + [("peer_up", T) for T in range(NT)]
    tables = {n: dram[n].rearrange("l e d -> (l e) d") for n in ("peer_down", "peer_up")}
    u0, i0, d0, c0 = free.n - GRING, idx_ready.n, dots.n, copied.n
    L0 = row_landed[0].n
    with kit.sb("rows", [P, GRING, D]) as ring, kit.sb("slot_idx", [P, 2, GRING], U32) as slot_idx, \
            kit.sb("dot16", [P, UN]) as dot16, kit.sb("dot", [P, NT, PICKS]) as dot, \
            kit.sb("acc", [P, NT, D]) as acc, kit.sb("layer_idx", [P, NT, PICKS], U32) as lidx, nc.Block() as block:
        @block.gpsimd
        def _(pool):
            if layer:
                pool.wait_ge(idx_ready.sem, i0 + 1)
            src_idx = lidx if layer else idx
            extra = 1 if layer else 0
            for ph, (name, T) in enumerate(phases):
                g0 = ph * PICKS
                with pool.Fori(0, rounds) as i:
                    for half in range(2):
                        j = g0 + half * GRING
                        pool.wait_ge(free.sem, i * UN + (u0 + j + 1))
                        nc.gpsimd.tensor_copy(slot_idx[:, half], src_idx[:, T, bass.ds(i * UN + half * GRING, GRING)]) \
                            .then_inc(idx_ready.sem, 1)
                        pool.wait_ge(idx_ready.sem, i * 2 + (i0 + extra + ph * 2 * rounds + half + 1))
                        for s in range(GRING):
                            pool.wait_ge(free.sem, i * UN + (u0 + j + s + 1))
                            pool.sem_inc(claimed.sem, 1)
                            nc.gpsimd.indirect_dma_start(
                                ring[:, s], None, tables[name],
                                bass.IndirectOffsetOnAxis(ap=slot_idx[:, half, s:s + 1], axis=0)) \
                                .then_inc(row_landed[s].sem, 16)

        @block.vector
        def _(dve):
            if layer:
                kit.dve(nc.vector.tensor_copy(dot[:], idx[:]))
                kit.dve(nc.vector.tensor_scalar(dot[:], dot[:], float(layer * NKEYS * NKEYS), None, ALU.add))
                nc.vector.tensor_copy(lidx[:], dot[:]).then_inc(idx_ready.sem, 1)
                dve.wait_ge(idx_ready.sem, i0 + 1)
            kit.dve(nc.vector.memset(acc[:], 0.0))
            for ph, (name, T) in enumerate(phases):
                if ph >= NT:
                    dve.wait_ge(copied.sem, c0 + T + 1)
                    kit.dve(nc.vector.tensor_tensor(gate[:, T], gate[:, T], dot[:, T], ALU.mult))
                with dve.Fori(0, rounds) as i:
                    for n in range(UN):
                        g = ph * PICKS + n
                        s = n % GRING
                        dve.wait_ge(row_landed[s].sem, i * 32 + (L0 + 16 * (ph * PICKS // GRING + n // GRING + 1)))
                        if ph < NT:
                            if n == 0:
                                dve.wait_ge(dots.sem, i + (d0 + ph * rounds))
                            nc.vector.tensor_tensor_reduce(out=ring[:, s], in0=ring[:, s], in1=h[:, T], scale=1.0, scalar=0.0,
                                                           op0=ALU.mult, op1=ALU.add, accum_out=dot16[:, n:n + 1]) \
                                .then_inc(free.sem, 1)
                        else:
                            dve.wait_ge(free.sem, i * UN + (u0 + GRING + g))
                            nc.vector.scalar_tensor_tensor(out=acc[:, T], in0=ring[:, s],
                                                           scalar=gate[:, T, bass.ds(i * UN + n, 1)], in1=acc[:, T],
                                                           op0=ALU.mult, op1=ALU.add).then_inc(free.sem, 1)
                    if ph < NT:
                        dve.wait_ge(free.sem, i * UN + (u0 + GRING + ph * PICKS + UN))
                        nc.vector.tensor_copy(dot[:, T, bass.ds(i * UN, UN)], dot16[:]).then_inc(dots.sem, 1)
            dve.wait_ge(free.sem, u0 + GRING + len(phases) * PICKS)
            g2 = mod[:, 5 * D:6 * D].unsqueeze(1).to_broadcast([P, NT, D])
            kit.dve(nc.vector.tensor_tensor(acc[:], acc[:], g2, ALU.mult))
            nc.vector.tensor_tensor(x[:], x[:], acc[:], ALU.add)

        @block.scalar
        def _(act):
            for T in range(NT):
                act.wait_ge(dots.sem, d0 + (T + 1) * rounds)
                nc.scalar.activation(dot[:, T], dot[:, T], ACT.Gelu_apprx_tanh).then_inc(copied.sem, 1)
    free.n += len(phases) * PICKS
    idx_ready.n += len(phases) * 2 * rounds + (1 if layer else 0)
    dots.n += NT * rounds
    copied.n += NT
    for c in row_landed:
        c.n += len(phases) * PICKS // GRING * 16



def ffn_blocks(dram, layer, which):
    g = columns(dram["ffn_w_gate_2"][layer, which])
    u = columns(dram["ffn_w_up_2"][layer, which])
    d = dram["ffn_w_down_2"][layer, which].rearrange("(f s p) n -> f p s n", s=2, p=P)
    out = [g[0], u[0]]
    for f in range(1, FF_BLOCKS):
        out += [g[f], u[f], d[f - 1]]
    return out + [d[FF_BLOCKS - 1]]


def swiglu(kit, dram, layer, which):
    nc, W = kit.nc, kit.weights
    x, h, hT = kit.x, kit.h, kit.hT
    norm_plain(kit, x, dram["ffn_norm_2"][layer, which:which + 1, :], h)
    transpose_tokens(kit, h, hT)
    b0 = W.used
    nb = 3 * FF_BLOCKS
    loops = (FF_BLOCKS - 1) // 2
    silued, ready = kit.count("gate_silued"), kit.count("hidden_ready")
    s0, r0 = silued.n, ready.n
    gate_w = dram["ffn_w_gate_2"][layer, which].rearrange("(k p) n -> p k n", p=P)
    up_w = dram["ffn_w_up_2"][layer, which].rearrange("(k p) n -> p k n", p=P)
    down_w = dram["ffn_w_down_2"][layer, which]

    def up_block(f, v):
        return b0 + v if f == 0 else b0 + 3 * f - 1 + v

    def wait(eng, sem, value, reg, per_round):
        eng.wait_ge(sem, value if reg is None else reg * per_round + value)

    with kit.sb("act_gate", [P, 2, 2 * SEQ]) as ag, kit.sb("hidden", [P, 2, 2, SEQ]) as hid, nc.Block() as block:
        @block.sync
        def _(sp):
            W.issue(sp, b0 + 2 + 6)
            with sp.Fori(0, loops - 1) as i:
                for v in range(6):
                    b, f = b0 + 8 + v, 3 + v // 3
                    sp.wait_ge(W.multiplied, i * 6 + (b - SLOTS + 1))
                    if v % 3 < 2:
                        src = (gate_w, up_w)[v % 3][:, :, bass.ds(i * (2 * BLK) + f * BLK, BLK)]
                    else:
                        src = down_w[bass.ds(i * (2 * BLK) + (f - 1) * BLK, BLK), :].rearrange("(s p) n -> p s n", p=P)
                    sp.dma_start(W.tile(b, KD if v % 3 < 2 else 2), src).then_inc(W.landed[b % SLOTS], 16)
            W.issued = b0 + nb - 1
            W.issue(sp, b0 + nb + SLOTS)

        def up_products(pe, f, reg=None):
            for v in range(2):
                b = up_block(f, v)
                wait(pe, W.landed[b % SLOTS], 16 * (b // SLOTS + 1), reg, 16)
                if v == 0 and reg is not None:
                    wait(pe, ready.sem, r0 + f - 1, reg, 2)
                w = W.tile(b, KD)
                for s in range(2):
                    for k in range(KD):
                        mm = nc.tensor.matmul(kit.bank[2 * (f % 2) + v][:, s * SEQ:(s + 1) * SEQ],
                                              w[:, k, s * P:(s + 1) * P], hT[:, k, :],
                                              start=(k == 0), stop=(k == KD - 1))
                mm.then_inc(W.multiplied, 1)

        def down_products(pe, f, reg=None, last=False):
            b = b0 + 3 * f + 4 if not last else b0 + nb - 1
            wait(pe, W.landed[b % SLOTS], 16 * (b // SLOTS + 1), reg, 16)
            wait(pe, ready.sem, r0 + f + 1, reg, 2)
            w = W.tile(b, 2)
            for T in range(NT):
                for half in range(2):
                    for s in range(2):
                        mm = nc.tensor.matmul(kit.bank[4 + 2 * T + half][:, :], hid[:, f % 2, s, T * P:(T + 1) * P],
                                              w[:, s, half * 512:(half + 1) * 512],
                                              start=False, stop=(last and s == 1), skip_group_check=True)
            mm.then_inc(W.multiplied, 1)

        @block.tensor
        def _(pe):
            for bnk in range(4, 8):
                nc.tensor.matmul(kit.bank[bnk][:, :], kit.zeros[0:1, 0:P], kit.zeros[0:1, :], start=True, stop=False,
                                 skip_group_check=True)
            up_products(pe, 0)
            with pe.Fori(0, loops) as i:
                for f in (1, 2):
                    up_products(pe, f, reg=i)
                    down_products(pe, f - 1, reg=i)
            down_products(pe, FF_BLOCKS - 1, last=True)

        @block.scalar
        def _(act):
            def gate(f, reg=None):
                wait(act, W.multiplied, up_block(f, 0) + 1, reg, 6)
                if reg is not None:
                    wait(act, ready.sem, r0 + f - 1, reg, 2)
                nc.scalar.activation(ag[:, f % 2], kit.bank[2 * (f % 2)][:, :], ACT.Silu).then_inc(silued.sem, 1)
            gate(0)
            with act.Fori(0, loops) as i:
                for f in (1, 2):
                    gate(f, reg=i)

        @block.vector
        def _(dve):
            def make_hidden(f, reg=None):
                wait(dve, W.multiplied, up_block(f, 1) + 1, reg, 6)
                wait(dve, silued.sem, s0 + f + 1, reg, 2)
                nc.vector.tensor_tensor(hid[:, f % 2].rearrange("p s t -> p (s t)"), ag[:, f % 2],
                                        kit.bank[2 * (f % 2) + 1][:, :], ALU.mult).then_inc(ready.sem, 1)
            make_hidden(0)
            with dve.Fori(0, loops) as i:
                for f in (1, 2):
                    make_hidden(f, reg=i)
            dve.wait_ge(W.multiplied, b0 + nb)
            for T in range(NT):
                for half in range(2):
                    xs = x[:, T, half * 512:(half + 1) * 512]
                    nc.vector.scalar_tensor_tensor(out=xs, in0=kit.bank[4 + 2 * T + half][:, :], scalar=0.5, in1=xs,
                                                   op0=ALU.mult, op1=ALU.add)
    silued.n += FF_BLOCKS
    ready.n += FF_BLOCKS
    W.used += nb



def parallel_attention(kit, dram):
    nc, W = kit.nc, kit.weights
    x, h, hT = kit.x, kit.h, kit.hT
    norm_plain(kit, x, dram["mix_norm_2"][0:1, :], h)
    transpose_tokens(kit, h, hT)
    QK0, NQK = 3 * SB_HEADS * HD, 2 * DIL_HEADS * HD
    V0 = QK0 + NQK
    width = (SB_HEADS + GROUP_HEADS) * HD
    with kit.sb("cat2", [P, NT, width]) as cat:
        with kit.sb("proj2", [P, NT, 3 * D]) as proj, kit.sb("tT", [P, 16, SEQ]) as tT:
            linear(kit, hT, 12, False, copy_out(kit, proj))
            head_norms(kit, dram, proj, QK0)
            cols = [i * P for i in range(4)] + [QK0 + i * P for i in range(12)]
            jobs = []
            for T in range(NT):
                for c in range(0, 16, 4):
                    jobs.append(([proj[:, T, cols[c + i]:cols[c + i] + P] for i in range(4)],
                                 tT[:, c:c + 4, T * P:(T + 1) * P]))
            transposes(kit, jobs)
            stick_breaking(kit, proj, tT, cat)
            dilated(kit, dram, proj, tT, cat, V0)
        transpose_tokens(kit, cat, hT, kc=4)
        b0 = W.used
        done = kit.count("attention_projected")
        d0 = done.n
        with nc.Block() as block:
            @block.sync
            def _(sp):
                W.issue(sp, b0 + 2 + SLOTS)

            @block.tensor
            def _(pe):
                for b in range(2):
                    W.wait(pe, b0 + b)
                    w = W.tile(b0 + b, 4)
                    for T in range(NT):
                        for k in range(4):
                            mm = nc.tensor.matmul(kit.bank[2 * b + T][:, :], hT[:, k, T * P:(T + 1) * P], w[:, k, :],
                                                  start=(k == 0), stop=(k == 3))
                    mm.then_inc(W.multiplied, 1)

            @block.vector
            def _(dve):
                for b in range(2):
                    dve.wait_ge(W.multiplied, b0 + b + 1)
                    for T in range(NT):
                        xs = x[:, T, b * 512:(b + 1) * 512]
                        nc.vector.tensor_tensor(xs, xs, kit.bank[2 * b + T][:, :], ALU.add)
        W.used += 2


def head_norms(kit, dram, proj, c0):
    nc = kit.nc
    n = DIL_HEADS
    loaded = kit.count("loaded")
    l0 = loaded.n
    with kit.sb("qkg", [P, 2, HD]) as qkg, kit.sb("sq", [P, 2 * n, HD]) as sq, kit.sb("st", [P, 3, 2 * n]) as st, \
            nc.Block() as block:
        @block.sync
        def _(sp):
            kit.load(sp, qkg[:, 0], bcast(dram["attn_q_norm_2"], HD))
            kit.load(sp, qkg[:, 1], bcast(dram["attn_k_norm_2"], HD))

        @block.scalar
        def _(act):
            kit.roots(act, [(st[:, 2], st[:, 1])] * NT)

        @block.vector
        def _(dve):
            for T in range(NT):
                v = proj[:, T, c0:c0 + 2 * n * HD].rearrange("p (g d) -> p g d", d=HD)
                kit.dve(nc.vector.tensor_tensor(sq[:], v, v, ALU.mult))
                kit.dve(nc.vector.tensor_reduce(st[:, 0], sq[:], AX, ALU.add))
                kit.rsqrt(dve, nc.vector.tensor_scalar(st[:, 1], st[:, 0], 1.0 / HD, EPS, ALU.mult, ALU.add), st[:, 2], st[:, 2])
                kit.dve(nc.vector.tensor_tensor(v, v, st[:, 2].unsqueeze(2).to_broadcast([P, 2 * n, HD]), ALU.mult))
                if T == 0:
                    dve.wait_ge(loaded.sem, l0 + 32)
                for s in range(2):
                    vs = v[:, s * n:(s + 1) * n]
                    kit.dve(nc.vector.tensor_tensor(vs, vs, qkg[:, s].unsqueeze(1).to_broadcast([P, n, HD]), ALU.mult))


def stick_breaking(kit, proj, tT, cat):
    nc = kit.nc
    H = SB_HEADS
    scored, zed, logged, kept, summed, logw, weighed, ready, mixed = (
        kit.count(n) for n in ("sb_scored", "sb_z", "sb_log", "sb_kept", "sb_after", "sb_logw", "sb_exped", "sb_ready",
                               "sb_mixed"))
    base = {c: c.n for c in (scored, zed, logged, kept, summed, logw, weighed, ready, mixed)}
    with kit.sb("z", [P, H, NT, SEQ]) as z, kit.sb("lg", [P, H, NT, SEQ]) as lg, kit.sb("lk", [P, H, NT, SEQ]) as lk, \
            nc.Block() as block:
        @block.tensor
        def _(pe):
            for hh in range(H):
                b, c = hh % 2 * HD, hh // 2
                for kt in range(NT):
                    mm = nc.tensor.matmul(kit.bank[hh][:, kt * SEQ:(kt + 1) * SEQ],
                                          tT[b:b + HD, 2 + c, kt * P:(kt + 1) * P], tT[b:b + HD, c, :],
                                          start=True, stop=True)
                scored.up(mm)
            for hh in range(H):
                pe.wait_ge(kept.sem, base[kept] + hh + 1)
                bank = kit.bank[4 + hh % 4]
                nc.tensor.matmul(bank[:, 0:SEQ], kit.after, lk[:, hh, 0, :], start=True, stop=False)
                nc.tensor.matmul(bank[:, 0:SEQ], kit.ones[:, 0:P], lk[:, hh, 1, :], start=False, stop=True)
                summed.up(nc.tensor.matmul(bank[:, SEQ:2 * SEQ], kit.after, lk[:, hh, 1, :], start=True, stop=True))
            for hh in range(H):
                pe.wait_ge(ready.sem, base[ready] + hh + 1)
                for T in range(NT):
                    for kt in range(T + 1):
                        mm = nc.tensor.matmul(kit.bank[0][:, (T * H + hh) * HD:(T * H + hh + 1) * HD],
                                              z[:, hh, kt, T * P:(T + 1) * P],
                                              proj[:, kt, (2 * H + hh) * HD:(2 * H + hh + 1) * HD],
                                              start=(kt == 0), stop=(kt == T))
                mixed.up(mm)

        @block.scalar
        def _(act):
            for hh in range(H):
                act.wait_ge(scored.sem, base[scored] + hh + 1)
                zv = z[:, hh].rearrange("p k q -> p (k q)")
                lv = lg[:, hh].rearrange("p k q -> p (k q)")
                zed.up(nc.scalar.activation(zv, kit.bank[hh][:, :], ACT.Copy, scale=SCALE))
                kit.act(nc.scalar.activation(lv, kit.bank[hh][:, :], ACT.Abs, scale=SCALE))
                kit.act(nc.scalar.activation(lv, lv, ACT.Exp, scale=-1.0))
                logged.up(nc.scalar.activation(lv, lv, ACT.Ln, bias=1.0))
            for hh in range(H):
                act.wait_ge(logw.sem, base[logw] + hh + 1)
                zv = z[:, hh].rearrange("p k q -> p (k q)")
                weighed.up(nc.scalar.activation(zv, zv, ACT.Exp))
            act.wait_ge(mixed.sem, base[mixed] + H)
            nc.scalar.copy(cat[:, :, 0:H * HD], kit.bank[0][:, :].rearrange("p (t n) -> p t n", t=NT))

        @block.vector
        def _(dve):
            for hh in range(H):
                dve.wait_ge(zed.sem, base[zed] + hh + 1)
                dve.wait_ge(logged.sem, base[logged] + hh + 1)
                kit.dve(nc.vector.scalar_tensor_tensor(out=lg[:, hh], in0=z[:, hh], scalar=0.0, in1=lg[:, hh],
                                                       op0=ALU.max, op1=ALU.add))
                kept.up(nc.vector.scalar_tensor_tensor(out=lk[:, hh], in0=lg[:, hh], scalar=-1.0, in1=kit.strict,
                                                       op0=ALU.mult, op1=ALU.mult))
                kit.dve(nc.vector.tensor_tensor(z[:, hh], z[:, hh], lg[:, hh], ALU.subtract))
            for hh in range(H):
                dve.wait_ge(summed.sem, base[summed] + hh + 1)
                logw.up(nc.vector.tensor_tensor(z[:, hh], z[:, hh], kit.bank[4 + hh % 4][:, :].rearrange(
                    "p (k q) -> p k q", k=NT), ALU.add))
            for hh in range(H):
                dve.wait_ge(weighed.sem, base[weighed] + hh + 1)
                ready.up(nc.vector.tensor_tensor(z[:, hh], z[:, hh], kit.strict, ALU.mult))


def dilated(kit, dram, proj, tT, cat, v0):
    nc = kit.nc
    G, J = DIL_GROUPS, GROUP_HEADS
    loaded, rowed, copied, stored = (kit.count(n) for n in ("loaded", "bias_rows", "bias_copied", "bias_stored"))
    l0, r0, c0, t0 = loaded.n, rowed.n, copied.n, stored.n
    scratch = dram["bias_scratch"]
    with kit.sb("bias", [P, NT, DIL_HEADS, SEQ]) as bias:
        with kit.sb("onehot", [N_BUCKETS + 1, G, 512]) as onehot, kit.sb("table", [N_BUCKETS + 1, DIL_HEADS]) as table, \
                kit.sb("bias_rows", [J, G, 512]) as rows, nc.Block() as block:
            @block.vector
            def _(dve):
                nc.vector.memset(table[N_BUCKETS:N_BUCKETS + 1, :], NEG).then_inc(rowed.sem, 1)
                rowed.n += 1

            @block.sync
            def _(sp):
                kit.load(sp, onehot[:], dram["onehot"])
                kit.load(sp, table[0:N_BUCKETS, :], dram["rel_bias_2"])
                sp.wait_ge(copied.sem, c0 + G)
                stored.up(sp.dma_start(scratch.rearrange("(g j) n -> j g n", g=G), rows[:]), 16)
                sp.wait_ge(stored.sem, t0 + 16)
                for T in range(NT):
                    src = bass.AP(scratch.tensor, scratch.offset + T * P, [[1, P], [512, DIL_HEADS], [1, SEQ]])
                    kit.load(sp, bias[:, T], src)
                sp.wait_ge(loaded.sem, l0 + 64)

            @block.tensor
            def _(pe):
                pe.wait_ge(loaded.sem, l0 + 32)
                pe.wait_ge(rowed.sem, r0 + 1)
                for g in range(G):
                    rowed.up(nc.tensor.matmul(kit.bank[g][0:J, :], table[:, g * J:(g + 1) * J], onehot[:, g, :],
                                              start=True, stop=True))

            @block.scalar
            def _(act):
                for g in range(G):
                    act.wait_ge(rowed.sem, r0 + 2 + g)
                    copied.up(nc.scalar.copy(rows[:, g, :], kit.bank[g][0:J, :]))

        units = [(T, j) for T in range(NT) for j in range(J)]
        nu = len(units)
        scored, masked = kit.count("scored"), kit.count("score_masked")
        negmax, exped = kit.count("negmax_ready"), kit.count("exped")
        s0, k0, n0, x0 = scored.n, masked.n, negmax.n, exped.n
        with kit.sb("probs", [P, nu, G * SEQ]) as probs, kit.sb("PT", [P, 4, 4, P]) as PT, \
                kit.sb("gmax", [P, nu, G]) as gmax, kit.sb("rows", [P, 4, nu]) as rows:
            chunks = [[c for c in range(2 * G) if c % 2 <= T] for T, _ in units]
            pe_side, act_side, m_end = attend(
                kit, chunks, PT, lambda u: kit.bank[4][:, u * HD:(u + 1) * HD],
                lambda u, c: probs[:, u, c * P:(c + 1) * P],
                lambda u, c: proj[:, c % 2, v0 + (c // 2 * J + units[u][1]) * HD:v0 + (c // 2 * J + units[u][1] + 1) * HD])
            mixed = kit.count("values_mixed")
            with nc.Block() as block:
                @block.tensor
                def _(pe):
                    for u, (T, j) in enumerate(units):
                        for g in range(G):
                            n = u * G + g
                            if n >= 4:
                                pe.wait_ge(masked.sem, k0 + n - 3)
                            hh = g * J + j
                            b = hh % 2 * HD
                            scored.up(nc.tensor.matmul(kit.bank[n % 4][:, 0:SEQ], tT[b:b + HD, 4 + hh // 2, T * P:(T + 1) * P],
                                                       tT[b:b + HD, 10 + hh // 2, :], start=True, stop=True))
                    pe.wait_ge(masked.sem, k0 + nu * G)
                    pe_side(pe, lambda pe, u: pe.wait_ge(exped.sem, x0 + u + 1))

                @block.vector
                def _(dve):
                    for u, (T, j) in enumerate(units):
                        for g in range(G):
                            n = u * G + g
                            dve.wait_ge(scored.sem, s0 + n + 1)
                            masked.up(nc.vector.tensor_tensor_reduce(
                                out=probs[:, u, g * SEQ:(g + 1) * SEQ], in0=kit.bank[n % 4][:, 0:SEQ],
                                in1=bias[:, T, g * J + j, ::-1], scale=SCALE, scalar=NEG, op0=ALU.add, op1=ALU.max,
                                accum_out=gmax[:, u, g:g + 1]))
                    dve.wait_ge(masked.sem, k0 + nu * G)
                    kit.dve(nc.vector.tensor_reduce(rows[:, 0], gmax[:], AX, ALU.max))
                    negmax.up(nc.vector.tensor_scalar(rows[:, 1], rows[:, 0], -1.0, None, ALU.mult))
                    dve.wait_ge(exped.sem, x0 + nu)
                    kit.dve(nc.vector.reciprocal(rows[:, 3], rows[:, 2]))
                    dve.wait_ge(mixed.sem, m_end)
                    for T in range(NT):
                        nc.vector.tensor_tensor(
                            cat[:, T, SB_HEADS * HD:].rearrange("p (j d) -> p j d", d=HD),
                            kit.bank[4][:, T * J * HD:(T + 1) * J * HD].rearrange("p (j d) -> p j d", d=HD),
                            rows[:, 3, T * J:(T + 1) * J].unsqueeze(2).to_broadcast([P, J, HD]), ALU.mult)

                @block.scalar
                def _(act):
                    act.wait_ge(negmax.sem, n0 + 1)
                    for u in range(nu):
                        exped.up(nc.scalar.activation(probs[:, u], probs[:, u], ACT.Exp, bias=rows[:, 1, u:u + 1],
                                                      accum_out=rows[:, 2, u:u + 1]))
                    act_side(act)



def load_only(kit, pairs):
    loaded = kit.count("loaded")
    l0 = loaded.n
    with kit.nc.Block() as block:
        @block.sync
        def _(sp):
            for dst, src in pairs:
                kit.load(sp, dst, src)
            sp.wait_ge(loaded.sem, l0 + 16 * len(pairs))


def vector_only(kit, body, roots=()):
    with kit.nc.Block() as block:
        @block.scalar
        def _(act):
            kit.roots(act, roots)

        @block.vector
        def _(dve):
            body(dve)


def time_mix(kit, dram):
    x, h, hT = kit.x, kit.h, kit.hT
    norm_plain(kit, x, dram["mix_norm_2"][1:2, :], h)
    transpose_tokens(kit, h, hT)
    sb = kit.sb
    with sb("R", [P, NT, D]) as R, sb("K", [P, NT, D]) as K, sb("V", [P, NT, D]) as V, sb("A", [P, NT, D]) as A, \
            sb("KK", [P, NT, D]) as KK, sb("G", [P, NT, D]) as G, sb("bonus", [P, NT, RH]) as bonus, \
            sb("chunk_decay", [P, KD, NT, CH]) as PC:
        with sb("L", [P, NT, D]) as L:
            projections(kit, dram, R, K, V, A, L, G)
            prepare_keys(kit, dram, R, K, A, KK, L, bonus, PC)
        with sb("inverseT", [P, NT * RH, P]) as inv:
            invert(kit, dram, A, KK, inv)
            with sb("states", [P, CH + 1, KD, HD]) as S:
                vector_only(kit, lambda dve: kit.nc.vector.memset(S[:, CH], 0.0))
                for T in range(NT):
                    recur(kit, T, R, K, V, A, KK, PC, inv, S)
        finish_mix(kit, dram, R, V, G, bonus)


def projections(kit, dram, R, K, V, A, L, G):
    nc, W = kit.nc, kit.weights
    hT = kit.hT
    xx = kit.h[:].rearrange("p t (a n) -> p (t a) n", n=SEQ)
    with kit.sb("mixed", [P, 3, KD, SEQ]) as xm, kit.sb("mix_rows", [6 * KD, P]) as mix_rows, kit.sb("mixT", [P, 6 * KD]) as mixT:
        load_only(kit, [(mix_rows[:], dram["rw_mix_2"].rearrange("e i (k p) -> (e i k) p", p=P))])
        transposes(kit, [([mix_rows[:]], mixT[:].unsqueeze(1))])

        def shift(dve):
            nc.vector.tensor_scalar(xx[:, :, 0:1], hT[:, :, 0:1], -1.0, None, ALU.mult)
            kit.dve(nc.vector.tensor_tensor(xx[:, :, 1:], hT[:, :, 0:SEQ - 1], hT[:, :, 1:], ALU.subtract))

        def mixes(which):
            def body(dve):
                if which[0] == 0:
                    shift(dve)
                for n, i in enumerate(which):
                    for k in range(KD):
                        nc.vector.scalar_tensor_tensor(out=xm[:, n, k], in0=xx[:, k], scalar=mixT[:, i * KD + k:i * KD + k + 1],
                                                       in1=hT[:, k], op0=ALU.mult, op1=ALU.add)
            return body

        vector_only(kit, mixes((0, 2, 3)))
        linear(kit, None, 12, False,
               lambda b, bank: nc.scalar.copy((R, K, V)[b // 4][:, :, b % 4 * BLK:(b % 4 + 1) * BLK], bank),
               lhs_of=lambda pe, b: xm[:, b // 4])
        vector_only(kit, mixes((1, 4, 5)))
        with kit.sb("w1", [P, KD, 64]) as w1, kit.sb("a1", [P, KD, 64]) as a1, kit.sb("g1", [P, KD, 160]) as g1, \
                kit.sb("w2", [64, D]) as w2, kit.sb("a2", [64, D]) as a2, kit.sb("g2", [P, D]) as g2, \
                kit.sb("g2b", [32, D]) as g2b, kit.sb("w0", [P, D]) as w0, kit.sb("a0", [P, D]) as a0, \
                kit.sb("tw", [64, SEQ]) as tw, kit.sb("ta", [64, SEQ]) as ta, kit.sb("tg", [P, SEQ]) as tg, \
                kit.sb("tgb", [32, SEQ]) as tgb:
            load_only(kit, [(t[:], dram[n][0].rearrange("(k p) n -> p k n", p=P)) for t, n in
                            ((w1, "rw_w1_2"), (a1, "rw_a1_2"), (g1, "rw_g1_2"))] +
                      [(w2[:], dram["rw_w2_2"][0]), (a2[:], dram["rw_a2_2"][0]), (g2[:], dram["rw_g2_2"][0, 0:P]),
                       (g2b[:], dram["rw_g2_2"][0, P:160]), (w0[:], bcast(dram["rw_w0_2"], D)),
                       (a0[:], bcast(dram["rw_a0_2"], D))])
            inner, innered, outer, biased = (kit.count(n) for n in ("lora_in", "lora_in_copied", "lora_out", "lora_biased"))
            i0, c0, o0, z0 = inner.n, innered.n, outer.n, biased.n
            with nc.Block() as block:
                @block.tensor
                def _(pe):
                    for n, (w, lo, hi) in enumerate(((w1, 0, 64), (a1, 0, 64), (g1, 0, P), (g1, P, 160))):
                        for k in range(KD):
                            mm = nc.tensor.matmul(kit.bank[n][0:hi - lo, 0:SEQ], w[:, k, lo:hi], xm[:, min(n, 2), k],
                                                  start=(k == 0), stop=(k == KD - 1))
                        inner.up(mm)
                    for n, parts in enumerate((((tw, w2),), ((ta, a2),), ((tg, g2), (tgb, g2b)))):
                        pe.wait_ge(innered.sem, c0 + (1 if n == 0 else 4))
                        for q in range(4):
                            T, half = q // 2, q % 2
                            if n == 2:
                                pe.wait_ge(biased.sem, z0 + q + 1)
                            for i, (t, w) in enumerate(parts):
                                mm = nc.tensor.matmul(kit.bank[(4 if n != 1 else 0) + q][:, :], t[:, T * P:(T + 1) * P],
                                                      w[:, half * 512:(half + 1) * 512],
                                                      start=(i == 0), stop=(i == len(parts) - 1))
                            outer.up(mm)

                @block.scalar
                def _(act):
                    for n, (t, rows, func) in enumerate(((tw, 64, ACT.Tanh), (ta, 64, ACT.Copy), (tg, P, ACT.Sigmoid),
                                                         (tgb, 32, ACT.Sigmoid))):
                        act.wait_ge(inner.sem, i0 + n + 1)
                        innered.up(nc.scalar.activation(t[:], kit.bank[n][0:rows, 0:SEQ], func))
                    for n, dst in enumerate((L, A)):
                        act.wait_ge(biased.sem, z0 + 4 * n + 4)
                        nc.scalar.activation(dst[:], dst[:], ACT.Sigmoid)
                    for q in range(4):
                        act.wait_ge(outer.sem, o0 + 8 + q + 1)
                        nc.scalar.copy(G[:, q // 2, q % 2 * 512:(q % 2 + 1) * 512], kit.bank[4 + q][:, :])

                @block.vector
                def _(dve):
                    for n, (dst, row) in enumerate(((L, w0), (A, a0))):
                        for q in range(4):
                            T, cols = q // 2, slice(q % 2 * 512, (q % 2 + 1) * 512)
                            dve.wait_ge(outer.sem, o0 + 4 * n + q + 1)
                            biased.up(nc.vector.tensor_tensor(dst[:, T, cols], kit.bank[(4 if n == 0 else 0) + q][:, :],
                                                              row[:, cols], ALU.add))


def heads(a):
    return a.rearrange("p (h d) -> p h d", d=HD)


def wide(row, n=HD):
    return row.unsqueeze(2).to_broadcast([P, row.shape[1], n])


def prepare_keys(kit, dram, R, K, A, KK, L, bonus, PC):
    nc = kit.nc
    ready, summed, exped, tmp_free, shifted = (kit.count(n) for n in ("log_decay_ready", "log_decay_summed", "decay_exped",
                                                                     "tmp_free", "log_decay_shifted"))
    r0, s0, x0, t0, h0 = ready.n, summed.n, exped.n, tmp_free.n, shifted.n
    with kit.sb("kk_w", [P, 3, D]) as rows, kit.sb("decay", [P, NT, D]) as up, kit.sb("rsum", [P, 4, RH]) as rs:
        down = kit.h
        load_only(kit, [(rows[:, 0], bcast(dram["rw_kk_2"], D)), (rows[:, 1], bcast(dram["rw_ka_2"], D)),
                        (rows[:, 2], bcast(dram["rw_rk_2"].rearrange("e h d -> e (h d)"), D))])
        with nc.Block() as block:
            @block.vector
            def _(dve):
                ready.up(nc.vector.tensor_scalar(L[:], L[:], -float(np.exp(-0.5)), None, ALU.mult))
                for T in range(NT):
                    t = down[:, T]
                    kit.dve(nc.vector.tensor_tensor(KK[:, T], K[:, T], rows[:, 0], ALU.mult))
                    kit.dve(nc.vector.tensor_tensor(t, KK[:, T], KK[:, T], ALU.mult))
                    kit.dve(nc.vector.tensor_reduce(rs[:, 0], heads(t), AX, ALU.add))
                    kit.rsqrt(dve, nc.vector.tensor_scalar(rs[:, 1], rs[:, 0], 1e-24, None, ALU.max), rs[:, 2], rs[:, 2])
                    kit.dve(nc.vector.tensor_tensor(heads(KK[:, T]), heads(KK[:, T]), wide(rs[:, 2]), ALU.mult))
                    kit.dve(nc.vector.scalar_tensor_tensor(out=t, in0=A[:, T], scalar=-1.0, in1=rows[:, 1],
                                                           op0=ALU.add, op1=ALU.mult))
                    kit.dve(nc.vector.scalar_tensor_tensor(out=K[:, T], in0=t, scalar=1.0, in1=K[:, T],
                                                           op0=ALU.add, op1=ALU.mult))
                    kit.dve(nc.vector.tensor_tensor(t, R[:, T], K[:, T], ALU.mult))
                    kit.dve(nc.vector.tensor_tensor(t, t, rows[:, 2], ALU.mult))
                    kit.dve(nc.vector.tensor_reduce(bonus[:, T], heads(t), AX, ALU.add))
                    kit.dve(nc.vector.tensor_tensor(A[:, T], A[:, T], KK[:, T], ALU.mult))
                tmp_free.up(nc.vector.memset(kit.spare[:, 0:1], 0.0))
                dve.wait_ge(summed.sem, s0 + 2)
                for q in range(4):
                    T, cols = q // 2, slice(q % 2 * 512, (q % 2 + 1) * 512)
                    shifted.up(nc.vector.tensor_tensor(L[:, T, cols], kit.bank[q][:, :], L[:, T, cols], ALU.subtract))
                dve.wait_ge(exped.sem, x0 + 4)
                nc.vector.tensor_tensor(R[:], R[:], up[:], ALU.mult)
                dve.wait_ge(exped.sem, x0 + 8)
                nc.vector.tensor_tensor(K[:], K[:], down[:], ALU.mult)
                nc.vector.tensor_tensor(A[:], A[:], down[:], ALU.mult)
                dve.wait_ge(exped.sem, x0 + 9)
                nc.vector.scalar_tensor_tensor(out=KK[:], in0=KK[:], scalar=-1.0, in1=L[:], op0=ALU.mult, op1=ALU.mult)

            @block.tensor
            def _(pe):
                pe.wait_ge(ready.sem, r0 + 1)
                for q in range(4):
                    mm = nc.tensor.matmul(kit.bank[q][:, :], kit.le, L[:, q // 2, q % 2 * 512:(q % 2 + 1) * 512],
                                          start=True, stop=True)
                summed.up(mm)
                for k in range(KD):
                    for T in range(NT):
                        n = (k * NT + T) * CH
                        mm = nc.tensor.matmul(kit.bank[4][:, n:n + CH], L[:, T, k * P:(k + 1) * P], kit.ends,
                                              start=True, stop=True)
                summed.up(mm)

            @block.scalar
            def _(act):
                kit.roots(act, [(rs[:, 2], rs[:, 1])] * NT)
                act.wait_ge(summed.sem, s0 + 2)
                nc.scalar.activation(PC[:].rearrange("p k t c -> p (k t c)"), kit.bank[4][:, 0:KD * NT * CH], ACT.Exp)
                for q in range(4):
                    act.wait_ge(shifted.sem, h0 + q + 1)
                    exped.up(nc.scalar.activation(up[:, q // 2, q % 2 * 512:(q % 2 + 1) * 512], kit.bank[q][:, :], ACT.Exp))
                act.wait_ge(tmp_free.sem, t0 + 1)
                for q in range(4):
                    exped.up(nc.scalar.activation(down[:, q // 2, q % 2 * 512:(q % 2 + 1) * 512], kit.bank[q][:, :],
                                                  ACT.Exp, scale=-1.0))
                act.wait_ge(shifted.sem, h0 + 4)
                exped.up(nc.scalar.activation(L[:], L[:], ACT.Exp))


def invert(kit, dram, A, KK, inv):
    nc = kit.nc
    NS = NT * RH
    grams, masked, stored, loaded, solved = (kit.count(n) for n in ("grams", "grams_masked", "systems_stored", "loaded",
                                                                    "solved"))
    g0, m0, t0, l0, v0 = grams.n, masked.n, stored.n, loaded.n, solved.n
    tri, out = (dram[n].rearrange("(u c) (j t) -> c j u t", c=CH, j=C) for n in ("systems", "inverses"))
    with kit.sb("sysd", [P, NS, C]) as sysd, kit.sb("sys", [P, C, C]) as sy, kit.sb("XT", [P, C, C]) as XT, \
            kit.sb("terms", [P, C, C]) as terms:
        with kit.sb("aT", [P, NT * KD, P]) as aT, kit.sb("bT", [P, NT * KD, P]) as bT:
            transposes(kit, [([src[:, T, (k + i) * P:(k + i + 1) * P] for i in range(4)],
                              dst[:, T * KD + k:T * KD + k + 4, :])
                             for src, dst in ((KK, aT), (A, bT)) for T in range(NT) for k in (0, 4)])
            with nc.Block() as block:
                @block.tensor
                def _(pe):
                    for n in range(NS // 4):
                        if n >= 4:
                            pe.wait_ge(masked.sem, m0 + (n - 3) * CH)
                        for i in range(4):
                            b, p = n % 2 * HD, n // 2 * 4 + i
                            mm = nc.tensor.matmul(kit.bank[n % 4][:, i * P:(i + 1) * P], bT[b:b + HD, p, :],
                                                  aT[b:b + HD, p, :], start=True, stop=True)
                        grams.up(mm)

                @block.vector
                def _(dve):
                    for n in range(NS // 4):
                        dve.wait_ge(grams.sem, g0 + n + 1)
                        for c in range(CH):
                            r = slice(c * C, (c + 1) * C)
                            bank = kit.bank[n % 4][:, :].rearrange("p (u t) -> p u t", u=4)
                            u = n // 2 * 8 + n % 2
                            masked.up(nc.vector.tensor_tensor(sysd[r, u:u + 7:2, :], bank[r, :, r],
                                                              kit.lt[r, r].unsqueeze(1).to_broadcast([C, 4, C]), ALU.mult))

        with nc.Block() as block:
            @block.sync
            def _(sp):
                for c in range(CH):
                    stored.up(sp.dma_start(tri[c], sysd[c * C:(c + 1) * C]), 16)
                sp.wait_ge(stored.sem, t0 + 16 * CH)
                kit.load(sp, sy[:], dram["systems"].rearrange("s (j t) -> s j t", j=C))
                sp.wait_ge(solved.sem, v0 + 1)
                stored.up(sp.dma_start(dram["inverses"].rearrange("s (j t) -> s j t", j=C), XT[:]), 16)
                sp.wait_ge(stored.sem, t0 + 16 * (CH + 1))
                for c in range(CH):
                    r = slice(c * C, (c + 1) * C)
                    kit.load(sp, inv[r, :, r], out[c])
                sp.wait_ge(loaded.sem, l0 + 16 * (CH + 1))

            @block.vector
            def _(dve):
                kit.dve(nc.vector.memset(XT[:], 0.0))
                kit.dve(nc.vector.memset(XT[:].rearrange("p j t -> p (j t)")[:, 0::C + 1], 1.0))
                nc.vector.memset(inv[:], 0.0)
                dve.wait_ge(loaded.sem, l0 + 16)
                for t in range(1, C):
                    kit.dve(nc.vector.tensor_tensor(terms[:, 0:t, 0:t], XT[:, 0:t, 0:t],
                                                    sy[:, 0:t, t].unsqueeze(1).to_broadcast([P, t, t]), ALU.mult))
                    ins = nc.vector.tensor_reduce(XT[:, 0:t, t], terms[:, 0:t, 0:t], AX, ALU.add)
                    if t < C - 1:
                        kit.dve(ins)
                    else:
                        solved.up(ins)


def recur(kit, T, R, K, V, A, KK, PC, inv, S):
    nc = kit.nc
    KT = kit.hT[:].rearrange("p a n -> p (a n)")[:, 0:KD * P].rearrange("p (a n) -> p a n", n=P)
    BT = kit.hT[:].rearrange("p a n -> p (a n)")[:, KD * P:].rearrange("p (a n) -> p a n", n=P)
    Q, U = kit.h[:, 0], kit.h[:, 1]
    with kit.sb("arT", [P, KD, 2, P]) as arT, kit.sb("GK", [P, RH, 2 * P]) as GK, kit.sb("GB", [P, RH, P]) as GB, \
            kit.sb("W1T", [P, KD, P]) as W1T, kit.sb("W2", [P, D]) as W2:
        flat = arT[:].rearrange("p k s t -> p (k s) t")
        jobs = []
        for k in range(0, KD, 2):
            jobs.append(([s[:, T, (k + i) * P:(k + i + 1) * P] for i in range(2) for s in (KK, R)], flat[:, 2 * k:2 * k + 4]))
        for src, dst in ((K, KT), (A, BT)):
            for k in (0, 4):
                jobs.append(([src[:, T, (k + i) * P:(k + i + 1) * P] for i in range(4)], dst[:, k:k + 4]))
        transposes(kit, jobs)
        place = lambda hh: (slice(hh % 2 * HD, (hh % 2 + 1) * HD), hh // 2)
        cols = lambda hh: slice(hh * HD, (hh + 1) * HD)
        parity = lambda a, i: a.rearrange("p (a b d) -> p a b d", b=2, d=HD)[:, :, i]

        grams, masked = kit.count("grams"), kit.count("grams_masked")
        g0, m0 = grams.n, masked.n
        with nc.Block() as block:
            @block.tensor
            def _(pe):
                for n in range(KD):
                    if n >= 4:
                        pe.wait_ge(masked.sem, m0 + n - 3)
                    r, _ = place(n % 2)
                    for i in range(2):
                        p = n // 2 * 2 + i
                        mm = nc.tensor.matmul(kit.bank[n % 4][:, i * BLK:(i + 1) * BLK], KT[r, p, :],
                                              arT[r, p].rearrange("p s t -> p (s t)"), start=True, stop=True)
                    grams.up(mm)
                for n in range(4):
                    r, _ = place(n % 2)
                    for i in range(4):
                        p = n // 2 * 4 + i
                        mm = nc.tensor.matmul(kit.bank[4 + n][:, i * P:(i + 1) * P], BT[r, p, :], arT[r, p, 1, :],
                                              start=True, stop=True)
                    grams.up(mm)

            @block.vector
            def _(dve):
                for p in range(KD):
                    dve.wait_ge(grams.sem, g0 + p + 1)
                    u = p // 2 * 4 + p % 2
                    masked.up(nc.vector.tensor_tensor(GK[:, u:u + 3:2], kit.bank[p % 4][:, :].rearrange(
                        "p (a t) -> p a t", a=2), kit.ltle.unsqueeze(1).to_broadcast([P, 2, 2 * P]), ALU.mult))
                for n in range(4):
                    dve.wait_ge(grams.sem, g0 + KD + n + 1)
                    u = n // 2 * 8 + n % 2
                    nc.vector.tensor_tensor(GB[:, u:u + 7:2], kit.bank[4 + n][:, :].rearrange(
                        "p (a t) -> p a t", a=4), kit.le.unsqueeze(1).to_broadcast([P, 4, P]), ALU.mult)

        made, copied = kit.count("within_made"), kit.count("within_copied")
        d0, c0 = made.n, copied.n
        with nc.Block() as block:
            @block.tensor
            def _(pe):
                for hh in range(RH):
                    mm = nc.tensor.matmul(kit.bank[hh // 8][:, hh % 8 * HD:(hh % 8 + 1) * HD], GK[:, hh, 0:P],
                                          V[:, T, cols(hh)], start=True, stop=True)
                made.up(mm)
                for hh in range(RH):
                    r, p = place(hh)
                    mm = nc.tensor.matmul(kit.bank[2 + p // 4][r, p % 4 * P:(p % 4 + 1) * P], KK[:, T, cols(hh)],
                                          inv[:, T * RH + hh, :], start=True, stop=True)
                made.up(mm)
                pe.wait_ge(copied.sem, c0 + 2)
                for hh in range(RH):
                    mm = nc.tensor.matmul(kit.bank[4 + hh // 8][:, hh % 8 * HD:(hh % 8 + 1) * HD],
                                          inv[:, T * RH + hh, :], Q[:, cols(hh)], start=True, stop=True)
                made.up(mm)

            @block.scalar
            def _(act):
                act.wait_ge(made.sem, d0 + 1)
                for i in range(2):
                    copied.up(nc.scalar.copy(Q[:, i * 512:(i + 1) * 512], kit.bank[i][:, :]))
                act.wait_ge(made.sem, d0 + 2)
                for i in range(2):
                    nc.scalar.copy(W1T[:, 4 * i:4 * i + 4], kit.bank[2 + i][:, :].rearrange("p (a t) -> p a t", a=4))

            @block.vector
            def _(dve):
                nc.vector.tensor_copy(S[:, 0], S[:, CH])
                dve.wait_ge(made.sem, d0 + 3)
                for i in range(2):
                    nc.vector.tensor_copy(W2[:, i * 512:(i + 1) * 512], kit.bank[4 + i][:, :])

        read, filled, written, grown = (kit.count(n) for n in ("state_read", "u_filled", "state_products", "state_grown"))
        e0, f0, w0, n0 = read.n, filled.n, written.n, grown.n
        with nc.Block() as block:
            @block.tensor
            def _(pe):
                for c in range(CH):
                    t = slice(c * C, (c + 1) * C)
                    if c:
                        pe.wait_ge(grown.sem, n0 + c)
                    for hh in range(RH):
                        r, p = place(hh)
                        mm = nc.tensor.matmul(kit.bank[hh % 2][t, cols(p)], W1T[r, p, t],
                                              S[r, c, p, :], start=True, stop=True)
                    read.up(mm)
                    pe.wait_ge(filled.sem, f0 + 2 * c + 2)
                    for hh in range(RH):
                        r, p = place(hh)
                        o = kit.bank[2][r, p * HD:(p + 1) * HD]
                        nc.tensor.matmul(o, K[t, T, cols(hh)], V[t, T, cols(hh)], start=True, stop=False,
                                         tile_position=(c * C, hh % 2 * HD))
                        mm = nc.tensor.matmul(o, A[t, T, cols(hh)], U[t, cols(hh)], start=False, stop=True,
                                              tile_position=(c * C, hh % 2 * HD))
                    written.up(mm)

            @block.vector
            def _(dve):
                for c in range(CH):
                    t = slice(c * C, (c + 1) * C)
                    dve.wait_ge(read.sem, e0 + c + 1)
                    for i in range(2):
                        filled.up(nc.vector.tensor_tensor(parity(U, i)[t], heads(kit.bank[i][:, :])[t],
                                                          parity(W2[:], i)[t], ALU.add))
                    dve.wait_ge(written.sem, w0 + c + 1)
                    kit.dve(nc.vector.tensor_tensor(S[:, c + 1], kit.bank[2][:, :].rearrange("p (a v) -> p a v", v=HD),
                                                    S[:, c], ALU.add))
                    grown.up(nc.vector.tensor_tensor(S[:, c + 1], S[:, c + 1], wide(PC[:, :, T, c]), ALU.mult))

        y0 = made.n
        with nc.Block() as block:
            @block.tensor
            def _(pe):
                for hh in range(RH):
                    r, p = place(hh)
                    o = kit.bank[hh // 8][:, hh % 8 * HD:(hh % 8 + 1) * HD]
                    nc.tensor.matmul(o, GK[:, hh, P:2 * P], V[:, T, cols(hh)], start=True, stop=False)
                    mm = nc.tensor.matmul(o, GB[:, hh, :], U[:, cols(hh)], start=False, stop=True)
                made.up(mm)
                for hh in range(RH):
                    r, p = place(hh)
                    for c in range(CH):
                        t = slice(c * C, (c + 1) * C)
                        mm = nc.tensor.matmul(kit.bank[2 + hh % 2][t, cols(p)],
                                              arT[r, p, 1, t], S[r, c, p, :], start=True, stop=True)
                made.up(mm)

            @block.vector
            def _(dve):
                dve.wait_ge(made.sem, y0 + 1)
                for i in range(2):
                    kit.dve(nc.vector.tensor_copy(R[:, T, i * 512:(i + 1) * 512], kit.bank[i][:, :]))
                dve.wait_ge(made.sem, y0 + 2)
                for i in range(2):
                    v = parity(R[:, T], i)
                    kit.dve(nc.vector.tensor_tensor(v, v, heads(kit.bank[2 + i][:, :]), ALU.add))


def finish_mix(kit, dram, R, V, G, bonus):
    nc = kit.nc
    with kit.sb("ln", [P, 2, D]) as ln, kit.sb("sq", [P, D]) as sq, kit.sb("st", [P, 4, RH]) as st:
        load_only(kit, [(ln[:, 0], bcast(dram["rw_lnx_g_2"], D)), (ln[:, 1], bcast(dram["rw_lnx_b_2"], D))])

        def body(dve):
            for T in range(NT):
                y, v = R[:, T], V[:, T]
                kit.dve(nc.vector.tensor_reduce(st[:, 0], heads(y), AX, ALU.add))
                kit.dve(nc.vector.tensor_scalar(st[:, 0], st[:, 0], 1.0 / HD, None, ALU.mult))
                kit.dve(nc.vector.tensor_tensor(heads(y), heads(y), wide(st[:, 0]), ALU.subtract))
                kit.dve(nc.vector.tensor_tensor(sq[:], y, y, ALU.mult))
                kit.dve(nc.vector.tensor_reduce(st[:, 1], heads(sq[:]), AX, ALU.add))
                kit.rsqrt(dve, nc.vector.tensor_scalar(st[:, 2], st[:, 1], 1.0 / HD, GN_EPS, ALU.mult, ALU.add), st[:, 3], st[:, 3])
                kit.dve(nc.vector.tensor_tensor(heads(y), heads(y), wide(st[:, 3]), ALU.mult))
                kit.dve(nc.vector.tensor_tensor(y, y, ln[:, 0], ALU.mult))
                kit.dve(nc.vector.tensor_tensor(y, y, ln[:, 1], ALU.add))
                kit.dve(nc.vector.tensor_tensor(heads(v), heads(v), wide(bonus[:, T]), ALU.mult))
                kit.dve(nc.vector.tensor_tensor(y, y, v, ALU.add))
                kit.dve(nc.vector.tensor_tensor(y, y, G[:, T], ALU.mult))
        vector_only(kit, body, roots=[(st[:, 3], st[:, 2])] * NT)
    transpose_tokens(kit, R, kit.hT)

    def add(b, bank):
        c = slice(b * BLK, (b + 1) * BLK)
        return nc.vector.tensor_tensor(kit.x[:, :, c], kit.x[:, :, c], bank, ALU.add)
    linear(kit, kit.hT, 4, False, add, on_dve=True)



def plan_weights(W, dram):
    W.add(columns(dram["mod_w"][0]))
    W.add(columns(dram["attn_in_w"][0]))
    W.add(columns(dram["attn_out_w"][0]))
    W.add(columns(dram["peer_w_q"][0]))
    W.add(columns(dram["mod_w"][1]))
    W.add([dram["pool_w"].rearrange("e g (k p) n -> p (e g k) n", p=P)])
    W.add(columns(dram["peer_w_q"][1]))
    W.add(ffn_blocks(dram, 0, 0))
    W.add(columns(dram["attn_w_in_2"][0]))
    wo = dram["attn_w_out_2"][0].rearrange("(k p) n -> p k n", p=P)
    W.add([wo[:, :, 0:512], wo[:, :, 512:1024]])
    W.add(ffn_blocks(dram, 0, 1))
    W.add(ffn_blocks(dram, 1, 0))
    for n in ("rw_wr_2", "rw_wk_2", "rw_wv_2"):
        W.add(columns(dram[n][0]))
    W.add(columns(dram["rw_wo_2"][0]))
    W.add(ffn_blocks(dram, 1, 1))


def build(nc, dram, out):
    kit = Kit(nc, dram)
    kit.x = nc.alloc_sbuf_tensor("x_res", [P, NT, D], F32)
    kit.h = nc.alloc_sbuf_tensor("h", [P, NT, D], F32)
    kit.hT = nc.alloc_sbuf_tensor("hT", [P, KD, SEQ], F32)
    kit.ones = nc.alloc_sbuf_tensor("ones", [P, P], F32)
    kit.zeros = nc.alloc_sbuf_tensor("zeros", [1, 512], F32)
    kit.eps = nc.alloc_sbuf_tensor("eps", [P, 1], F32)[:]
    kit.spare = nc.alloc_sbuf_tensor("spare8", [P, GRING], F32)
    kit.consts = nc.alloc_sbuf_tensor("const_table", [P, sum(n for _, n in CONST_PARTS)], F32)
    at = {}
    o = 0
    for name, n in CONST_PARTS:
        at[name] = kit.consts[:, o:o + n]
        if name == "lt":
            kit.ltle = kit.consts[:, o:o + 2 * P]
        o += n
    kit.ident, kit.after, kit.lt, kit.le, kit.ends, kit.iota16 = (at[n] for n in ("ident", "after", "lt", "le", "ends", "iota16"))
    kit.strict = at["strict"].rearrange("p (t n) -> p t n", t=NT)
    kit.window = at["window"].rearrange("p (t n) -> p t n", t=NT)
    kit.cos = at["cos"].rearrange("p (t n) -> p t n", t=NT)
    kit.sin = at["sin"].rearrange("p (t n) -> p t n", t=NT)
    kit.weights = Weights(kit)
    plan_weights(kit.weights, dram)

    load_constants(kit, dram)
    with kit.sb("mod", [P, N_MOD * D]) as mod:
        with kit.sb("mod_ctx", [P, 2 * D]) as mod_ctx:
            modulation(kit, dram, 0, mod, mod_ctx)
            mixer(kit, dram, mod, mod_ctx)
        peer(kit, dram, 0, mod)
        modulation(kit, dram, 1, mod, None)
        pooling(kit, dram, mod)
        peer(kit, dram, 1, mod)
    norm_plain(kit, kit.x, dram["final_g"].rearrange("(a d) -> a d", a=1), kit.x)
    swiglu(kit, dram, 0, 0)
    parallel_attention(kit, dram)
    swiglu(kit, dram, 0, 1)
    swiglu(kit, dram, 1, 0)
    time_mix(kit, dram)
    swiglu(kit, dram, 1, 1)
    stored = kit.count("stored")
    with nc.Block() as block:
        @block.sync
        def _(sp):
            stored.up(sp.dma_start(out.rearrange("a (t p) d -> p (a t) d", p=P), kit.x[:]), 16)
            sp.wait_ge(stored.sem, 16)


INPUTS = ["x", "c", "ctx", "c_ctx", "mod_w", "mod_b", "norm1_g", "norm2_g", "attn_in_w", "attn_out_w", "attn_sink",
          "gmlp_w_s", "gmlp_b_s", "pool_w", "pool_scale", "peer_w_q", "peer_sub_keys", "peer_down", "peer_up", "final_g",
          "ffn_norm_2", "ffn_w_gate_2", "ffn_w_up_2", "ffn_w_down_2", "mix_norm_2", "rel_bias_2", "attn_w_in_2",
          "attn_q_norm_2", "attn_k_norm_2", "attn_w_out_2", "rw_mix_2", "rw_w0_2", "rw_w1_2", "rw_w2_2", "rw_a0_2",
          "rw_a1_2", "rw_a2_2", "rw_g1_2", "rw_g2_2", "rw_kk_2", "rw_ka_2", "rw_rk_2", "rw_wr_2", "rw_wk_2", "rw_wv_2",
          "rw_wo_2", "rw_lnx_g_2", "rw_lnx_b_2"]


def kernel(**inputs):
    import numpy as _np
    import concourse.bacc as _bacc
    from concourse.bass_utils import run_bass_kernel_spmd as _run

    nc = _bacc.Bacc("TRN2", target_bir_lowering=False, num_devices=1)
    arrays, dram = {}, {}
    for name in INPUTS:
        a = _np.ascontiguousarray(inputs[name])
        arrays[f"in_{name}"] = a
        dram[name] = nc.dram_tensor(f"in_{name}", a.shape, mybir.dt.from_np(a.dtype), kind="ExternalInput").ap()
    for name, a in layout_constants().items():
        arrays[f"in_{name}"] = a
        dram[name] = nc.dram_tensor(f"in_{name}", a.shape, F32, kind="ExternalInput").ap()
    for name, shape in (("bias_scratch", (DIL_HEADS, 512)), ("systems", (P, C * C)), ("inverses", (P, C * C))):
        dram[name] = nc.dram_tensor(name, shape, F32, kind="Internal").ap()
    out = nc.dram_tensor("out_0", (1, SEQ, D), F32, kind="ExternalOutput").ap()
    build(nc, dram, out)
    r = _run(nc, [arrays], core_ids=[0])
    return r.results[0]["out_0"]
```

```python
from contextlib import contextmanager

import numpy as np
import concourse.bass as bass
from concourse import mybir

F32 = mybir.dt.float32
U32 = mybir.dt.uint32
F32R = mybir.dt.float32r
ALU = mybir.AluOpType
ACT = mybir.ActivationFunctionType
AX = mybir.AxisListType.X

P = 128
SEQ = 256
NT = SEQ // P
D = 1024
KD = D // P
EPS = 1e-6
GN_EPS = 64e-5
NEG = -1e30
HD = 64
SCALE = HD ** -0.5

N_MOD = 6
Q_W, KV_W, A_W = 512, 128, 512
HEADS, GQA = 8, 4
GROUPS = 8
POOL_WINDOWS = (2, 4, 8, 16)

PH = 8
NKEYS = 128
TOPK = 16
PICKS = PH * TOPK

D_FF = 2816
BLK = 256
FF_BLOCKS = D_FF // BLK

SB_HEADS, DIL_HEADS, DIL_GROUPS, GROUP_HEADS = 4, 12, 3, 4
DIL_PATTERNS = ((128, 1), (512, 4), (2048, 16))
N_BUCKETS, MAX_DISTANCE = 32, 2048

RH = 16
C = 32
CH = P // C

SLOTS = 6
SPLIT_SLOTS = 3
GRING = 8
PE_ROWS = 32

CONST_PARTS = [("ident", P), ("after", P), ("lt", P), ("le", P), ("ends", CH), ("iota16", 16),
               ("strict", NT * SEQ), ("window", NT * 512), ("cos", NT * HD), ("sin", NT * HD)]


def layout_constants():
    t = np.arange(SEQ)
    pi = np.arange(P)
    same = (pi[:, None] // C) == (pi[None, :] // C)
    quarter = HD // 4
    inv = np.power(np.float32(10000.0), -np.arange(quarter, dtype=np.float32) / np.float32(quarter))
    row, col = (t // 64).astype(np.float32), (t % 64).astype(np.float32)
    ar, ac = row[:, None] * inv[None, :], col[:, None] * inv[None, :]
    cos = np.concatenate([np.cos(ar), np.cos(ar), np.cos(ac), np.cos(ac)], 1)
    sin = np.concatenate([-np.sin(ar), np.sin(ar), -np.sin(ac), np.sin(ac)], 1)
    window = np.zeros((SEQ, 512), np.float32)
    window[:, :SEQ] = np.where(np.abs(t[:, None] - t[None, :]) <= 128, 0.0, NEG)

    def tiles(a):
        return a.reshape(NT, P, -1).transpose(1, 0, 2).reshape(P, -1)

    parts = {
        "ident": np.eye(P), "after": (pi[:, None] > pi[None, :]),
        "lt": same & (pi[:, None] < pi[None, :]), "le": same & (pi[:, None] <= pi[None, :]),
        "ends": (pi[:, None] // C) == np.arange(CH)[None, :],
        "iota16": np.broadcast_to(np.arange(16), (P, 16)),
        "strict": tiles((t[:, None] < t[None, :]).astype(np.float32)),
        "window": tiles(window), "cos": tiles(cos), "sin": tiles(sin),
    }
    consts = np.concatenate([np.asarray(parts[n], np.float32) for n, _ in CONST_PARTS], 1)
    bands = np.zeros((len(POOL_WINDOWS), SEQ, SEQ), np.float32)
    for g, w in enumerate(POOL_WINDOWS):
        lo, hi = np.clip(t - w // 2, 0, SEQ), np.clip(t + w // 2, 0, SEQ)
        inside = (t[:, None] >= lo[None, :]) & (t[:, None] < hi[None, :])
        bands[g] = inside / (hi - lo).astype(np.float32)[None, :] - np.eye(SEQ)
    dist = np.arange(512) - (SEQ - 1)
    half = N_BUCKETS // 2
    large = half + (np.log(np.maximum(dist, 1).astype(np.float32) / half) / np.log(MAX_DISTANCE / half)
                    * (N_BUCKETS - half)).astype(np.int32)
    bucket = np.where(dist < half, dist, np.minimum(large, N_BUCKETS - 1))
    onehot = np.zeros((N_BUCKETS + 1, DIL_GROUPS, 512), np.float32)
    for g, (w, r) in enumerate(DIL_PATTERNS):
        ok = (dist >= 0) & (dist % r == 0) & (dist <= w)
        for j in range(512):
            if ok[j]:
                onehot[bucket[j], g, j] = 1.0 / SCALE
            else:
                onehot[N_BUCKETS, g, j] = 1.0
    return {"consts": np.ascontiguousarray(consts), "bands": bands, "onehot": onehot}


class Count:

    def __init__(self, nc, name):
        self.sem, self.n = nc.alloc_semaphore(name), 0

    def up(self, ins, by=1):
        ins.then_inc(self.sem, by)
        self.n += by
        return self.n


class Kit:

    def __init__(self, nc, dram):
        self.nc, self.dram, self.counts, self.taken = nc, dram, {}, 0
        self.bank = [nc.alloc_psum_tensor(f"bank{i}", [P, 512], F32) for i in range(8)]
        self.step = {e: Count(nc, f"{e}_step") for e in ("dve", "act", "pool")}

    def count(self, name):
        if name not in self.counts:
            self.counts[name] = Count(self.nc, name)
        return self.counts[name]

    def sb(self, name, shape, dt=F32):
        self.taken += 1
        return self.nc.sbuf_tensor(f"{name}_{self.taken}", shape, dt)

    def dve(self, ins):
        self.nc.vector.wait_ge(self.step["dve"].sem, self.step["dve"].up(ins))

    def act(self, ins):
        self.nc.scalar.wait_ge(self.step["act"].sem, self.step["act"].up(ins))

    def roots(self, act, jobs):
        ready, made = self.count("variance_ready"), self.count("root_made")
        for i, (dst, src) in enumerate(jobs):
            act.wait_ge(ready.sem, made.n + 1)
            made.up(self.nc.scalar.activation(dst, src, ACT.Sqrt))

    def rsqrt(self, dve, ins, dst, src):
        n = self.count("variance_ready").up(ins)
        dve.wait_ge(self.count("root_made").sem, n)
        self.dve(self.nc.vector.reciprocal(dst, src))

    def load(self, eng, dst, src, slow=False):
        self.count("loaded").up(eng.dma_start(dst, src, allow_slow_non_contiguous=slow), 16)


class Weights:

    def __init__(self, kit):
        nc = kit.nc
        self.ring = nc.alloc_sbuf_tensor("weight_ring", [P, SLOTS, 2048], F32)
        self.landed = [nc.alloc_semaphore(f"block_landed{i}") for i in range(SLOTS)]
        self.multiplied = nc.alloc_semaphore("block_multiplied")
        self.blocks, self.issued, self.used = [], 0, 0

    def add(self, srcs):
        self.blocks += srcs

    def tile(self, b, kc):
        return self.ring[:, b % SLOTS, :].rearrange("p (k n) -> p k n", k=kc)

    def issue(self, sp, upto):
        for b in range(self.issued, min(upto, len(self.blocks))):
            if b >= SLOTS:
                sp.wait_ge(self.multiplied, b - SLOTS + 1)
            src = self.blocks[b]
            sp.dma_start(self.tile(b, src.shape[1]), src).then_inc(self.landed[b % SLOTS], 16)
        self.issued = max(self.issued, min(upto, len(self.blocks)))

    def wait(self, pe, b):
        pe.wait_ge(self.landed[b % SLOTS], 16 * (b // SLOTS + 1))


def bcast(row, n):
    return row.partition_broadcast(P).rearrange("p a n -> p (a n)")


def columns(w):
    v = w.rearrange("(k p) n -> p k n", p=P)
    return [v[:, :, b * BLK:(b + 1) * BLK] for b in range(w.shape[1] // BLK)]



def transposes(kit, jobs):
    nc = kit.nc
    turned, freed = kit.count("turned"), [kit.count("turned_out_act"), kit.count("turned_out_dve")]
    b0, f0 = turned.n, [f.n for f in freed]
    with nc.Block() as block:
        @block.tensor
        def _(pe):
            for j, (ins, _) in enumerate(jobs):
                if j >= 4:
                    pe.wait_ge(freed[j % 2].sem, f0[j % 2] + (j - 4) // 2 + 1)
                n = ins[0].shape[0]
                for i, a in enumerate(ins):
                    mm = nc.tensor.transpose(kit.bank[j % 4][:, i * n:(i + 1) * n], a, kit.ident[0:n, 0:n])
                turned.up(mm)

        def source(j):
            n, t = len(jobs[j][0]), jobs[j][0][0].shape[0]
            return kit.bank[j % 4][:, 0:n * t].rearrange("p (n t) -> p n t", n=n)

        @block.scalar
        def _(act):
            for j in range(0, len(jobs), 2):
                act.wait_ge(turned.sem, b0 + j + 1)
                freed[0].up(nc.scalar.copy(jobs[j][1], source(j)))

        @block.vector
        def _(dve):
            for j in range(1, len(jobs), 2):
                dve.wait_ge(turned.sem, b0 + j + 1)
                freed[1].up(nc.vector.tensor_copy(jobs[j][1], source(j)))



def transposes_split(kit, jobs):
    nc = kit.nc
    turned, high, freed = kit.count("turned"), kit.count("turned_high"), kit.count("turned_out_dve")
    b0, h0, f0 = turned.n, high.n, freed.n
    with nc.Block() as block:
        @block.tensor
        def _(pe):
            for j, (ins, _, _) in enumerate(jobs):
                if j >= 4:
                    pe.wait_ge(freed.sem, f0 + j - 3)
                n = ins[0].shape[0]
                for i, a in enumerate(ins):
                    mm = nc.tensor.transpose(kit.bank[j % 4][:, i * n:(i + 1) * n], a, kit.ident[0:n, 0:n])
                turned.up(mm)

        def source(j):
            n, t = len(jobs[j][0]), jobs[j][0][0].shape[0]
            return kit.bank[j % 4][:, 0:n * t].rearrange("p (n t) -> p n t", n=n)

        @block.scalar
        def _(act):
            for j in range(len(jobs)):
                act.wait_ge(turned.sem, b0 + j + 1)
                high.up(nc.scalar.copy(jobs[j][1], source(j)))

        @block.vector
        def _(dve):
            for j in range(len(jobs)):
                dve.wait_ge(high.sem, h0 + j + 1)
                freed.up(nc.vector.tensor_tensor(jobs[j][2], source(j), jobs[j][1].bitcast(F32), ALU.subtract))


def transpose_tokens_split(kit, src, hi, lo, kc=KD):
    jobs = []
    for T in range(NT):
        for k in range(0, kc, 4):
            jobs.append(([src[:, T, (k + i) * P:(k + i + 1) * P] for i in range(4)],
                         hi[:, k:k + 4, T * P:(T + 1) * P], lo[:, k:k + 4, T * P:(T + 1) * P]))
    transposes_split(kit, jobs)


def transpose_tokens(kit, src, dstT, kc=KD):
    jobs = []
    for T in range(NT):
        for k in range(0, kc, 4):
            jobs.append(([src[:, T, (k + i) * P:(k + i + 1) * P] for i in range(4)],
                         dstT[:, k:k + 4, T * P:(T + 1) * P]))
    transposes(kit, jobs)


def norm(kit, x, gain, shift, out, load=()):
    nc = kit.nc
    squares, loaded = kit.count("squares_summed"), kit.count("loaded")
    s0, l0 = squares.n, loaded.n
    with kit.sb("ss", [P, 8]) as ss, kit.sb("junk", [P, D]) as junk, nc.Block() as block:
        @block.sync
        def _(sp):
            for dst, src in load:
                kit.load(sp, dst, src)

        @block.scalar
        def _(act):
            for T in range(NT):
                kit.act(nc.scalar.activation(junk[:], x[:, T], ACT.Square, accum_out=ss[:, T:T + 1]))
            squares.up(nc.scalar.activation(ss[:, 4:4 + NT], ss[:, 0:NT], ACT.Sqrt, scale=1.0 / D, bias=kit.eps))

        @block.vector
        def _(dve):
            dve.wait_ge(squares.sem, s0 + 1)
            if load:
                dve.wait_ge(loaded.sem, l0 + 16 * len(load))
            kit.dve(nc.vector.reciprocal(ss[:, 6:6 + NT], ss[:, 4:4 + NT]))
            for T in range(NT):
                ins = nc.vector.scalar_tensor_tensor(out=out[:, T], in0=x[:, T], scalar=ss[:, 6 + T:7 + T],
                                                     in1=gain, op0=ALU.mult, op1=ALU.mult)
                if shift is not None:
                    kit.dve(ins)
                    nc.vector.tensor_tensor(out[:, T], out[:, T], shift, ALU.add)


def norm_modulated(kit, x, g_row, scale, shift, out):
    nc = kit.nc
    loaded = kit.count("loaded")
    l0 = loaded.n
    with kit.sb("gain", [P, D]) as gain:
        with nc.Block() as block:
            @block.sync
            def _(sp):
                kit.load(sp, gain[:], bcast(g_row, D))

            @block.vector
            def _(dve):
                dve.wait_ge(loaded.sem, l0 + 16)
                nc.vector.scalar_tensor_tensor(out=gain[:], in0=scale, scalar=1.0, in1=gain[:],
                                               op0=ALU.add, op1=ALU.mult)
        norm(kit, x, gain[:], shift, out)


def norm_plain(kit, x, g_row, out):
    with kit.sb("gain", [P, D]) as gain:
        norm(kit, x, gain[:], None, out, load=[(gain[:], bcast(g_row, D))])


def linear(kit, xT, nblocks, transposed, evacuate, on_dve=False, kc=KD, extra=None, lhs_of=None, extra_evacuate=None, load=()):
    nc, W = kit.nc, kit.weights
    b0 = W.used
    emptied = kit.count("bank_emptied")
    e0 = emptied.n
    extra_done = kit.count("extra_multiplied")
    x0 = extra_done.n
    with nc.Block() as block:
        @block.sync
        def _(sp):
            for dst, src in load:
                kit.load(sp, dst, src)
            W.issue(sp, b0 + nblocks + SLOTS)
            if load:
                sp.wait_ge(kit.count("loaded").sem, kit.count("loaded").n)

        @block.tensor
        def _(pe):
            for b in range(nblocks):
                w = W.tile(b0 + b, kc)
                W.wait(pe, b0 + b)
                if b >= 4:
                    pe.wait_ge(emptied.sem, e0 + b - 3)
                if lhs_of is not None:
                    xin = lhs_of(pe, b)
                else:
                    xin = xT
                if extra is not None and extra[0] == b:
                    for T in range(NT):
                        for k in range(kc):
                            mm = nc.tensor.matmul(kit.bank[4][:, T * BLK:(T + 1) * BLK], extra[1][:, k, T * P:(T + 1) * P],
                                                  w[:, k, :], start=(k == 0), stop=(k == kc - 1))
                    extra_done.up(mm)
                for half in range(2):
                    for k in range(kc):
                        o = kit.bank[b % 4][:, half * BLK:(half + 1) * BLK]
                        if transposed:
                            mm = nc.tensor.matmul(o, w[:, k, half * P:(half + 1) * P], xin[:, k, :],
                                                  start=(k == 0), stop=(k == kc - 1))
                        else:
                            mm = nc.tensor.matmul(o, xin[:, k, half * P:(half + 1) * P], w[:, k, :],
                                                  start=(k == 0), stop=(k == kc - 1))
                mm.then_inc(W.multiplied, 1)

        def empty(eng):
            if extra is not None:
                eng.wait_ge(extra_done.sem, x0 + 1)
                extra_evacuate(kit.bank[4][:, :].rearrange("p (t n) -> p t n", t=2))
            for b in range(nblocks):
                eng.wait_ge(W.multiplied, b0 + b + 1)
                if on_dve and b:
                    eng.wait_ge(emptied.sem, e0 + b)
                emptied.up(evacuate(b, kit.bank[b % 4][:, :].rearrange("p (t n) -> p t n", t=2)))

        if on_dve:
            @block.vector
            def _(dve):
                empty(dve)
        else:
            @block.scalar
            def _(act):
                empty(act)
    W.used += nblocks


def add_gated(kit, x, tmp, gate):
    nc = kit.nc

    def evacuate(b, bank):
        cols = slice(b * BLK, (b + 1) * BLK)
        g = gate[:, cols].unsqueeze(1).to_broadcast([P, NT, BLK])
        kit.dve(nc.vector.tensor_tensor(tmp[:], bank, g, ALU.mult))
        return nc.vector.tensor_tensor(x[:, :, cols], x[:, :, cols], tmp[:], ALU.add)
    return evacuate


def copy_out(kit, dst):
    def evacuate(b, bank):
        return kit.nc.scalar.copy(dst[:, :, b * BLK:(b + 1) * BLK], bank)
    return evacuate



def load_constants(kit, dram):
    nc = kit.nc
    loaded = kit.count("loaded")
    with nc.Block() as block:
        @block.sync
        def _(sp):
            kit.load(sp, kit.consts[:], dram["consts"])
            kit.load(sp, kit.x[:], dram["x"].rearrange("a (t p) d -> p (a t) d", p=P))
            kit.weights.issue(sp, SLOTS)
            sp.wait_ge(loaded.sem, 32)

        @block.vector
        def _(dve):
            nc.vector.memset(kit.ones[:], 1.0)
            nc.vector.memset(kit.zeros[:], 0.0)
            nc.vector.memset(kit.eps, EPS)
            for s in range(GRING):
                kit.count("row_slots_freed").up(nc.vector.memset(kit.spare[:, s:s + 1], 0.0))
            dve.wait_ge(kit.count("row_slots_freed").sem, GRING)
            kit.count("dots_copied").up(nc.vector.memset(kit.spare[:, 0:1], 0.0))
            kit.count("hidden_ready").up(nc.vector.memset(kit.spare[:, 1:2], 0.0))


@contextmanager
def modulation_space(kit, vectors):
    with kit.sb("ccol", [P, 2, KD]) as ccol, kit.sb("cwide", [P, vectors, KD, P]) as cwide, \
            kit.sb("mod_b_row", [1, N_MOD * D]) as brow:
        yield ccol, cwide, brow


class Parts:

    def __init__(self, sync, tensor, scalar, vector):
        self.sync, self.tensor, self.scalar, self.vector = sync, tensor, scalar, vector


def modulation(kit, dram, layer, mod, mod_ctx):
    with modulation_space(kit, 2) as space, kit.nc.Block() as block:
        parts = modulation_parts(kit, dram, layer, mod, mod_ctx, space)
        block.sync(parts.sync)
        block.vector(parts.vector)
        block.tensor(parts.tensor)
        block.scalar(parts.scalar)


def modulation_parts(kit, dram, layer, mod, mod_ctx, space):
    nc, W = kit.nc, kit.weights
    b0 = W.used
    nb = N_MOD * D // BLK
    ctx_blocks = 2 * D // BLK if mod_ctx is not None else 0
    peeled = 2 * SLOTS if mod_ctx is not None else 0
    rounds = (nb - peeled) // SLOTS
    names = ("c", "c_ctx") if mod_ctx is not None else ("c",)
    loaded, ready = kit.count("loaded"), kit.count("mod_input_ready")
    emptied, ctx_emptied, ctx_done = kit.count("mod_emptied"), kit.count("mod_ctx_emptied"), kit.count("mod_ctx_done")
    l0, r0, e0, c0, d0 = loaded.n, ready.n, emptied.n, ctx_emptied.n, ctx_done.n
    ccol, cwide, brow = space
    def sync(sp):
        W.issue(sp, b0 + max(peeled, SLOTS))
        done = max(peeled, SLOTS)
        n = (nb - done) // SLOTS
        v = dram["mod_w"][layer].rearrange("(k p) n -> p k n", p=P)
        with sp.Fori(0, n) as i:
            for u in range(SLOTS):
                b = b0 + done + u
                sp.wait_ge(W.multiplied, i * SLOTS + (b - SLOTS + 1))
                sp.dma_start(W.tile(b, KD), v[:, :, bass.ds(i * (SLOTS * BLK) + (done + u) * BLK, BLK)]) \
                    .then_inc(W.landed[b % SLOTS], 16)
        W.issued = b0 + nb
        W.issue(sp, b0 + nb + SLOTS)

    def vector(dve):
        dve.wait_ge(ready.sem, r0 + 1)
        for n in range(len(names)):
            ready.up(nc.vector.tensor_copy(cwide[:, n], ccol[:, n].unsqueeze(2).to_broadcast([P, KD, P])))

    def tensor(pe):
        pe.wait_ge(ready.sem, r0 + 1 + len(names))

        def one(u, slot, bias_cols, ctx=False):
            dst = kit.bank[6 + u % 2] if ctx else kit.bank[u]
            n = 1 if ctx else 0
            nc.tensor.matmul(dst[:, 0:BLK], kit.ones[0:1, :], brow[0:1, bias_cols], start=True, stop=False)
            for k in range(KD):
                mm = nc.tensor.matmul(dst[:, 0:BLK], cwide[:, n, k, :], W.tile(slot, KD)[:, k, :],
                                      start=False, stop=(k == KD - 1))
            return mm

        for b in range(peeled):
            W.wait(pe, b0 + b)
            if b < ctx_blocks:
                if b >= 2:
                    pe.wait_ge(ctx_emptied.sem, c0 + b - 1)
                ctx_done.up(one(b, b0 + b, slice(b * BLK, (b + 1) * BLK), ctx=True))
            if b >= SLOTS:
                pe.wait_ge(emptied.sem, e0 + b - SLOTS + 1)
            one(b % SLOTS, b0 + b, slice(b * BLK, (b + 1) * BLK)).then_inc(W.multiplied, 1)
        with pe.Fori(0, rounds) as i:
            for u in range(SLOTS):
                b = b0 + peeled + u
                pe.wait_ge(W.landed[b % SLOTS], i * 16 + 16 * (b // SLOTS + 1))
                if peeled:
                    pe.wait_ge(emptied.sem, i * SLOTS + (e0 + peeled + u - SLOTS + 1))
                else:
                    pe.wait_ge(emptied.sem, i * SLOTS + e0)
                one(u, b, bass.ds(i * (SLOTS * BLK) + (peeled + u) * BLK, BLK)).then_inc(W.multiplied, 1)

    def scalar(act):
        kit.load(act, ccol[:, 0], dram["c"].rearrange("a (k p) -> p (a k)", p=P), slow=True)
        kit.load(act, ccol[:, 1], dram["c_ctx"].rearrange("(k p) -> p k", p=P), slow=True)
        kit.load(act, brow[:], dram["mod_b"][layer:layer + 1, :])
        act.wait_ge(loaded.sem, l0 + 48)
        ready.up(nc.scalar.activation(ccol[:], ccol[:], ACT.Silu))
        for b in range(peeled):
            if b < ctx_blocks:
                act.wait_ge(ctx_done.sem, d0 + b + 1)
                ctx_emptied.up(nc.scalar.copy(mod_ctx[:, b * BLK:(b + 1) * BLK], kit.bank[6 + b % 2][:, 0:BLK]))
            act.wait_ge(W.multiplied, b0 + b + 1)
            nc.scalar.copy(mod[:, b * BLK:(b + 1) * BLK], kit.bank[b % SLOTS][:, 0:BLK]).then_inc(emptied.sem, 1)
        with act.Fori(0, rounds) as i:
            for u in range(SLOTS):
                act.wait_ge(W.multiplied, i * SLOTS + (b0 + peeled + u + 1))
                nc.scalar.copy(mod[:, bass.ds(i * (SLOTS * BLK) + (peeled + u) * BLK, BLK)],
                               kit.bank[u][:, 0:BLK]).then_inc(emptied.sem, 1)
    W.used += nb
    emptied.n = e0 + nb
    return Parts(sync, tensor, scalar, vector)



def attend(kit, units, PT, cat_bank, probs_of, values_of):
    nc = kit.nc
    turned, copied, mixed = kit.count("probs_turned"), kit.count("probs_copied"), kit.count("values_mixed")
    t0, c0, m0 = turned.n, copied.n, mixed.n
    jobs = []
    for u, chunks in enumerate(units):
        for a in range(0, len(chunks), 4):
            jobs.append((u, a, chunks[a:a + 4], a + 4 >= len(chunks)))

    def pe_side(pe, before_unit):
        def turn(j):
            u, a, cs, last = jobs[j]
            if a == 0:
                before_unit(pe, u)
            if j >= 4:
                pe.wait_ge(copied.sem, c0 + j - 3)
            for i, c in enumerate(cs):
                mm = nc.tensor.transpose(kit.bank[j % 4][:, i * P:(i + 1) * P], probs_of(u, c), kit.ident)
            turned.up(mm)

        def mix(j):
            u, a, cs, last = jobs[j]
            pe.wait_ge(copied.sem, c0 + j + 1)
            for i, c in enumerate(cs):
                mm = nc.tensor.matmul(cat_bank(u), PT[:, j % 4, i, :], values_of(u, c),
                                      start=(a == 0 and i == 0), stop=(last and i == len(cs) - 1))
            mixed.up(mm)

        for j in range(len(jobs)):
            turn(j)
            if j >= 2:
                mix(j - 2)
        for j in range(max(0, len(jobs) - 2), len(jobs)):
            mix(j)

    def act_side(act):
        for j, (u, a, cs, last) in enumerate(jobs):
            act.wait_ge(turned.sem, t0 + j + 1)
            if j >= 4:
                act.wait_ge(mixed.sem, m0 + j - 3)
            copied.up(nc.scalar.copy(PT[:, j % 4, 0:len(cs), :], kit.bank[j % 4][:, 0:len(cs) * P].rearrange(
                "p (n t) -> p n t", n=len(cs))))

    return pe_side, act_side, m0 + len(jobs)


def window_attention(kit, dram, proj, kvc, cat):
    nc = kit.nc
    nqk = (Q_W + KV_W) // HD
    loaded = kit.count("loaded")
    l0 = loaded.n
    with kit.sb("qT", [P, GQA, SEQ]) as qT, kit.sb("kT", [P, 2 * SEQ]) as kT, kit.sb("sink", [P, HEADS]) as sink:
        with kit.sb("rot", [P, NT, nqk * HD]) as rot, kit.sb("rot2", [P, NT, nqk * HD]) as rot2, \
                kit.sb("turned", [P, NT, nqk * HD]) as turned:
            with nc.Block() as block:
                @block.sync
                def _(sp):
                    kit.load(sp, sink[:], bcast(dram["attn_sink"], HEADS))

                @block.vector
                def _(dve):
                    for T in range(NT):
                        x = proj[:, T, 0:nqk * HD]
                        cos = kit.cos[:, T].unsqueeze(1).to_broadcast([P, nqk, HD])
                        nc.vector.tensor_tensor(rot[:, T].rearrange("p (h d) -> p h d", d=HD),
                                                x.rearrange("p (h d) -> p h d", d=HD), cos, ALU.mult)
                        xs = x.rearrange("p (h f s c) -> p h f s c", f=2, s=2, c=16)
                        o = rot2[:, T].rearrange("p (h f s c) -> p h f s c", f=2, s=2, c=16)
                        sn = kit.sin[:, T].rearrange("p (f s c) -> p f s c", f=2, s=2)
                        for s in range(2):
                            ins = nc.vector.tensor_tensor(o[:, :, :, s], xs[:, :, :, 1 - s],
                                                          sn[:, :, s].unsqueeze(1).to_broadcast([P, nqk, 2, 16]),
                                                          ALU.mult)
                        kit.dve(ins)
                        by_chunk = lambda a: a[:, T, 0:Q_W].rearrange("p (v c d) -> p c v d", v=2, d=HD)
                        nc.vector.tensor_tensor(turned[:, T, 0:Q_W].rearrange("p (c v d) -> p c v d", v=2, d=HD),
                                                by_chunk(rot), by_chunk(rot2), ALU.add)
                        nc.vector.tensor_tensor(turned[:, T, Q_W:], rot[:, T, Q_W:], rot2[:, T, Q_W:], ALU.add)
                    dve.wait_ge(loaded.sem, l0 + 16)
            jobs = []
            for T in range(NT):
                jobs.append(([turned[:, T, c * P:(c + 1) * P] for c in range(GQA)], qT[:, :, T * P:(T + 1) * P]))
            jobs.append(([turned[:, T, Q_W:Q_W + KV_W] for T in range(NT)] + [kvc[:, T, 0:KV_W] for T in range(NT)],
                         kT[:].rearrange("p (n t) -> p n t", t=P)))
            transposes(kit, jobs)

        units = [(T, h) for T in range(NT) for h in range(HEADS)]
        nu = len(units)
        with kit.sb("probs", [P, nu, 512]) as probs, kit.sb("PT", [P, 4, 4, P]) as PT, \
                kit.sb("rows", [P, 8, nu]) as rows:
            scored, masked = kit.count("scored"), kit.count("score_masked")
            s0, k0 = scored.n, masked.n
            negmax, exped, normed = kit.count("negmax_ready"), kit.count("exped"), kit.count("denominators")
            n0, x0, d0 = negmax.n, exped.n, normed.n
            cat_bank = lambda u: kit.bank[4 + u // HEADS][:, (u % HEADS) * HD:(u % HEADS + 1) * HD]
            values = lambda u, c: (proj[:, c, Q_W + KV_W:][:, (u % HEADS) // GQA * HD:((u % HEADS) // GQA + 1) * HD]
                                   if c < NT else
                                   kvc[:, c - NT, KV_W + (u % HEADS) // GQA * HD:KV_W + ((u % HEADS) // GQA + 1) * HD])
            pe_side, act_side, m_end = attend(kit, [range(4)] * nu, PT, cat_bank,
                                              lambda u, c: probs[:, u, c * P:(c + 1) * P], values)
            mixed = kit.count("values_mixed")
            with nc.Block() as block:
                @block.tensor
                def _(pe):
                    for u, (T, h) in enumerate(units):
                        if u >= 4:
                            pe.wait_ge(masked.sem, k0 + u - 3)
                        v, c = h // GQA, h % GQA
                        scored.up(nc.tensor.matmul(kit.bank[u % 4][:, :], qT[v * HD:(v + 1) * HD, c, T * P:(T + 1) * P],
                                                   kT[v * HD:(v + 1) * HD, :], start=True, stop=True))
                    pe.wait_ge(masked.sem, k0 + nu)
                    pe_side(pe, lambda pe, u: pe.wait_ge(exped.sem, x0 + u + 1))

                @block.vector
                def _(dve):
                    for u, (T, h) in enumerate(units):
                        dve.wait_ge(scored.sem, s0 + u + 1)
                        masked.up(nc.vector.tensor_tensor_reduce(
                            out=probs[:, u], in0=kit.bank[u % 4][:, :], in1=kit.window[:, T], scale=SCALE,
                            scalar=NEG, op0=ALU.add, op1=ALU.max, accum_out=rows[:, 0, u:u + 1]))
                    dve.wait_ge(masked.sem, k0 + nu)
                    sk = sink[:].unsqueeze(1).to_broadcast([P, NT, HEADS])
                    r = lambda i: rows[:, i].rearrange("p (t h) -> p t h", t=NT)
                    kit.dve(nc.vector.tensor_tensor(r(1), r(0), sk, ALU.max))
                    nc.vector.tensor_tensor(r(3), sk, r(1), ALU.subtract).then_inc(negmax.sem, 1)
                    nc.vector.tensor_scalar(rows[:, 2], rows[:, 1], -1.0, None, ALU.mult).then_inc(negmax.sem, 1)
                    negmax.n += 2
                    dve.wait_ge(exped.sem, x0 + nu + 1)
                    kit.dve(nc.vector.tensor_tensor(rows[:, 6], rows[:, 5], rows[:, 4], ALU.add))
                    kit.dve(nc.vector.reciprocal(rows[:, 7], rows[:, 6]))
                    dve.wait_ge(mixed.sem, m_end)
                    for T in range(NT):
                        nc.vector.tensor_tensor(
                            cat[:, T, 0:Q_W].rearrange("p (h d) -> p h d", d=HD),
                            kit.bank[4 + T][:, :].rearrange("p (h d) -> p h d", d=HD),
                            rows[:, 7, T * HEADS:(T + 1) * HEADS].unsqueeze(2).to_broadcast([P, HEADS, HD]), ALU.mult)

                @block.scalar
                def _(act):
                    act.wait_ge(negmax.sem, n0 + 2)
                    for u in range(nu):
                        exped.up(nc.scalar.activation(probs[:, u], probs[:, u], ACT.Exp, bias=rows[:, 2, u:u + 1],
                                                      accum_out=rows[:, 4, u:u + 1]))
                    exped.up(nc.scalar.activation(rows[:, 5], rows[:, 3], ACT.Exp))
                    act_side(act)


def gmlp(kit, dram, proj, cat):
    nc = kit.nc
    loaded = kit.count("loaded")
    l0 = loaded.n
    u0 = Q_W + 2 * KV_W
    with kit.sb("ws", [P, GROUPS, P]) as ws, kit.sb("wsT", [P, GROUPS, P]) as wsT, kit.sb("bs", [P, GROUPS]) as bs, \
            kit.sb("stat", [P, 4, NT * GROUPS]) as stat, kit.sb("sq", [P, NT, A_W]) as sq:
        gelued = kit.count("gelued")
        g0 = gelued.n
        with nc.Block() as block:
            @block.sync
            def _(sp):
                kit.load(sp, ws[:], dram["gmlp_w_s"].rearrange("e g p q -> p (e g) q"))
                kit.load(sp, bs[:], dram["gmlp_b_s"].rearrange("e g p -> p (e g)"), slow=True)
                sp.wait_ge(loaded.sem, l0 + 32)

            @block.scalar
            def _(act):
                for T in range(NT):
                    gelued.up(nc.scalar.activation(proj[:, T, u0:u0 + 2 * A_W], proj[:, T, u0:u0 + 2 * A_W],
                                                   ACT.Gelu_apprx_tanh))
                kit.roots(act, [(stat[:, 3, T * GROUPS:(T + 1) * GROUPS], stat[:, 2, T * GROUPS:(T + 1) * GROUPS])
                                for T in range(NT)])

            @block.vector
            def _(dve):
                for T in range(NT):
                    dve.wait_ge(gelued.sem, g0 + T + 1)
                    v = proj[:, T, u0 + A_W:u0 + 2 * A_W].rearrange("p (g d) -> p g d", d=HD)
                    s = sq[:, T].rearrange("p (g d) -> p g d", d=HD)
                    st = lambda i: stat[:, i, T * GROUPS:(T + 1) * GROUPS]
                    wide = lambda i: st(i).unsqueeze(2).to_broadcast([P, GROUPS, HD])
                    kit.dve(nc.vector.tensor_reduce(st(0), v, AX, ALU.add))
                    kit.dve(nc.vector.tensor_scalar(st(0), st(0), 1.0 / HD, None, ALU.mult))
                    kit.dve(nc.vector.tensor_tensor(v, v, wide(0), ALU.subtract))
                    kit.dve(nc.vector.tensor_tensor(s, v, v, ALU.mult))
                    kit.dve(nc.vector.tensor_reduce(st(1), s, AX, ALU.add))
                    kit.rsqrt(dve, nc.vector.tensor_scalar(st(2), st(1), 1.0 / HD, EPS, ALU.mult, ALU.add), st(3), st(3))
                    kit.dve(nc.vector.tensor_tensor(v, v, wide(3), ALU.mult))
        transposes(kit, [([ws[:, g + i, :] for i in range(4)], wsT[:, g:g + 4, :]) for g in (0, 4)])
        spread = kit.count("tokens_mixed")
        s0 = spread.n
        with nc.Block() as block:
            @block.tensor
            def _(pe):
                for g in range(GROUPS):
                    spread.up(nc.tensor.matmul(kit.bank[g // 4][:, g % 4 * P:(g % 4 + 1) * P], wsT[:, g, :],
                                               proj[:, :, u0 + A_W + g * HD:u0 + A_W + (g + 1) * HD],
                                               start=True, stop=True))

            @block.vector
            def _(dve):
                dve.wait_ge(spread.sem, s0 + GROUPS)
                for g in range(GROUPS):
                    nc.vector.scalar_tensor_tensor(
                        out=cat[:, :, Q_W + g * HD:Q_W + (g + 1) * HD],
                        in0=kit.bank[g // 4][:, g % 4 * P:(g % 4 + 1) * P].rearrange("p (t d) -> p t d", t=NT),
                        scalar=bs[:, g:g + 1], in1=proj[:, :, u0 + g * HD:u0 + (g + 1) * HD],
                        op0=ALU.add, op1=ALU.mult)


def mixer(kit, dram, mod, mod_ctx):
    x, h, hT = kit.x, kit.h, kit.hT
    nc = kit.nc
    with kit.sb("cat", [P, NT, D]) as cat:
        with kit.sb("proj", [P, NT, Q_W + 2 * KV_W + 2 * A_W]) as proj, kit.sb("kvc", [P, NT, 2 * KV_W]) as kvc:
            with kit.sb("hcT", [P, KD, SEQ]) as hcT:
                with kit.sb("xc", [P, NT, D]) as xc:
                    loaded = kit.count("loaded")
                    l0 = loaded.n
                    with nc.Block() as block:
                        @block.sync
                        def _(sp):
                            kit.load(sp, xc[:], dram["ctx"].rearrange("a (t p) d -> p (a t) d", p=P))
                            sp.wait_ge(loaded.sem, l0 + 16)
                    norm_modulated(kit, xc, dram["norm1_g"][0:1, :], mod_ctx[:, D:2 * D], mod_ctx[:, 0:D], h)
                transpose_tokens(kit, h, hcT)
                norm_modulated(kit, x, dram["norm1_g"][0:1, :], mod[:, D:2 * D], mod[:, 0:D], h)
                transpose_tokens(kit, h, hT)
                linear(kit, hT, 7, False, copy_out(kit, proj), extra=(Q_W // BLK, hcT),
                       extra_evacuate=lambda bank: nc.scalar.copy(kvc[:], bank))
            window_attention(kit, dram, proj, kvc, cat)
            gmlp(kit, dram, proj, cat)
        transpose_tokens(kit, cat, hT)
        with kit.sb("tmp", [P, NT, BLK]) as tmp:
            linear(kit, hT, 4, False, add_gated(kit, x, tmp, mod[:, 2 * D:3 * D]), on_dve=True)


def pooling(kit, dram, mod):
    nc, W = kit.nc, kit.weights
    x, h = kit.x, kit.h
    norm_modulated(kit, x, dram["norm1_g"][1:2, :], mod[:, D:2 * D], mod[:, 0:D], h)
    b0 = W.used
    loaded, pooled, copied, done = kit.count("loaded"), kit.count("pooled"), kit.count("pooled_copied"), kit.count("pool_projected")
    l0, p0, c0, d0 = loaded.n, pooled.n, copied.n, done.n
    G = len(POOL_WINDOWS)
    with kit.sb("bands", [P, G, NT, SEQ]) as bands, kit.sb("pooledT", [P, KD, SEQ]) as pT, \
            kit.sb("gs", [P, D]) as gs, kit.sb("tmp", [P, D]) as tmp, nc.Block() as block:
        @block.sync
        def _(sp):
            kit.load(sp, bands[:], dram["bands"].rearrange("g (t p) n -> p g t n", p=P))
            kit.load(sp, gs[:], bcast(dram["pool_scale"], D))
            W.issue(sp, b0 + 1 + SLOTS)

        @block.tensor
        def _(pe):
            pe.wait_ge(loaded.sem, l0 + 32)
            for k in range(KD):
                for t in range(NT):
                    mm = nc.tensor.matmul(kit.bank[k // 2][:, k % 2 * SEQ:(k % 2 + 1) * SEQ], h[:, t, k * P:(k + 1) * P],
                                          bands[:, k // 2, t, :], start=(t == 0), stop=(t == NT - 1))
                pooled.up(mm)
            W.wait(pe, b0)
            w = W.tile(b0, KD)
            for T in range(NT):
                for g in range(G):
                    pe.wait_ge(copied.sem, c0 + g + 1)
                    for cc in range(2):
                        mm = nc.tensor.matmul(kit.bank[4 + 2 * T + g // 2][:, g % 2 * BLK:(g % 2 + 1) * BLK],
                                              pT[:, 2 * g + cc, T * P:(T + 1) * P], w[:, 2 * g + cc, :],
                                              start=(cc == 0), stop=(cc == 1))
                if T == NT - 1:
                    mm.then_inc(W.multiplied, 1)
                else:
                    done.up(mm)

        @block.scalar
        def _(act):
            for g in range(G):
                act.wait_ge(pooled.sem, p0 + 2 * g + 2)
                copied.up(nc.scalar.copy(pT[:, 2 * g:2 * g + 2, :], kit.bank[g][:, :].rearrange("p (a n) -> p a n", a=2)))

        @block.vector
        def _(dve):
            dve.wait_ge(loaded.sem, l0 + 32)
            kit.dve(nc.vector.tensor_tensor(gs[:], gs[:], mod[:, 2 * D:3 * D], ALU.mult))
            for T in range(NT):
                if T == NT - 1:
                    dve.wait_ge(W.multiplied, b0 + 1)
                else:
                    dve.wait_ge(done.sem, d0 + 1)
                for i in range(2):
                    kit.dve(nc.vector.tensor_tensor(tmp[:, i * 512:(i + 1) * 512], kit.bank[4 + 2 * T + i][:, :],
                                                    gs[:, i * 512:(i + 1) * 512], ALU.mult))
                kit.dve(nc.vector.tensor_tensor(x[:, T], x[:, T], tmp[:], ALU.add))
    W.used += 1



def peer(kit, dram, layer, mod, next_modulation):
    nc = kit.nc
    x, h, hT = kit.x, kit.h, kit.hT
    norm_modulated(kit, x, dram["norm2_g"][layer:layer + 1, :], mod[:, 4 * D:5 * D], mod[:, 3 * D:4 * D], h)
    transpose_tokens(kit, h, hT)
    with kit.sb("scores", [P, NT, 2 * PH, NKEYS]) as scores:
        with kit.sb("peer_q", [P, PH, 2, SEQ]) as qT, kit.sb("keys", [P, 2, P]) as keys, kit.sb("keysT", [P, 2, P]) as keysT:
            linear(kit, hT, 8, True, lambda b, bank: nc.scalar.copy(qT[:, b], bank),
                   load=[(keys[:], dram["peer_sub_keys"][layer].rearrange("s n k -> n s k"))])
            transposes(kit, [([keys[:, s, :] for s in range(2)], keysT[:])])
            score_keys(kit, qT, keysT, scores)
        experts(kit, dram, layer, scores, mod, next_modulation)


def score_keys(kit, qT, keysT, sc):
    nc = kit.nc
    nu = 2 * PH
    scored, copied = kit.count("keys_scored"), kit.count("key_scores_copied")
    s0, c0 = scored.n, copied.n
    with nc.Block() as block:
        @block.tensor
        def _(pe):
            for T in range(NT):
                for q in range(nu // 4):
                    b = T * (nu // 4) + q
                    if b >= 4:
                        pe.wait_ge(copied.sem, c0 + b - 3)
                    for i in range(4):
                        hh, s = (4 * q + i) // 2, i % 2
                        mm = nc.tensor.matmul(kit.bank[b % 4][:, i * P:(i + 1) * P], qT[:, hh, s, T * P:(T + 1) * P],
                                              keysT[:, s, :], start=True, stop=True)
                    scored.up(mm)

        @block.scalar
        def _(act):
            for T in range(NT):
                for q in range(nu // 4):
                    b = T * (nu // 4) + q
                    act.wait_ge(scored.sem, s0 + b + 1)
                    copied.up(nc.scalar.copy(sc[:, T, 4 * q:4 * q + 4, :], kit.bank[b % 4][:, :].rearrange(
                        "p (a n) -> p a n", a=4)))


def top16s(kit, dve, jobs):
    nc = kit.nc
    step = kit.step["dve"]
    last = [n for _, _, _, _, n in jobs]
    for stage in range(5):
        for j, (values, indices, data, spare, _) in enumerate(jobs):
            if last[j]:
                dve.wait_ge(step.sem, last[j])
            if stage == 0:
                ins = nc.vector.max(values[:, 0:8], data)
            elif stage == 1:
                ins = nc.vector.max_index(indices[:, 0:8], values[:, 0:8], data)
            elif stage == 2:
                ins = nc.vector.match_replace(spare, values[:, 0:8], data, -3e38)
            elif stage == 3:
                ins = nc.vector.max(values[:, 8:16], spare)
            else:
                ins = nc.vector.max_index(indices[:, 8:16], values[:, 8:16], spare)
            last[j] = step.up(ins)


def choose(kit, dve, layer, T, sc, small, wide, idx, gate, shifted):
    nc = kit.nc
    nu = 2 * PH
    step = kit.step["dve"]
    top, itop, ftop, best, pos, part, fpart, row, fidx = small
    cand = wide[:, 0:4 * 256].rearrange("p (j n) -> p j n", j=4)
    spare = wide[:, 4 * 256:8 * 256].rearrange("p (j n) -> p j n", j=4)
    for q in range(0, nu, 4):
        top16s(kit, dve, [(top[:, u // 2, u % 2], itop[:, u // 2, u % 2], sc[:, T, u], spare[:, u - q, 0:NKEYS], 0)
                          for u in range(q, q + 4)])
        dve.wait_ge(step.sem, step.n)
    for q in range(0, PH, 4):
        made = [step.up(nc.vector.tensor_tensor(
            cand[:, hh - q].rearrange("p (a b) -> p a b", a=16), top[:, hh, 0].unsqueeze(2).to_broadcast([P, 16, 16]),
            top[:, hh, 1].unsqueeze(1).to_broadcast([P, 16, 16]), ALU.add)) for hh in range(q, q + 4)]
        top16s(kit, dve, [(best[:, hh], pos[:, hh], cand[:, hh - q], spare[:, hh - q], made[hh - q])
                          for hh in range(q, q + 4)])
        dve.wait_ge(step.sem, step.n)
    g = gate[:, T].rearrange("p (h k) -> p h k", h=PH)
    shifted.up(nc.vector.tensor_tensor(g, best[:], best[:, :, 0:1].to_broadcast([P, PH, TOPK]), ALU.subtract))
    flat = pos[:].rearrange("p h k -> p (h k)")
    nc.vector.tensor_copy(ftop[:], itop[:])
    nc.vector.tensor_scalar(part[:, 0], flat, 4, None, ALU.logical_shift_right)
    kit.dve(nc.vector.tensor_scalar(part[:, 1], flat, 15, None, ALU.bitwise_and))
    kit.dve(nc.vector.tensor_copy(fpart[:], part[:]))
    for s in range(2):
        sel = wide.rearrange("p (k i) -> p k i", i=16)
        kit.dve(nc.vector.tensor_tensor(sel, fpart[:, s].unsqueeze(2).to_broadcast([P, PICKS, 16]),
                                        kit.iota16.unsqueeze(1).to_broadcast([P, PICKS, 16]), ALU.is_equal))
        sv = sel.rearrange("p (h k) i -> p h k i", h=PH)
        kit.dve(nc.vector.tensor_tensor(sv, sv, ftop[:, :, s].unsqueeze(2).to_broadcast([P, PH, TOPK, 16]), ALU.mult))
        kit.dve(nc.vector.tensor_reduce(row[:, s], sel, AX, ALU.add))
    kit.dve(nc.vector.scalar_tensor_tensor(out=fidx[:], in0=row[:, 0], scalar=float(NKEYS), in1=row[:, 1],
                                           op0=ALU.mult, op1=ALU.add))
    if layer:
        kit.dve(nc.vector.tensor_scalar(fidx[:], fidx[:], float(layer * NKEYS * NKEYS), None, ALU.add))
    return nc.vector.tensor_copy(idx[:, T], fidx[:])


def experts(kit, dram, layer, sc, mod, next_modulation):
    nc = kit.nc
    x, h = kit.x, kit.h
    UN = 2 * GRING
    rounds = PICKS // UN
    row_landed = [kit.count(f"row_landed{i}") for i in range(GRING)]
    claimed = kit.count("row_slots_claimed")
    free, idx_ready, dots, gelued = (kit.count("row_slots_freed"), kit.count("slot_indices"), kit.count("dots_copied"),
                                     kit.count("gelu_done"))
    chosen, shifted, exped = kit.count("experts_chosen"), kit.count("best_shifted"), kit.count("best_exped")
    weighted, diag_made = kit.count("row_weights_ready"), kit.count("diagonal_made")
    phases = [(name, T) for T in range(NT) for name in ("peer_down", "peer_up")]
    tables = {n: dram[n].rearrange("l e d -> (l e) d") for n in ("peer_down", "peer_up")}
    u0, i0, d0, g0, c0 = free.n - GRING, idx_ready.n, dots.n, gelued.n, chosen.n
    h0, x0, w0, m0 = shifted.n, exped.n, weighted.n, diag_made.n
    L0 = row_landed[0].n
    with kit.sb("rows", [P, GRING, D]) as ring, kit.sb("slot_idx", [P, 2, GRING], U32) as slot_idx, \
            kit.sb("dot16", [P, UN]) as dot16, kit.sb("dot", [P, PICKS]) as dot, kit.sb("acc", [P, D]) as acc, \
            kit.sb("idx", [P, NT, PICKS], U32) as idx, kit.sb("gate", [P, NT, PICKS]) as gate, \
            kit.sb("top", [P, PH, 2, TOPK]) as top, kit.sb("itop", [P, PH, 2, TOPK], U32) as itop, \
            kit.sb("ftop", [P, PH, 2, TOPK]) as ftop, kit.sb("best", [P, PH, TOPK]) as best, \
            kit.sb("pos", [P, PH, TOPK], U32) as pos, kit.sb("part", [P, 2, PICKS], U32) as part, \
            kit.sb("fpart", [P, 2, PICKS]) as fpart, kit.sb("row", [P, 2, PICKS]) as row, \
            kit.sb("fidx", [P, PICKS]) as fidx, kit.sb("den", [P, 2, PH]) as den, \
            kit.sb("diag", [P, 4, P]) as diag, kit.sb("g2", [P, D]) as g2, \
            (modulation_space(kit, 1) if next_modulation else kit.sb("none", [1, 8])) as space, nc.Block() as block:
        small = (top, itop, ftop, best, pos, part, fpart, row, fidx)
        wide = kit.hT[:].rearrange("p k n -> p (k n)")
        also = modulation_parts(kit, dram, layer + 1, mod, None, space) if next_modulation else None

        if also:
            @block.sync
            def _(sp):
                also.sync(sp)

        @block.gpsimd
        def _(pool):
            for ph, (name, T) in enumerate(phases):
                if name == "peer_down":
                    pool.wait_ge(chosen.sem, c0 + T + 1)
                p0 = ph * PICKS
                with pool.Fori(0, rounds) as i:
                    for half in range(2):
                        j = p0 + half * GRING
                        pool.wait_ge(free.sem, i * UN + (u0 + j + 1))
                        nc.gpsimd.tensor_copy(slot_idx[:, half], idx[:, T, bass.ds(i * UN + half * GRING, GRING)]) \
                            .then_inc(idx_ready.sem, 1)
                        pool.wait_ge(idx_ready.sem, i * 2 + (i0 + ph * 2 * rounds + half + 1))
                        for s in range(GRING):
                            pool.wait_ge(free.sem, i * UN + (u0 + j + s + 1))
                            pool.sem_inc(claimed.sem, 1)
                            nc.gpsimd.indirect_dma_start(
                                ring[:, s], None, tables[name],
                                bass.IndirectOffsetOnAxis(ap=slot_idx[:, half, s:s + 1], axis=0)) \
                                .then_inc(row_landed[s].sem, 16)

        def wait_row(eng, i, ph, n):
            eng.wait_ge(row_landed[n % GRING].sem, i * 32 + (L0 + 16 * (ph * PICKS // GRING + n // GRING + 1)))

        @block.tensor
        def _(pe):
            if also:
                also.tensor(pe)
            for half in range(2):
                nc.tensor.matmul(kit.bank[6 + half][:, :], kit.zeros[0:1, 0:P], kit.zeros[0:1, :], start=True, stop=False,
                                 skip_group_check=True)
            with pe.Fori(0, PE_ROWS // UN) as i:
                for n in range(UN):
                    wait_row(pe, i, 1, n)
                    pe.wait_ge(diag_made.sem, i * UN + (m0 + n + 1))
                    for half in range(2):
                        mm = nc.tensor.matmul(kit.bank[6 + half][:, :], diag[:, n % 4], ring[:, n % GRING, half * 512:(half + 1) * 512],
                                              start=False, stop=False, skip_group_check=True)
                    mm.then_inc(free.sem, 1)

        @block.scalar
        def _(act):
            g2_kept = nc.scalar.copy(g2[:], mod[:, 5 * D:6 * D])
            if also:
                kit.act(g2_kept)
                also.scalar(act)
            for T in range(NT):
                act.wait_ge(shifted.sem, h0 + T + 1)
                exped.up(nc.scalar.activation(gate[:, T], gate[:, T], ACT.Exp))
                act.wait_ge(dots.sem, d0 + (T + 1) * rounds)
                gelued.up(nc.scalar.activation(dot[:], dot[:], ACT.Gelu_apprx_tanh))
                if T == 0:
                    act.wait_ge(weighted.sem, w0 + 1)
                    with act.Fori(0, PE_ROWS // UN) as i:
                        for n in range(UN):
                            act.wait_ge(free.sem, i * UN + (u0 + GRING + PICKS + n - 3))
                            nc.scalar.activation(diag[:, n % 4], kit.ident, ACT.Copy,
                                                 scale=gate[:, 0, bass.ds(i * UN + n, 1)]).then_inc(diag_made.sem, 1)

        @block.vector
        def _(dve):
            def down(ph, T):
                with dve.Fori(0, rounds) as i:
                    for n in range(UN):
                        s = n % GRING
                        wait_row(dve, i, ph, n)
                        if n == 0:
                            dve.wait_ge(dots.sem, i + (d0 + T * rounds))
                        nc.vector.tensor_tensor_reduce(out=ring[:, s], in0=ring[:, s], in1=h[:, T], scale=1.0, scalar=0.0,
                                                       op0=ALU.mult, op1=ALU.add, accum_out=dot16[:, n:n + 1]) \
                            .then_inc(free.sem, 1)
                    dve.wait_ge(free.sem, i * UN + (u0 + GRING + ph * PICKS + UN))
                    nc.vector.tensor_copy(dot[:, bass.ds(i * UN, UN)], dot16[:]).then_inc(dots.sem, 1)

            def weigh(T):
                dve.wait_ge(exped.sem, x0 + T + 1)
                g = gate[:, T].rearrange("p (h k) -> p h k", h=PH)
                kit.dve(nc.vector.tensor_reduce(den[:, 0], g, AX, ALU.add))
                kit.dve(nc.vector.reciprocal(den[:, 1], den[:, 0]))
                kit.dve(nc.vector.tensor_tensor(g, g, den[:, 1].unsqueeze(2).to_broadcast([P, PH, TOPK]), ALU.mult))
                dve.wait_ge(gelued.sem, g0 + T + 1)
                kit.dve(nc.vector.tensor_tensor(gate[:, T], gate[:, T], dot[:], ALU.mult))
                weighted.up(nc.vector.memset(kit.spare[:, 0:1], 0.0))

            def up(ph, T, first):
                with dve.Fori(0, rounds - first // UN) as i:
                    for n in range(UN):
                        g = ph * PICKS + first + n
                        wait_row(dve, i, ph, first + n)
                        dve.wait_ge(free.sem, i * UN + (u0 + GRING + g))
                        nc.vector.scalar_tensor_tensor(out=acc[:], in0=ring[:, n % GRING],
                                                       scalar=gate[:, T, bass.ds(i * UN + first + n, 1)], in1=acc[:],
                                                       op0=ALU.mult, op1=ALU.add).then_inc(free.sem, 1)
                dve.wait_ge(free.sem, u0 + GRING + (ph + 1) * PICKS)
                kit.dve(nc.vector.tensor_tensor(acc[:], acc[:], g2[:], ALU.mult))
                kit.dve(nc.vector.tensor_tensor(x[:, T], x[:, T], acc[:], ALU.add))

            if also:
                also.vector(dve)
            chosen.up(choose(kit, dve, layer, 0, sc, small, wide, idx, gate, shifted))
            down(0, 0)
            weigh(0)
            chosen.up(choose(kit, dve, layer, 1, sc, small, wide, idx, gate, shifted))
            dve.wait_ge(free.sem, u0 + GRING + PICKS + PE_ROWS)
            nc.vector.tensor_copy(acc[:, 0:512], kit.bank[6][:, :])
            kit.dve(nc.vector.tensor_copy(acc[:, 512:D], kit.bank[7][:, :]))
            up(1, 0, PE_ROWS)
            down(2, 1)
            weigh(1)
            kit.dve(nc.vector.memset(acc[:], 0.0))
            up(3, 1, 0)
    free.n += len(phases) * PICKS
    idx_ready.n += len(phases) * 2 * rounds
    dots.n += NT * rounds
    diag_made.n += PE_ROWS
    for c in row_landed:
        c.n += len(phases) * PICKS // GRING * 16



def ffn_blocks(dram, layer, which):
    g = columns(dram["ffn_w_gate_2"][layer, which])
    u = columns(dram["ffn_w_up_2"][layer, which])
    d = dram["ffn_w_down_2"][layer, which].rearrange("(f s p) n -> f p s n", s=2, p=P)
    out = [g[0], u[0]]
    for f in range(1, FF_BLOCKS):
        out += [g[f], u[f], d[f - 1]]
    return out + [d[FF_BLOCKS - 1]]


def swiglu(kit, dram, layer, which):
    nc, W = kit.nc, kit.weights
    x, h = kit.x, kit.h
    norm_plain(kit, x, dram["ffn_norm_2"][layer, which:which + 1, :], h)
    b0 = W.used
    nb = 3 * FF_BLOCKS
    loops = (FF_BLOCKS - 1) // 2
    silued, ready = kit.count("gate_silued"), kit.count("hidden_ready")
    high_made, split = kit.count("block_high_made"), kit.count("block_split")
    s0, r0, h0, p0 = silued.n, ready.n, high_made.n, split.n
    gate_w = dram["ffn_w_gate_2"][layer, which].rearrange("(k p) n -> p k n", p=P)
    up_w = dram["ffn_w_up_2"][layer, which].rearrange("(k p) n -> p k n", p=P)
    down_w = dram["ffn_w_down_2"][layer, which]

    def up_block(f, v):
        return v if f == 0 else 3 * f - 1 + v

    def wait(eng, sem, value, reg, per_round):
        eng.wait_ge(sem, value if reg is None else reg * per_round + value)

    with kit.sb("hT_high", [P, KD, SEQ], F32R) as hT, kit.sb("hT_low", [P, KD, SEQ], F32R) as hT_low, \
            kit.sb("high", [P, SPLIT_SLOTS, 2048], F32R) as high, kit.sb("low", [P, SPLIT_SLOTS, 2048], F32R) as low, \
            kit.sb("act_gate", [P, 2, 2 * SEQ]) as ag, kit.sb("hidden", [P, 2, 2, SEQ], F32R) as hid, \
            kit.sb("hidden_low", [P, 2, 2, SEQ], F32R) as hid_low:
        transpose_tokens_split(kit, h, hT, hT_low)

        def parts(b):
            return W.ring[:, (b0 + b) % SLOTS, :], high[:, b % SPLIT_SLOTS, :], low[:, b % SPLIT_SLOTS, :]

        def shaped(b, k):
            return [a.rearrange("p (k n) -> p k n", k=k) for a in parts(b)[1:]]

        with nc.Block() as block:
            @block.sync
            def _(sp):
                W.issue(sp, b0 + 2 + 6)
                with sp.Fori(0, loops - 1) as i:
                    for v in range(6):
                        b, f = b0 + 8 + v, 3 + v // 3
                        sp.wait_ge(W.multiplied, i * 6 + (b - SLOTS + 1))
                        if v % 3 < 2:
                            src = (gate_w, up_w)[v % 3][:, :, bass.ds(i * (2 * BLK) + f * BLK, BLK)]
                        else:
                            src = down_w[bass.ds(i * (2 * BLK) + (f - 1) * BLK, BLK), :].rearrange("(s p) n -> p s n", p=P)
                        sp.dma_start(W.tile(b, KD if v % 3 < 2 else 2), src).then_inc(W.landed[b % SLOTS], 16)
                W.issued = b0 + nb - 1
                W.issue(sp, b0 + nb + SLOTS)

            def up_products(pe, f, reg=None):
                for v in range(2):
                    b = up_block(f, v)
                    wait(pe, split.sem, p0 + b + 1, reg, 6)
                    if v == 0 and reg is not None:
                        wait(pe, ready.sem, r0 + f - 1, reg, 2)
                    w_hi, w_lo = shaped(b, KD)
                    for s in range(2):
                        o = kit.bank[2 * (f % 2) + v][:, s * SEQ:(s + 1) * SEQ]
                        for k in range(KD):
                            terms = [(w_lo, hT), (w_hi, hT_low), (w_hi, hT)]
                            for n, (w, t) in enumerate(terms):
                                mm = nc.tensor.matmul(o, w[:, k, s * P:(s + 1) * P], t[:, k, :],
                                                      start=(k == 0 and n == 0), stop=(k == KD - 1 and n == 2))
                    mm.then_inc(W.multiplied, 1)

            def down_products(pe, f, reg=None, last=False):
                b = 3 * f + 4 if not last else nb - 1
                wait(pe, split.sem, p0 + b + 1, reg, 6)
                wait(pe, ready.sem, r0 + f + 1, reg, 2)
                w_hi, w_lo = shaped(b, 2)
                for T in range(NT):
                    for half in range(2):
                        for s in range(2):
                            for n, (hidden, w) in enumerate([(hid, w_lo), (hid_low, w_hi), (hid, w_hi)]):
                                mm = nc.tensor.matmul(kit.bank[4 + 2 * T + half][:, :],
                                                      hidden[:, f % 2, s, T * P:(T + 1) * P],
                                                      w[:, s, half * 512:(half + 1) * 512], start=False,
                                                      stop=(last and s == 1 and n == 2), skip_group_check=True)
                mm.then_inc(W.multiplied, 1)

            @block.tensor
            def _(pe):
                for bnk in range(4, 8):
                    nc.tensor.matmul(kit.bank[bnk][:, :], kit.zeros[0:1, 0:P], kit.zeros[0:1, :], start=True, stop=False,
                                     skip_group_check=True)
                up_products(pe, 0)
                with pe.Fori(0, loops) as i:
                    for f in (1, 2):
                        up_products(pe, f, reg=i)
                        down_products(pe, f - 1, reg=i)
                down_products(pe, FF_BLOCKS - 1, last=True)

            @block.scalar
            def _(act):
                def make_high(b, reg=None):
                    wait(act, W.landed[(b0 + b) % SLOTS], 16 * ((b0 + b) // SLOTS + 1), reg, 16)
                    if reg is not None:
                        wait(act, W.multiplied, b0 + b - SPLIT_SLOTS + 1, reg, 6)
                    w, hi, _ = parts(b)
                    nc.scalar.copy(hi, w).then_inc(high_made.sem, 1)

                def gate(f, reg=None):
                    wait(act, W.multiplied, b0 + up_block(f, 0) + 1, reg, 6)
                    if reg is not None:
                        wait(act, ready.sem, r0 + f - 1, reg, 2)
                    nc.scalar.activation(ag[:, f % 2], kit.bank[2 * (f % 2)][:, :], ACT.Silu).then_inc(silued.sem, 1)

                for b in range(3):
                    make_high(b)
                gate(0)
                with act.Fori(0, loops) as i:
                    for b, f in ((3, None), (4, 1), (5, None), (6, None), (7, 2), (8, None)):
                        make_high(b, reg=i)
                        if f:
                            gate(f, reg=i)

            @block.vector
            def _(dve):
                def make_low(b, reg=None):
                    wait(dve, high_made.sem, h0 + b + 1, reg, 6)
                    w, hi, lo = parts(b)
                    nc.vector.tensor_tensor(lo, w, hi.bitcast(F32), ALU.subtract).then_inc(split.sem, 1)

                def make_hidden(f, reg=None):
                    wait(dve, W.multiplied, b0 + up_block(f, 1) + 1, reg, 6)
                    wait(dve, silued.sem, s0 + f + 1, reg, 2)
                    flat = lambda a: a[:, f % 2].rearrange("p s t -> p (s t)")
                    nc.vector.tensor_tensor(ag[:, f % 2], ag[:, f % 2], kit.bank[2 * (f % 2) + 1][:, :],
                                            ALU.mult).then_inc(made.sem, 1)
                    wait(dve, made.sem, m0 + 2 * f + 1, reg, 4)
                    nc.vector.tensor_copy(flat(hid), ag[:, f % 2]).then_inc(made.sem, 1)
                    wait(dve, made.sem, m0 + 2 * f + 2, reg, 4)
                    nc.vector.tensor_tensor(flat(hid_low), ag[:, f % 2], flat(hid).bitcast(F32), ALU.subtract) \
                        .then_inc(ready.sem, 1)

                made = kit.count("hidden_steps")
                m0 = made.n
                for b in range(3):
                    make_low(b)
                make_hidden(0)
                with dve.Fori(0, loops) as i:
                    for b, f in ((3, None), (4, None), (5, 1), (6, None), (7, None), (8, 2)):
                        make_low(b, reg=i)
                        if f:
                            make_hidden(f, reg=i)
                made.n += 2 * FF_BLOCKS
                dve.wait_ge(W.multiplied, b0 + nb)
                for T in range(NT):
                    for half in range(2):
                        xs = x[:, T, half * 512:(half + 1) * 512]
                        nc.vector.scalar_tensor_tensor(out=xs, in0=kit.bank[4 + 2 * T + half][:, :], scalar=0.5, in1=xs,
                                                       op0=ALU.mult, op1=ALU.add)
    silued.n += FF_BLOCKS
    ready.n += FF_BLOCKS
    high_made.n += nb
    split.n += nb
    W.used += nb



def parallel_attention(kit, dram):
    nc, W = kit.nc, kit.weights
    x, h, hT = kit.x, kit.h, kit.hT
    norm_plain(kit, x, dram["mix_norm_2"][0:1, :], h)
    transpose_tokens(kit, h, hT)
    QK0, NQK = 3 * SB_HEADS * HD, 2 * DIL_HEADS * HD
    V0 = QK0 + NQK
    width = (SB_HEADS + GROUP_HEADS) * HD
    with kit.sb("cat2", [P, NT, width]) as cat:
        with kit.sb("proj2", [P, NT, 3 * D]) as proj, kit.sb("tT", [P, 16, SEQ]) as tT:
            linear(kit, hT, 12, False, copy_out(kit, proj))
            head_norms(kit, dram, proj, QK0)
            cols = [i * P for i in range(4)] + [QK0 + i * P for i in range(12)]
            jobs = []
            for T in range(NT):
                for c in range(0, 16, 4):
                    jobs.append(([proj[:, T, cols[c + i]:cols[c + i] + P] for i in range(4)],
                                 tT[:, c:c + 4, T * P:(T + 1) * P]))
            transposes(kit, jobs)
            stick_breaking(kit, proj, tT, cat)
            dilated(kit, dram, proj, tT, cat, V0)
        transpose_tokens(kit, cat, hT, kc=4)
        b0 = W.used
        done = kit.count("attention_projected")
        d0 = done.n
        with nc.Block() as block:
            @block.sync
            def _(sp):
                W.issue(sp, b0 + 2 + SLOTS)

            @block.tensor
            def _(pe):
                for b in range(2):
                    W.wait(pe, b0 + b)
                    w = W.tile(b0 + b, 4)
                    for T in range(NT):
                        for k in range(4):
                            mm = nc.tensor.matmul(kit.bank[2 * b + T][:, :], hT[:, k, T * P:(T + 1) * P], w[:, k, :],
                                                  start=(k == 0), stop=(k == 3))
                    mm.then_inc(W.multiplied, 1)

            @block.vector
            def _(dve):
                for b in range(2):
                    dve.wait_ge(W.multiplied, b0 + b + 1)
                    for T in range(NT):
                        xs = x[:, T, b * 512:(b + 1) * 512]
                        nc.vector.tensor_tensor(xs, xs, kit.bank[2 * b + T][:, :], ALU.add)
        W.used += 2


def head_norms(kit, dram, proj, c0):
    nc = kit.nc
    n = DIL_HEADS
    loaded = kit.count("loaded")
    l0 = loaded.n
    with kit.sb("qkg", [P, 2, HD]) as qkg, kit.sb("sq", [P, 2 * n, HD]) as sq, kit.sb("st", [P, 3, 2 * n]) as st, \
            nc.Block() as block:
        @block.sync
        def _(sp):
            kit.load(sp, qkg[:, 0], bcast(dram["attn_q_norm_2"], HD))
            kit.load(sp, qkg[:, 1], bcast(dram["attn_k_norm_2"], HD))

        @block.scalar
        def _(act):
            kit.roots(act, [(st[:, 2], st[:, 1])] * NT)

        @block.vector
        def _(dve):
            for T in range(NT):
                v = proj[:, T, c0:c0 + 2 * n * HD].rearrange("p (g d) -> p g d", d=HD)
                kit.dve(nc.vector.tensor_tensor(sq[:], v, v, ALU.mult))
                kit.dve(nc.vector.tensor_reduce(st[:, 0], sq[:], AX, ALU.add))
                kit.rsqrt(dve, nc.vector.tensor_scalar(st[:, 1], st[:, 0], 1.0 / HD, EPS, ALU.mult, ALU.add), st[:, 2], st[:, 2])
                kit.dve(nc.vector.tensor_tensor(v, v, st[:, 2].unsqueeze(2).to_broadcast([P, 2 * n, HD]), ALU.mult))
                if T == 0:
                    dve.wait_ge(loaded.sem, l0 + 32)
                for s in range(2):
                    vs = v[:, s * n:(s + 1) * n]
                    kit.dve(nc.vector.tensor_tensor(vs, vs, qkg[:, s].unsqueeze(1).to_broadcast([P, n, HD]), ALU.mult))


def stick_breaking(kit, proj, tT, cat):
    nc = kit.nc
    H = SB_HEADS
    scored, zed, logged, kept, summed, logw, weighed, ready, mixed = (
        kit.count(n) for n in ("sb_scored", "sb_z", "sb_log", "sb_kept", "sb_after", "sb_logw", "sb_exped", "sb_ready",
                               "sb_mixed"))
    base = {c: c.n for c in (scored, zed, logged, kept, summed, logw, weighed, ready, mixed)}
    with kit.sb("z", [P, H, NT, SEQ]) as z, kit.sb("lg", [P, H, NT, SEQ]) as lg, kit.sb("lk", [P, H, NT, SEQ]) as lk, \
            nc.Block() as block:
        @block.tensor
        def _(pe):
            for hh in range(H):
                b, c = hh % 2 * HD, hh // 2
                for kt in range(NT):
                    mm = nc.tensor.matmul(kit.bank[hh][:, kt * SEQ:(kt + 1) * SEQ],
                                          tT[b:b + HD, 2 + c, kt * P:(kt + 1) * P], tT[b:b + HD, c, :],
                                          start=True, stop=True)
                scored.up(mm)
            for hh in range(H):
                pe.wait_ge(kept.sem, base[kept] + hh + 1)
                bank = kit.bank[4 + hh % 4]
                nc.tensor.matmul(bank[:, 0:SEQ], kit.after, lk[:, hh, 0, :], start=True, stop=False)
                nc.tensor.matmul(bank[:, 0:SEQ], kit.ones[:, 0:P], lk[:, hh, 1, :], start=False, stop=True)
                summed.up(nc.tensor.matmul(bank[:, SEQ:2 * SEQ], kit.after, lk[:, hh, 1, :], start=True, stop=True))
            for hh in range(H):
                pe.wait_ge(ready.sem, base[ready] + hh + 1)
                for T in range(NT):
                    for kt in range(T + 1):
                        mm = nc.tensor.matmul(kit.bank[0][:, (T * H + hh) * HD:(T * H + hh + 1) * HD],
                                              z[:, hh, kt, T * P:(T + 1) * P],
                                              proj[:, kt, (2 * H + hh) * HD:(2 * H + hh + 1) * HD],
                                              start=(kt == 0), stop=(kt == T))
                mixed.up(mm)

        @block.scalar
        def _(act):
            for hh in range(H):
                act.wait_ge(scored.sem, base[scored] + hh + 1)
                zv = z[:, hh].rearrange("p k q -> p (k q)")
                lv = lg[:, hh].rearrange("p k q -> p (k q)")
                zed.up(nc.scalar.activation(zv, kit.bank[hh][:, :], ACT.Copy, scale=SCALE))
                kit.act(nc.scalar.activation(lv, kit.bank[hh][:, :], ACT.Abs, scale=SCALE))
                kit.act(nc.scalar.activation(lv, lv, ACT.Exp, scale=-1.0))
                logged.up(nc.scalar.activation(lv, lv, ACT.Ln, bias=1.0))
            for hh in range(H):
                act.wait_ge(logw.sem, base[logw] + hh + 1)
                zv = z[:, hh].rearrange("p k q -> p (k q)")
                weighed.up(nc.scalar.activation(zv, zv, ACT.Exp))
            act.wait_ge(mixed.sem, base[mixed] + H)
            nc.scalar.copy(cat[:, :, 0:H * HD], kit.bank[0][:, :].rearrange("p (t n) -> p t n", t=NT))

        @block.vector
        def _(dve):
            for hh in range(H):
                dve.wait_ge(zed.sem, base[zed] + hh + 1)
                dve.wait_ge(logged.sem, base[logged] + hh + 1)
                kit.dve(nc.vector.scalar_tensor_tensor(out=lg[:, hh], in0=z[:, hh], scalar=0.0, in1=lg[:, hh],
                                                       op0=ALU.max, op1=ALU.add))
                kept.up(nc.vector.scalar_tensor_tensor(out=lk[:, hh], in0=lg[:, hh], scalar=-1.0, in1=kit.strict,
                                                       op0=ALU.mult, op1=ALU.mult))
                kit.dve(nc.vector.tensor_tensor(z[:, hh], z[:, hh], lg[:, hh], ALU.subtract))
            for hh in range(H):
                dve.wait_ge(summed.sem, base[summed] + hh + 1)
                logw.up(nc.vector.tensor_tensor(z[:, hh], z[:, hh], kit.bank[4 + hh % 4][:, :].rearrange(
                    "p (k q) -> p k q", k=NT), ALU.add))
            for hh in range(H):
                dve.wait_ge(weighed.sem, base[weighed] + hh + 1)
                ready.up(nc.vector.tensor_tensor(z[:, hh], z[:, hh], kit.strict, ALU.mult))


def dilated(kit, dram, proj, tT, cat, v0):
    nc = kit.nc
    G, J = DIL_GROUPS, GROUP_HEADS
    loaded, rowed, copied, stored = (kit.count(n) for n in ("loaded", "bias_rows", "bias_copied", "bias_stored"))
    l0, r0, c0, t0 = loaded.n, rowed.n, copied.n, stored.n
    scratch = dram["bias_scratch"]
    with kit.sb("bias", [P, NT, DIL_HEADS, SEQ]) as bias:
        with kit.sb("onehot", [N_BUCKETS + 1, G, 512]) as onehot, kit.sb("table", [N_BUCKETS + 1, DIL_HEADS]) as table, \
                kit.sb("bias_rows", [J, G, 512]) as rows, nc.Block() as block:
            @block.vector
            def _(dve):
                nc.vector.memset(table[N_BUCKETS:N_BUCKETS + 1, :], NEG).then_inc(rowed.sem, 1)
                rowed.n += 1

            @block.sync
            def _(sp):
                kit.load(sp, onehot[:], dram["onehot"])
                kit.load(sp, table[0:N_BUCKETS, :], dram["rel_bias_2"])
                sp.wait_ge(copied.sem, c0 + G)
                stored.up(sp.dma_start(scratch.rearrange("(g j) n -> j g n", g=G), rows[:]), 16)
                sp.wait_ge(stored.sem, t0 + 16)
                for T in range(NT):
                    src = bass.AP(scratch.tensor, scratch.offset + T * P, [[1, P], [512, DIL_HEADS], [1, SEQ]])
                    kit.load(sp, bias[:, T], src)
                sp.wait_ge(loaded.sem, l0 + 64)

            @block.tensor
            def _(pe):
                pe.wait_ge(loaded.sem, l0 + 32)
                pe.wait_ge(rowed.sem, r0 + 1)
                for g in range(G):
                    rowed.up(nc.tensor.matmul(kit.bank[g][0:J, :], table[:, g * J:(g + 1) * J], onehot[:, g, :],
                                              start=True, stop=True))

            @block.scalar
            def _(act):
                for g in range(G):
                    act.wait_ge(rowed.sem, r0 + 2 + g)
                    copied.up(nc.scalar.copy(rows[:, g, :], kit.bank[g][0:J, :]))

        units = [(T, j) for T in range(NT) for j in range(J)]
        nu = len(units)
        scored, masked = kit.count("scored"), kit.count("score_masked")
        negmax, exped = kit.count("negmax_ready"), kit.count("exped")
        s0, k0, n0, x0 = scored.n, masked.n, negmax.n, exped.n
        with kit.sb("probs", [P, nu, G * SEQ]) as probs, kit.sb("PT", [P, 4, 4, P]) as PT, \
                kit.sb("gmax", [P, nu, G]) as gmax, kit.sb("rows", [P, 4, nu]) as rows:
            chunks = [[c for c in range(2 * G) if c % 2 <= T] for T, _ in units]
            pe_side, act_side, m_end = attend(
                kit, chunks, PT, lambda u: kit.bank[4][:, u * HD:(u + 1) * HD],
                lambda u, c: probs[:, u, c * P:(c + 1) * P],
                lambda u, c: proj[:, c % 2, v0 + (c // 2 * J + units[u][1]) * HD:v0 + (c // 2 * J + units[u][1] + 1) * HD])
            mixed = kit.count("values_mixed")
            with nc.Block() as block:
                @block.tensor
                def _(pe):
                    for u, (T, j) in enumerate(units):
                        for g in range(G):
                            n = u * G + g
                            if n >= 4:
                                pe.wait_ge(masked.sem, k0 + n - 3)
                            hh = g * J + j
                            b = hh % 2 * HD
                            scored.up(nc.tensor.matmul(kit.bank[n % 4][:, 0:SEQ], tT[b:b + HD, 4 + hh // 2, T * P:(T + 1) * P],
                                                       tT[b:b + HD, 10 + hh // 2, :], start=True, stop=True))
                    pe.wait_ge(masked.sem, k0 + nu * G)
                    pe_side(pe, lambda pe, u: pe.wait_ge(exped.sem, x0 + u + 1))

                @block.vector
                def _(dve):
                    for u, (T, j) in enumerate(units):
                        for g in range(G):
                            n = u * G + g
                            dve.wait_ge(scored.sem, s0 + n + 1)
                            masked.up(nc.vector.tensor_tensor_reduce(
                                out=probs[:, u, g * SEQ:(g + 1) * SEQ], in0=kit.bank[n % 4][:, 0:SEQ],
                                in1=bias[:, T, g * J + j, ::-1], scale=SCALE, scalar=NEG, op0=ALU.add, op1=ALU.max,
                                accum_out=gmax[:, u, g:g + 1]))
                    dve.wait_ge(masked.sem, k0 + nu * G)
                    kit.dve(nc.vector.tensor_reduce(rows[:, 0], gmax[:], AX, ALU.max))
                    negmax.up(nc.vector.tensor_scalar(rows[:, 1], rows[:, 0], -1.0, None, ALU.mult))
                    dve.wait_ge(exped.sem, x0 + nu)
                    kit.dve(nc.vector.reciprocal(rows[:, 3], rows[:, 2]))
                    dve.wait_ge(mixed.sem, m_end)
                    for T in range(NT):
                        nc.vector.tensor_tensor(
                            cat[:, T, SB_HEADS * HD:].rearrange("p (j d) -> p j d", d=HD),
                            kit.bank[4][:, T * J * HD:(T + 1) * J * HD].rearrange("p (j d) -> p j d", d=HD),
                            rows[:, 3, T * J:(T + 1) * J].unsqueeze(2).to_broadcast([P, J, HD]), ALU.mult)

                @block.scalar
                def _(act):
                    act.wait_ge(negmax.sem, n0 + 1)
                    for u in range(nu):
                        exped.up(nc.scalar.activation(probs[:, u], probs[:, u], ACT.Exp, bias=rows[:, 1, u:u + 1],
                                                      accum_out=rows[:, 2, u:u + 1]))
                    act_side(act)



def load_only(kit, pairs):
    loaded = kit.count("loaded")
    l0 = loaded.n
    with kit.nc.Block() as block:
        @block.sync
        def _(sp):
            for dst, src in pairs:
                kit.load(sp, dst, src)
            sp.wait_ge(loaded.sem, l0 + 16 * len(pairs))


def vector_only(kit, body, roots=()):
    with kit.nc.Block() as block:
        @block.scalar
        def _(act):
            kit.roots(act, roots)

        @block.vector
        def _(dve):
            body(dve)


def time_mix(kit, dram):
    x, h, hT = kit.x, kit.h, kit.hT
    norm_plain(kit, x, dram["mix_norm_2"][1:2, :], h)
    transpose_tokens(kit, h, hT)
    sb = kit.sb
    with sb("R", [P, NT, D]) as R, sb("K", [P, NT, D]) as K, sb("V", [P, NT, D]) as V, sb("A", [P, NT, D]) as A, \
            sb("KK", [P, NT, D]) as KK, sb("G", [P, NT, D]) as G, sb("bonus", [P, NT, RH]) as bonus, \
            sb("chunk_decay", [P, KD, NT, CH]) as PC:
        with sb("L", [P, NT, D]) as L:
            projections(kit, dram, R, K, V, A, L, G)
            prepare_keys(kit, dram, R, K, A, KK, L, bonus, PC)
        with sb("inverseT", [P, NT * RH, P]) as inv:
            invert(kit, dram, A, KK, inv)
            with sb("states", [P, CH + 1, KD, HD]) as S:
                vector_only(kit, lambda dve: kit.nc.vector.memset(S[:, CH], 0.0))
                for T in range(NT):
                    recur(kit, T, R, K, V, A, KK, PC, inv, S)
        finish_mix(kit, dram, R, V, G, bonus)


def projections(kit, dram, R, K, V, A, L, G):
    nc, W = kit.nc, kit.weights
    hT = kit.hT
    xx = kit.h[:].rearrange("p t (a n) -> p (t a) n", n=SEQ)
    with kit.sb("mixed", [P, 3, KD, SEQ]) as xm, kit.sb("mix_rows", [6 * KD, P]) as mix_rows, kit.sb("mixT", [P, 6 * KD]) as mixT:
        load_only(kit, [(mix_rows[:], dram["rw_mix_2"].rearrange("e i (k p) -> (e i k) p", p=P))])
        transposes(kit, [([mix_rows[:]], mixT[:].unsqueeze(1))])

        def shift(dve):
            nc.vector.tensor_scalar(xx[:, :, 0:1], hT[:, :, 0:1], -1.0, None, ALU.mult)
            kit.dve(nc.vector.tensor_tensor(xx[:, :, 1:], hT[:, :, 0:SEQ - 1], hT[:, :, 1:], ALU.subtract))

        def mixes(which):
            def body(dve):
                if which[0] == 0:
                    shift(dve)
                for n, i in enumerate(which):
                    for k in range(KD):
                        nc.vector.scalar_tensor_tensor(out=xm[:, n, k], in0=xx[:, k], scalar=mixT[:, i * KD + k:i * KD + k + 1],
                                                       in1=hT[:, k], op0=ALU.mult, op1=ALU.add)
            return body

        vector_only(kit, mixes((0, 2, 3)))
        linear(kit, None, 12, False,
               lambda b, bank: nc.scalar.copy((R, K, V)[b // 4][:, :, b % 4 * BLK:(b % 4 + 1) * BLK], bank),
               lhs_of=lambda pe, b: xm[:, b // 4])
        vector_only(kit, mixes((1, 4, 5)))
        with kit.sb("w1", [P, KD, 64]) as w1, kit.sb("a1", [P, KD, 64]) as a1, kit.sb("g1", [P, KD, 160]) as g1, \
                kit.sb("w2", [64, D]) as w2, kit.sb("a2", [64, D]) as a2, kit.sb("g2", [P, D]) as g2, \
                kit.sb("g2b", [32, D]) as g2b, kit.sb("w0", [P, D]) as w0, kit.sb("a0", [P, D]) as a0, \
                kit.sb("tw", [64, SEQ]) as tw, kit.sb("ta", [64, SEQ]) as ta, kit.sb("tg", [P, SEQ]) as tg, \
                kit.sb("tgb", [32, SEQ]) as tgb:
            load_only(kit, [(t[:], dram[n][0].rearrange("(k p) n -> p k n", p=P)) for t, n in
                            ((w1, "rw_w1_2"), (a1, "rw_a1_2"), (g1, "rw_g1_2"))] +
                      [(w2[:], dram["rw_w2_2"][0]), (a2[:], dram["rw_a2_2"][0]), (g2[:], dram["rw_g2_2"][0, 0:P]),
                       (g2b[:], dram["rw_g2_2"][0, P:160]), (w0[:], bcast(dram["rw_w0_2"], D)),
                       (a0[:], bcast(dram["rw_a0_2"], D))])
            inner, innered, outer, biased = (kit.count(n) for n in ("lora_in", "lora_in_copied", "lora_out", "lora_biased"))
            i0, c0, o0, z0 = inner.n, innered.n, outer.n, biased.n
            with nc.Block() as block:
                @block.tensor
                def _(pe):
                    for n, (w, lo, hi) in enumerate(((w1, 0, 64), (a1, 0, 64), (g1, 0, P), (g1, P, 160))):
                        for k in range(KD):
                            mm = nc.tensor.matmul(kit.bank[n][0:hi - lo, 0:SEQ], w[:, k, lo:hi], xm[:, min(n, 2), k],
                                                  start=(k == 0), stop=(k == KD - 1))
                        inner.up(mm)
                    for n, parts in enumerate((((tw, w2),), ((ta, a2),), ((tg, g2), (tgb, g2b)))):
                        pe.wait_ge(innered.sem, c0 + (1 if n == 0 else 4))
                        for q in range(4):
                            T, half = q // 2, q % 2
                            if n == 2:
                                pe.wait_ge(biased.sem, z0 + q + 1)
                            for i, (t, w) in enumerate(parts):
                                mm = nc.tensor.matmul(kit.bank[(4 if n != 1 else 0) + q][:, :], t[:, T * P:(T + 1) * P],
                                                      w[:, half * 512:(half + 1) * 512],
                                                      start=(i == 0), stop=(i == len(parts) - 1))
                            outer.up(mm)

                @block.scalar
                def _(act):
                    for n, (t, rows, func) in enumerate(((tw, 64, ACT.Tanh), (ta, 64, ACT.Copy), (tg, P, ACT.Sigmoid),
                                                         (tgb, 32, ACT.Sigmoid))):
                        act.wait_ge(inner.sem, i0 + n + 1)
                        innered.up(nc.scalar.activation(t[:], kit.bank[n][0:rows, 0:SEQ], func))
                    for n, dst in enumerate((L, A)):
                        act.wait_ge(biased.sem, z0 + 4 * n + 4)
                        nc.scalar.activation(dst[:], dst[:], ACT.Sigmoid)
                    for q in range(4):
                        act.wait_ge(outer.sem, o0 + 8 + q + 1)
                        nc.scalar.copy(G[:, q // 2, q % 2 * 512:(q % 2 + 1) * 512], kit.bank[4 + q][:, :])

                @block.vector
                def _(dve):
                    for n, (dst, row) in enumerate(((L, w0), (A, a0))):
                        for q in range(4):
                            T, cols = q // 2, slice(q % 2 * 512, (q % 2 + 1) * 512)
                            dve.wait_ge(outer.sem, o0 + 4 * n + q + 1)
                            biased.up(nc.vector.tensor_tensor(dst[:, T, cols], kit.bank[(4 if n == 0 else 0) + q][:, :],
                                                              row[:, cols], ALU.add))


def heads(a):
    return a.rearrange("p (h d) -> p h d", d=HD)


def wide(row, n=HD):
    return row.unsqueeze(2).to_broadcast([P, row.shape[1], n])


def prepare_keys(kit, dram, R, K, A, KK, L, bonus, PC):
    nc = kit.nc
    ready, summed, exped, tmp_free, shifted = (kit.count(n) for n in ("log_decay_ready", "log_decay_summed", "decay_exped",
                                                                     "tmp_free", "log_decay_shifted"))
    r0, s0, x0, t0, h0 = ready.n, summed.n, exped.n, tmp_free.n, shifted.n
    with kit.sb("kk_w", [P, 3, D]) as rows, kit.sb("decay", [P, NT, D]) as up, kit.sb("rsum", [P, 4, RH]) as rs:
        down = kit.h
        load_only(kit, [(rows[:, 0], bcast(dram["rw_kk_2"], D)), (rows[:, 1], bcast(dram["rw_ka_2"], D)),
                        (rows[:, 2], bcast(dram["rw_rk_2"].rearrange("e h d -> e (h d)"), D))])
        with nc.Block() as block:
            @block.vector
            def _(dve):
                ready.up(nc.vector.tensor_scalar(L[:], L[:], -float(np.exp(-0.5)), None, ALU.mult))
                for T in range(NT):
                    t = down[:, T]
                    kit.dve(nc.vector.tensor_tensor(KK[:, T], K[:, T], rows[:, 0], ALU.mult))
                    kit.dve(nc.vector.tensor_tensor(t, KK[:, T], KK[:, T], ALU.mult))
                    kit.dve(nc.vector.tensor_reduce(rs[:, 0], heads(t), AX, ALU.add))
                    kit.rsqrt(dve, nc.vector.tensor_scalar(rs[:, 1], rs[:, 0], 1e-24, None, ALU.max), rs[:, 2], rs[:, 2])
                    kit.dve(nc.vector.tensor_tensor(heads(KK[:, T]), heads(KK[:, T]), wide(rs[:, 2]), ALU.mult))
                    kit.dve(nc.vector.scalar_tensor_tensor(out=t, in0=A[:, T], scalar=-1.0, in1=rows[:, 1],
                                                           op0=ALU.add, op1=ALU.mult))
                    kit.dve(nc.vector.scalar_tensor_tensor(out=K[:, T], in0=t, scalar=1.0, in1=K[:, T],
                                                           op0=ALU.add, op1=ALU.mult))
                    kit.dve(nc.vector.tensor_tensor(t, R[:, T], K[:, T], ALU.mult))
                    kit.dve(nc.vector.tensor_tensor(t, t, rows[:, 2], ALU.mult))
                    kit.dve(nc.vector.tensor_reduce(bonus[:, T], heads(t), AX, ALU.add))
                    kit.dve(nc.vector.tensor_tensor(A[:, T], A[:, T], KK[:, T], ALU.mult))
                tmp_free.up(nc.vector.memset(kit.spare[:, 0:1], 0.0))
                dve.wait_ge(summed.sem, s0 + 2)
                for q in range(4):
                    T, cols = q // 2, slice(q % 2 * 512, (q % 2 + 1) * 512)
                    shifted.up(nc.vector.tensor_tensor(L[:, T, cols], kit.bank[q][:, :], L[:, T, cols], ALU.subtract))
                dve.wait_ge(exped.sem, x0 + 4)
                nc.vector.tensor_tensor(R[:], R[:], up[:], ALU.mult)
                dve.wait_ge(exped.sem, x0 + 8)
                nc.vector.tensor_tensor(K[:], K[:], down[:], ALU.mult)
                nc.vector.tensor_tensor(A[:], A[:], down[:], ALU.mult)
                dve.wait_ge(exped.sem, x0 + 9)
                nc.vector.scalar_tensor_tensor(out=KK[:], in0=KK[:], scalar=-1.0, in1=L[:], op0=ALU.mult, op1=ALU.mult)

            @block.tensor
            def _(pe):
                pe.wait_ge(ready.sem, r0 + 1)
                for q in range(4):
                    mm = nc.tensor.matmul(kit.bank[q][:, :], kit.le, L[:, q // 2, q % 2 * 512:(q % 2 + 1) * 512],
                                          start=True, stop=True)
                summed.up(mm)
                for k in range(KD):
                    for T in range(NT):
                        n = (k * NT + T) * CH
                        mm = nc.tensor.matmul(kit.bank[4][:, n:n + CH], L[:, T, k * P:(k + 1) * P], kit.ends,
                                              start=True, stop=True)
                summed.up(mm)

            @block.scalar
            def _(act):
                kit.roots(act, [(rs[:, 2], rs[:, 1])] * NT)
                act.wait_ge(summed.sem, s0 + 2)
                nc.scalar.activation(PC[:].rearrange("p k t c -> p (k t c)"), kit.bank[4][:, 0:KD * NT * CH], ACT.Exp)
                for q in range(4):
                    act.wait_ge(shifted.sem, h0 + q + 1)
                    exped.up(nc.scalar.activation(up[:, q // 2, q % 2 * 512:(q % 2 + 1) * 512], kit.bank[q][:, :], ACT.Exp))
                act.wait_ge(tmp_free.sem, t0 + 1)
                for q in range(4):
                    exped.up(nc.scalar.activation(down[:, q // 2, q % 2 * 512:(q % 2 + 1) * 512], kit.bank[q][:, :],
                                                  ACT.Exp, scale=-1.0))
                act.wait_ge(shifted.sem, h0 + 4)
                exped.up(nc.scalar.activation(L[:], L[:], ACT.Exp))


def invert(kit, dram, A, KK, inv):
    nc = kit.nc
    NS = NT * RH
    grams, masked, stored, loaded, solved = (kit.count(n) for n in ("grams", "grams_masked", "systems_stored", "loaded",
                                                                    "solved"))
    g0, m0, t0, l0, v0 = grams.n, masked.n, stored.n, loaded.n, solved.n
    tri, out = (dram[n].rearrange("(u c) (j t) -> c j u t", c=CH, j=C) for n in ("systems", "inverses"))
    with kit.sb("sysd", [P, NS, C]) as sysd, kit.sb("sys", [P, C, C]) as sy, kit.sb("XT", [P, C, C]) as XT, \
            kit.sb("terms", [P, C, C]) as terms:
        with kit.sb("aT", [P, NT * KD, P]) as aT, kit.sb("bT", [P, NT * KD, P]) as bT:
            transposes(kit, [([src[:, T, (k + i) * P:(k + i + 1) * P] for i in range(4)],
                              dst[:, T * KD + k:T * KD + k + 4, :])
                             for src, dst in ((KK, aT), (A, bT)) for T in range(NT) for k in (0, 4)])
            with nc.Block() as block:
                @block.tensor
                def _(pe):
                    for n in range(NS // 4):
                        if n >= 4:
                            pe.wait_ge(masked.sem, m0 + (n - 3) * CH)
                        for i in range(4):
                            b, p = n % 2 * HD, n // 2 * 4 + i
                            mm = nc.tensor.matmul(kit.bank[n % 4][:, i * P:(i + 1) * P], bT[b:b + HD, p, :],
                                                  aT[b:b + HD, p, :], start=True, stop=True)
                        grams.up(mm)

                @block.vector
                def _(dve):
                    for n in range(NS // 4):
                        dve.wait_ge(grams.sem, g0 + n + 1)
                        for c in range(CH):
                            r = slice(c * C, (c + 1) * C)
                            bank = kit.bank[n % 4][:, :].rearrange("p (u t) -> p u t", u=4)
                            u = n // 2 * 8 + n % 2
                            masked.up(nc.vector.tensor_tensor(sysd[r, u:u + 7:2, :], bank[r, :, r],
                                                              kit.lt[r, r].unsqueeze(1).to_broadcast([C, 4, C]), ALU.mult))

        with nc.Block() as block:
            @block.sync
            def _(sp):
                for c in range(CH):
                    stored.up(sp.dma_start(tri[c], sysd[c * C:(c + 1) * C]), 16)
                sp.wait_ge(stored.sem, t0 + 16 * CH)
                kit.load(sp, sy[:], dram["systems"].rearrange("s (j t) -> s j t", j=C))
                sp.wait_ge(solved.sem, v0 + 1)
                stored.up(sp.dma_start(dram["inverses"].rearrange("s (j t) -> s j t", j=C), XT[:]), 16)
                sp.wait_ge(stored.sem, t0 + 16 * (CH + 1))
                for c in range(CH):
                    r = slice(c * C, (c + 1) * C)
                    kit.load(sp, inv[r, :, r], out[c])
                sp.wait_ge(loaded.sem, l0 + 16 * (CH + 1))

            @block.vector
            def _(dve):
                kit.dve(nc.vector.memset(XT[:], 0.0))
                kit.dve(nc.vector.memset(XT[:].rearrange("p j t -> p (j t)")[:, 0::C + 1], 1.0))
                nc.vector.memset(inv[:], 0.0)
                dve.wait_ge(loaded.sem, l0 + 16)
                for t in range(1, C):
                    kit.dve(nc.vector.tensor_tensor(terms[:, 0:t, 0:t], XT[:, 0:t, 0:t],
                                                    sy[:, 0:t, t].unsqueeze(1).to_broadcast([P, t, t]), ALU.mult))
                    ins = nc.vector.tensor_reduce(XT[:, 0:t, t], terms[:, 0:t, 0:t], AX, ALU.add)
                    if t < C - 1:
                        kit.dve(ins)
                    else:
                        solved.up(ins)


def recur(kit, T, R, K, V, A, KK, PC, inv, S):
    nc = kit.nc
    KT = kit.hT[:].rearrange("p a n -> p (a n)")[:, 0:KD * P].rearrange("p (a n) -> p a n", n=P)
    BT = kit.hT[:].rearrange("p a n -> p (a n)")[:, KD * P:].rearrange("p (a n) -> p a n", n=P)
    Q, U = kit.h[:, 0], kit.h[:, 1]
    with kit.sb("arT", [P, KD, 2, P]) as arT, kit.sb("GK", [P, RH, 2 * P]) as GK, kit.sb("GB", [P, RH, P]) as GB, \
            kit.sb("W1T", [P, KD, P]) as W1T, kit.sb("W2", [P, D]) as W2:
        flat = arT[:].rearrange("p k s t -> p (k s) t")
        jobs = []
        for k in range(0, KD, 2):
            jobs.append(([s[:, T, (k + i) * P:(k + i + 1) * P] for i in range(2) for s in (KK, R)], flat[:, 2 * k:2 * k + 4]))
        for src, dst in ((K, KT), (A, BT)):
            for k in (0, 4):
                jobs.append(([src[:, T, (k + i) * P:(k + i + 1) * P] for i in range(4)], dst[:, k:k + 4]))
        transposes(kit, jobs)
        place = lambda hh: (slice(hh % 2 * HD, (hh % 2 + 1) * HD), hh // 2)
        cols = lambda hh: slice(hh * HD, (hh + 1) * HD)
        parity = lambda a, i: a.rearrange("p (a b d) -> p a b d", b=2, d=HD)[:, :, i]

        grams, masked = kit.count("grams"), kit.count("grams_masked")
        g0, m0 = grams.n, masked.n
        with nc.Block() as block:
            @block.tensor
            def _(pe):
                for n in range(KD):
                    if n >= 4:
                        pe.wait_ge(masked.sem, m0 + n - 3)
                    r, _ = place(n % 2)
                    for i in range(2):
                        p = n // 2 * 2 + i
                        mm = nc.tensor.matmul(kit.bank[n % 4][:, i * BLK:(i + 1) * BLK], KT[r, p, :],
                                              arT[r, p].rearrange("p s t -> p (s t)"), start=True, stop=True)
                    grams.up(mm)
                for n in range(4):
                    r, _ = place(n % 2)
                    for i in range(4):
                        p = n // 2 * 4 + i
                        mm = nc.tensor.matmul(kit.bank[4 + n][:, i * P:(i + 1) * P], BT[r, p, :], arT[r, p, 1, :],
                                              start=True, stop=True)
                    grams.up(mm)

            @block.vector
            def _(dve):
                for p in range(KD):
                    dve.wait_ge(grams.sem, g0 + p + 1)
                    u = p // 2 * 4 + p % 2
                    masked.up(nc.vector.tensor_tensor(GK[:, u:u + 3:2], kit.bank[p % 4][:, :].rearrange(
                        "p (a t) -> p a t", a=2), kit.ltle.unsqueeze(1).to_broadcast([P, 2, 2 * P]), ALU.mult))
                for n in range(4):
                    dve.wait_ge(grams.sem, g0 + KD + n + 1)
                    u = n // 2 * 8 + n % 2
                    nc.vector.tensor_tensor(GB[:, u:u + 7:2], kit.bank[4 + n][:, :].rearrange(
                        "p (a t) -> p a t", a=4), kit.le.unsqueeze(1).to_broadcast([P, 4, P]), ALU.mult)

        made, copied = kit.count("within_made"), kit.count("within_copied")
        d0, c0 = made.n, copied.n
        with nc.Block() as block:
            @block.tensor
            def _(pe):
                for hh in range(RH):
                    mm = nc.tensor.matmul(kit.bank[hh // 8][:, hh % 8 * HD:(hh % 8 + 1) * HD], GK[:, hh, 0:P],
                                          V[:, T, cols(hh)], start=True, stop=True)
                made.up(mm)
                for hh in range(RH):
                    r, p = place(hh)
                    mm = nc.tensor.matmul(kit.bank[2 + p // 4][r, p % 4 * P:(p % 4 + 1) * P], KK[:, T, cols(hh)],
                                          inv[:, T * RH + hh, :], start=True, stop=True)
                made.up(mm)
                pe.wait_ge(copied.sem, c0 + 2)
                for hh in range(RH):
                    mm = nc.tensor.matmul(kit.bank[4 + hh // 8][:, hh % 8 * HD:(hh % 8 + 1) * HD],
                                          inv[:, T * RH + hh, :], Q[:, cols(hh)], start=True, stop=True)
                made.up(mm)

            @block.scalar
            def _(act):
                act.wait_ge(made.sem, d0 + 1)
                for i in range(2):
                    copied.up(nc.scalar.copy(Q[:, i * 512:(i + 1) * 512], kit.bank[i][:, :]))
                act.wait_ge(made.sem, d0 + 2)
                for i in range(2):
                    nc.scalar.copy(W1T[:, 4 * i:4 * i + 4], kit.bank[2 + i][:, :].rearrange("p (a t) -> p a t", a=4))

            @block.vector
            def _(dve):
                nc.vector.tensor_copy(S[:, 0], S[:, CH])
                dve.wait_ge(made.sem, d0 + 3)
                for i in range(2):
                    nc.vector.tensor_copy(W2[:, i * 512:(i + 1) * 512], kit.bank[4 + i][:, :])

        read, filled, written, grown = (kit.count(n) for n in ("state_read", "u_filled", "state_products", "state_grown"))
        e0, f0, w0, n0 = read.n, filled.n, written.n, grown.n
        with nc.Block() as block:
            @block.tensor
            def _(pe):
                for c in range(CH):
                    t = slice(c * C, (c + 1) * C)
                    if c:
                        pe.wait_ge(grown.sem, n0 + c)
                    for hh in range(RH):
                        r, p = place(hh)
                        mm = nc.tensor.matmul(kit.bank[hh % 2][t, cols(p)], W1T[r, p, t],
                                              S[r, c, p, :], start=True, stop=True)
                    read.up(mm)
                    pe.wait_ge(filled.sem, f0 + 2 * c + 2)
                    for hh in range(RH):
                        r, p = place(hh)
                        o = kit.bank[2][r, p * HD:(p + 1) * HD]
                        nc.tensor.matmul(o, K[t, T, cols(hh)], V[t, T, cols(hh)], start=True, stop=False,
                                         tile_position=(c * C, hh % 2 * HD))
                        mm = nc.tensor.matmul(o, A[t, T, cols(hh)], U[t, cols(hh)], start=False, stop=True,
                                              tile_position=(c * C, hh % 2 * HD))
                    written.up(mm)

            @block.vector
            def _(dve):
                for c in range(CH):
                    t = slice(c * C, (c + 1) * C)
                    dve.wait_ge(read.sem, e0 + c + 1)
                    for i in range(2):
                        filled.up(nc.vector.tensor_tensor(parity(U, i)[t], heads(kit.bank[i][:, :])[t],
                                                          parity(W2[:], i)[t], ALU.add))
                    dve.wait_ge(written.sem, w0 + c + 1)
                    kit.dve(nc.vector.tensor_tensor(S[:, c + 1], kit.bank[2][:, :].rearrange("p (a v) -> p a v", v=HD),
                                                    S[:, c], ALU.add))
                    grown.up(nc.vector.tensor_tensor(S[:, c + 1], S[:, c + 1], wide(PC[:, :, T, c]), ALU.mult))

        y0 = made.n
        with nc.Block() as block:
            @block.tensor
            def _(pe):
                for hh in range(RH):
                    r, p = place(hh)
                    o = kit.bank[hh // 8][:, hh % 8 * HD:(hh % 8 + 1) * HD]
                    nc.tensor.matmul(o, GK[:, hh, P:2 * P], V[:, T, cols(hh)], start=True, stop=False)
                    mm = nc.tensor.matmul(o, GB[:, hh, :], U[:, cols(hh)], start=False, stop=True)
                made.up(mm)
                for hh in range(RH):
                    r, p = place(hh)
                    for c in range(CH):
                        t = slice(c * C, (c + 1) * C)
                        mm = nc.tensor.matmul(kit.bank[2 + hh % 2][t, cols(p)],
                                              arT[r, p, 1, t], S[r, c, p, :], start=True, stop=True)
                made.up(mm)

            @block.vector
            def _(dve):
                dve.wait_ge(made.sem, y0 + 1)
                for i in range(2):
                    kit.dve(nc.vector.tensor_copy(R[:, T, i * 512:(i + 1) * 512], kit.bank[i][:, :]))
                dve.wait_ge(made.sem, y0 + 2)
                for i in range(2):
                    v = parity(R[:, T], i)
                    kit.dve(nc.vector.tensor_tensor(v, v, heads(kit.bank[2 + i][:, :]), ALU.add))


def finish_mix(kit, dram, R, V, G, bonus):
    nc = kit.nc
    with kit.sb("ln", [P, 2, D]) as ln, kit.sb("sq", [P, D]) as sq, kit.sb("st", [P, 4, RH]) as st:
        load_only(kit, [(ln[:, 0], bcast(dram["rw_lnx_g_2"], D)), (ln[:, 1], bcast(dram["rw_lnx_b_2"], D))])

        def body(dve):
            for T in range(NT):
                y, v = R[:, T], V[:, T]
                kit.dve(nc.vector.tensor_reduce(st[:, 0], heads(y), AX, ALU.add))
                kit.dve(nc.vector.tensor_scalar(st[:, 0], st[:, 0], 1.0 / HD, None, ALU.mult))
                kit.dve(nc.vector.tensor_tensor(heads(y), heads(y), wide(st[:, 0]), ALU.subtract))
                kit.dve(nc.vector.tensor_tensor(sq[:], y, y, ALU.mult))
                kit.dve(nc.vector.tensor_reduce(st[:, 1], heads(sq[:]), AX, ALU.add))
                kit.rsqrt(dve, nc.vector.tensor_scalar(st[:, 2], st[:, 1], 1.0 / HD, GN_EPS, ALU.mult, ALU.add), st[:, 3], st[:, 3])
                kit.dve(nc.vector.tensor_tensor(heads(y), heads(y), wide(st[:, 3]), ALU.mult))
                kit.dve(nc.vector.tensor_tensor(y, y, ln[:, 0], ALU.mult))
                kit.dve(nc.vector.tensor_tensor(y, y, ln[:, 1], ALU.add))
                kit.dve(nc.vector.tensor_tensor(heads(v), heads(v), wide(bonus[:, T]), ALU.mult))
                kit.dve(nc.vector.tensor_tensor(y, y, v, ALU.add))
                kit.dve(nc.vector.tensor_tensor(y, y, G[:, T], ALU.mult))
        vector_only(kit, body, roots=[(st[:, 3], st[:, 2])] * NT)
    transpose_tokens(kit, R, kit.hT)

    def add(b, bank):
        c = slice(b * BLK, (b + 1) * BLK)
        return nc.vector.tensor_tensor(kit.x[:, :, c], kit.x[:, :, c], bank, ALU.add)
    linear(kit, kit.hT, 4, False, add, on_dve=True)



def plan_weights(W, dram):
    W.add(columns(dram["mod_w"][0]))
    W.add(columns(dram["attn_in_w"][0]))
    W.add(columns(dram["attn_out_w"][0]))
    W.add(columns(dram["peer_w_q"][0]))
    W.add(columns(dram["mod_w"][1]))
    W.add([dram["pool_w"].rearrange("e g (k p) n -> p (e g k) n", p=P)])
    W.add(columns(dram["peer_w_q"][1]))
    W.add(ffn_blocks(dram, 0, 0))
    W.add(columns(dram["attn_w_in_2"][0]))
    wo = dram["attn_w_out_2"][0].rearrange("(k p) n -> p k n", p=P)
    W.add([wo[:, :, 0:512], wo[:, :, 512:1024]])
    W.add(ffn_blocks(dram, 0, 1))
    W.add(ffn_blocks(dram, 1, 0))
    for n in ("rw_wr_2", "rw_wk_2", "rw_wv_2"):
        W.add(columns(dram[n][0]))
    W.add(columns(dram["rw_wo_2"][0]))
    W.add(ffn_blocks(dram, 1, 1))


def build(nc, dram, out):
    kit = Kit(nc, dram)
    kit.x = nc.alloc_sbuf_tensor("x_res", [P, NT, D], F32)
    kit.h = nc.alloc_sbuf_tensor("h", [P, NT, D], F32)
    kit.hT = nc.alloc_sbuf_tensor("hT", [P, KD, SEQ], F32)
    kit.ones = nc.alloc_sbuf_tensor("ones", [P, P], F32)
    kit.zeros = nc.alloc_sbuf_tensor("zeros", [1, 512], F32)
    kit.eps = nc.alloc_sbuf_tensor("eps", [P, 1], F32)[:]
    kit.spare = nc.alloc_sbuf_tensor("spare8", [P, GRING], F32)
    kit.consts = nc.alloc_sbuf_tensor("const_table", [P, sum(n for _, n in CONST_PARTS)], F32)
    at = {}
    o = 0
    for name, n in CONST_PARTS:
        at[name] = kit.consts[:, o:o + n]
        if name == "lt":
            kit.ltle = kit.consts[:, o:o + 2 * P]
        o += n
    kit.ident, kit.after, kit.lt, kit.le, kit.ends, kit.iota16 = (at[n] for n in ("ident", "after", "lt", "le", "ends", "iota16"))
    kit.strict = at["strict"].rearrange("p (t n) -> p t n", t=NT)
    kit.window = at["window"].rearrange("p (t n) -> p t n", t=NT)
    kit.cos = at["cos"].rearrange("p (t n) -> p t n", t=NT)
    kit.sin = at["sin"].rearrange("p (t n) -> p t n", t=NT)
    kit.weights = Weights(kit)
    plan_weights(kit.weights, dram)

    load_constants(kit, dram)
    with kit.sb("mod", [P, N_MOD * D]) as mod:
        with kit.sb("mod_ctx", [P, 2 * D]) as mod_ctx:
            modulation(kit, dram, 0, mod, mod_ctx)
            mixer(kit, dram, mod, mod_ctx)
        peer(kit, dram, 0, mod, True)
        pooling(kit, dram, mod)
        peer(kit, dram, 1, mod, False)
    norm_plain(kit, kit.x, dram["final_g"].rearrange("(a d) -> a d", a=1), kit.x)
    swiglu(kit, dram, 0, 0)
    parallel_attention(kit, dram)
    swiglu(kit, dram, 0, 1)
    swiglu(kit, dram, 1, 0)
    time_mix(kit, dram)
    swiglu(kit, dram, 1, 1)
    stored = kit.count("stored")
    with nc.Block() as block:
        @block.sync
        def _(sp):
            stored.up(sp.dma_start(out.rearrange("a (t p) d -> p (a t) d", p=P), kit.x[:]), 16)
            sp.wait_ge(stored.sem, 16)


INPUTS = ["x", "c", "ctx", "c_ctx", "mod_w", "mod_b", "norm1_g", "norm2_g", "attn_in_w", "attn_out_w", "attn_sink",
          "gmlp_w_s", "gmlp_b_s", "pool_w", "pool_scale", "peer_w_q", "peer_sub_keys", "peer_down", "peer_up", "final_g",
          "ffn_norm_2", "ffn_w_gate_2", "ffn_w_up_2", "ffn_w_down_2", "mix_norm_2", "rel_bias_2", "attn_w_in_2",
          "attn_q_norm_2", "attn_k_norm_2", "attn_w_out_2", "rw_mix_2", "rw_w0_2", "rw_w1_2", "rw_w2_2", "rw_a0_2",
          "rw_a1_2", "rw_a2_2", "rw_g1_2", "rw_g2_2", "rw_kk_2", "rw_ka_2", "rw_rk_2", "rw_wr_2", "rw_wk_2", "rw_wv_2",
          "rw_wo_2", "rw_lnx_g_2", "rw_lnx_b_2"]


def kernel(**inputs):
    import numpy as _np
    import concourse.bacc as _bacc
    from concourse.bass_utils import run_bass_kernel_spmd as _run

    nc = _bacc.Bacc("TRN2", target_bir_lowering=False, num_devices=1)
    arrays, dram = {}, {}
    for name in INPUTS:
        a = _np.ascontiguousarray(inputs[name])
        arrays[f"in_{name}"] = a
        dram[name] = nc.dram_tensor(f"in_{name}", a.shape, mybir.dt.from_np(a.dtype), kind="ExternalInput").ap()
    for name, a in layout_constants().items():
        arrays[f"in_{name}"] = a
        dram[name] = nc.dram_tensor(f"in_{name}", a.shape, F32, kind="ExternalInput").ap()
    for name, shape in (("bias_scratch", (DIL_HEADS, 512)), ("systems", (P, C * C)), ("inverses", (P, C * C))):
        dram[name] = nc.dram_tensor(name, shape, F32, kind="Internal").ap()
    out = nc.dram_tensor("out_0", (1, SEQ, D), F32, kind="ExternalOutput").ap()
    build(nc, dram, out)
    r = _run(nc, [arrays], core_ids=[0])
    return r.results[0]["out_0"]
```

```python
from contextlib import contextmanager

import numpy as np
import concourse.bass as bass
from concourse import mybir

F32 = mybir.dt.float32
U32 = mybir.dt.uint32
F32R = mybir.dt.float32r
ALU = mybir.AluOpType
ACT = mybir.ActivationFunctionType
AX = mybir.AxisListType.X

P = 128
SEQ = 256
NT = SEQ // P
D = 1024
KD = D // P
EPS = 1e-6
GN_EPS = 64e-5
NEG = -1e30
HD = 64
SCALE = HD ** -0.5

N_MOD = 6
Q_W, KV_W, A_W = 512, 128, 512
HEADS, GQA = 8, 4
GROUPS = 8
POOL_WINDOWS = (2, 4, 8, 16)

PH = 8
NKEYS = 128
TOPK = 16
PICKS = PH * TOPK

D_FF = 2816
BLK = 256
FF_BLOCKS = D_FF // BLK

SB_HEADS, DIL_HEADS, DIL_GROUPS, GROUP_HEADS = 4, 12, 3, 4
DIL_PATTERNS = ((128, 1), (512, 4), (2048, 16))
N_BUCKETS, MAX_DISTANCE = 32, 2048

RH = 16
C = 32
CH = P // C

SLOTS = 6
SPLIT_SLOTS = 3
GRING = 8
PE_ROWS = 32

CONST_PARTS = [("ident", P), ("after", P), ("lt", P), ("le", P), ("ends", CH), ("iota16", 16),
               ("strict", NT * SEQ), ("window", NT * 512), ("cos", NT * HD), ("sin", NT * HD)]


def layout_constants():
    t = np.arange(SEQ)
    pi = np.arange(P)
    same = (pi[:, None] // C) == (pi[None, :] // C)
    quarter = HD // 4
    inv = np.power(np.float32(10000.0), -np.arange(quarter, dtype=np.float32) / np.float32(quarter))
    row, col = (t // 64).astype(np.float32), (t % 64).astype(np.float32)
    ar, ac = row[:, None] * inv[None, :], col[:, None] * inv[None, :]
    cos = np.concatenate([np.cos(ar), np.cos(ar), np.cos(ac), np.cos(ac)], 1)
    sin = np.concatenate([-np.sin(ar), np.sin(ar), -np.sin(ac), np.sin(ac)], 1)
    window = np.zeros((SEQ, 512), np.float32)
    window[:, :SEQ] = np.where(np.abs(t[:, None] - t[None, :]) <= 128, 0.0, NEG)

    def tiles(a):
        return a.reshape(NT, P, -1).transpose(1, 0, 2).reshape(P, -1)

    parts = {
        "ident": np.eye(P), "after": (pi[:, None] > pi[None, :]),
        "lt": same & (pi[:, None] < pi[None, :]), "le": same & (pi[:, None] <= pi[None, :]),
        "ends": (pi[:, None] // C) == np.arange(CH)[None, :],
        "iota16": np.broadcast_to(np.arange(16), (P, 16)),
        "strict": tiles((t[:, None] < t[None, :]).astype(np.float32)),
        "window": tiles(window), "cos": tiles(cos), "sin": tiles(sin),
    }
    consts = np.concatenate([np.asarray(parts[n], np.float32) for n, _ in CONST_PARTS], 1)
    bands = np.zeros((len(POOL_WINDOWS), SEQ, SEQ), np.float32)
    for g, w in enumerate(POOL_WINDOWS):
        lo, hi = np.clip(t - w // 2, 0, SEQ), np.clip(t + w // 2, 0, SEQ)
        inside = (t[:, None] >= lo[None, :]) & (t[:, None] < hi[None, :])
        bands[g] = inside / (hi - lo).astype(np.float32)[None, :] - np.eye(SEQ)
    dist = np.arange(512) - (SEQ - 1)
    half = N_BUCKETS // 2
    large = half + (np.log(np.maximum(dist, 1).astype(np.float32) / half) / np.log(MAX_DISTANCE / half)
                    * (N_BUCKETS - half)).astype(np.int32)
    bucket = np.where(dist < half, dist, np.minimum(large, N_BUCKETS - 1))
    onehot = np.zeros((N_BUCKETS + 1, DIL_GROUPS, 512), np.float32)
    for g, (w, r) in enumerate(DIL_PATTERNS):
        ok = (dist >= 0) & (dist % r == 0) & (dist <= w)
        for j in range(512):
            if ok[j]:
                onehot[bucket[j], g, j] = 1.0 / SCALE
            else:
                onehot[N_BUCKETS, g, j] = 1.0
    return {"consts": np.ascontiguousarray(consts), "bands": bands, "onehot": onehot}


class Count:

    def __init__(self, nc, name):
        self.sem, self.n = nc.alloc_semaphore(name), 0

    def up(self, ins, by=1):
        ins.then_inc(self.sem, by)
        self.n += by
        return self.n


class Kit:

    def __init__(self, nc, dram):
        self.nc, self.dram, self.counts, self.taken = nc, dram, {}, 0
        self.bank = [nc.alloc_psum_tensor(f"bank{i}", [P, 512], F32) for i in range(8)]
        self.step = {e: Count(nc, f"{e}_step") for e in ("dve", "act", "pool")}

    def count(self, name):
        if name not in self.counts:
            self.counts[name] = Count(self.nc, name)
        return self.counts[name]

    def sb(self, name, shape, dt=F32):
        self.taken += 1
        return self.nc.sbuf_tensor(f"{name}_{self.taken}", shape, dt)

    def dve(self, ins):
        self.nc.vector.wait_ge(self.step["dve"].sem, self.step["dve"].up(ins))

    def act(self, ins):
        self.nc.scalar.wait_ge(self.step["act"].sem, self.step["act"].up(ins))

    def roots(self, act, jobs):
        ready, made = self.count("variance_ready"), self.count("root_made")
        for i, (dst, src) in enumerate(jobs):
            act.wait_ge(ready.sem, made.n + 1)
            made.up(self.nc.scalar.activation(dst, src, ACT.Sqrt))

    def rsqrt(self, dve, ins, dst, src):
        n = self.count("variance_ready").up(ins)
        dve.wait_ge(self.count("root_made").sem, n)
        self.dve(self.nc.vector.reciprocal(dst, src))

    def load(self, eng, dst, src, slow=False):
        self.count("loaded").up(eng.dma_start(dst, src, allow_slow_non_contiguous=slow), 16)


class Weights:

    def __init__(self, kit):
        nc = kit.nc
        self.ring = nc.alloc_sbuf_tensor("weight_ring", [P, SLOTS, 2048], F32)
        self.landed = [nc.alloc_semaphore(f"block_landed{i}") for i in range(SLOTS)]
        self.multiplied = nc.alloc_semaphore("block_multiplied")
        self.blocks, self.issued, self.used = [], 0, 0

    def add(self, srcs):
        self.blocks += srcs

    def tile(self, b, kc):
        return self.ring[:, b % SLOTS, :].rearrange("p (k n) -> p k n", k=kc)

    def issue(self, sp, upto):
        for b in range(self.issued, min(upto, len(self.blocks))):
            if b >= SLOTS:
                sp.wait_ge(self.multiplied, b - SLOTS + 1)
            src = self.blocks[b]
            sp.dma_start(self.tile(b, src.shape[1]), src).then_inc(self.landed[b % SLOTS], 16)
        self.issued = max(self.issued, min(upto, len(self.blocks)))

    def wait(self, pe, b):
        pe.wait_ge(self.landed[b % SLOTS], 16 * (b // SLOTS + 1))


def bcast(row, n):
    return row.partition_broadcast(P).rearrange("p a n -> p (a n)")


def columns(w):
    v = w.rearrange("(k p) n -> p k n", p=P)
    return [v[:, :, b * BLK:(b + 1) * BLK] for b in range(w.shape[1] // BLK)]



def transposes(kit, jobs):
    nc = kit.nc
    turned, freed = kit.count("turned"), [kit.count("turned_out_act"), kit.count("turned_out_dve")]
    b0, f0 = turned.n, [f.n for f in freed]
    with nc.Block() as block:
        @block.tensor
        def _(pe):
            for j, (ins, _) in enumerate(jobs):
                if j >= 4:
                    pe.wait_ge(freed[j % 2].sem, f0[j % 2] + (j - 4) // 2 + 1)
                n = ins[0].shape[0]
                for i, a in enumerate(ins):
                    mm = nc.tensor.transpose(kit.bank[j % 4][:, i * n:(i + 1) * n], a, kit.ident[0:n, 0:n])
                turned.up(mm)

        def source(j):
            n, t = len(jobs[j][0]), jobs[j][0][0].shape[0]
            return kit.bank[j % 4][:, 0:n * t].rearrange("p (n t) -> p n t", n=n)

        @block.scalar
        def _(act):
            for j in range(0, len(jobs), 2):
                act.wait_ge(turned.sem, b0 + j + 1)
                freed[0].up(nc.scalar.copy(jobs[j][1], source(j)))

        @block.vector
        def _(dve):
            for j in range(1, len(jobs), 2):
                dve.wait_ge(turned.sem, b0 + j + 1)
                freed[1].up(nc.vector.tensor_copy(jobs[j][1], source(j)))



def transposes_split(kit, jobs):
    nc = kit.nc
    turned, high, freed = kit.count("turned"), kit.count("turned_high"), kit.count("turned_out_dve")
    b0, h0, f0 = turned.n, high.n, freed.n
    with nc.Block() as block:
        @block.tensor
        def _(pe):
            for j, (ins, _, _) in enumerate(jobs):
                if j >= 4:
                    pe.wait_ge(freed.sem, f0 + j - 3)
                n = ins[0].shape[0]
                for i, a in enumerate(ins):
                    mm = nc.tensor.transpose(kit.bank[j % 4][:, i * n:(i + 1) * n], a, kit.ident[0:n, 0:n])
                turned.up(mm)

        def source(j):
            n, t = len(jobs[j][0]), jobs[j][0][0].shape[0]
            return kit.bank[j % 4][:, 0:n * t].rearrange("p (n t) -> p n t", n=n)

        @block.scalar
        def _(act):
            for j in range(len(jobs)):
                act.wait_ge(turned.sem, b0 + j + 1)
                high.up(nc.scalar.copy(jobs[j][1], source(j)))

        @block.vector
        def _(dve):
            for j in range(len(jobs)):
                dve.wait_ge(high.sem, h0 + j + 1)
                freed.up(nc.vector.tensor_tensor(jobs[j][2], source(j), jobs[j][1].bitcast(F32), ALU.subtract))


def transpose_tokens_split(kit, src, hi, lo, kc=KD):
    jobs = []
    for T in range(NT):
        for k in range(0, kc, 4):
            jobs.append(([src[:, T, (k + i) * P:(k + i + 1) * P] for i in range(4)],
                         hi[:, k:k + 4, T * P:(T + 1) * P], lo[:, k:k + 4, T * P:(T + 1) * P]))
    transposes_split(kit, jobs)


def transpose_tokens(kit, src, dstT, kc=KD):
    jobs = []
    for T in range(NT):
        for k in range(0, kc, 4):
            jobs.append(([src[:, T, (k + i) * P:(k + i + 1) * P] for i in range(4)],
                         dstT[:, k:k + 4, T * P:(T + 1) * P]))
    transposes(kit, jobs)


def norm(kit, x, gain, shift, out, load=()):
    nc = kit.nc
    squares, loaded = kit.count("squares_summed"), kit.count("loaded")
    s0, l0 = squares.n, loaded.n
    with kit.sb("ss", [P, 8]) as ss, kit.sb("junk", [P, D]) as junk, nc.Block() as block:
        @block.sync
        def _(sp):
            for dst, src in load:
                kit.load(sp, dst, src)

        @block.scalar
        def _(act):
            for T in range(NT):
                kit.act(nc.scalar.activation(junk[:], x[:, T], ACT.Square, accum_out=ss[:, T:T + 1]))
            squares.up(nc.scalar.activation(ss[:, 4:4 + NT], ss[:, 0:NT], ACT.Sqrt, scale=1.0 / D, bias=kit.eps))

        @block.vector
        def _(dve):
            dve.wait_ge(squares.sem, s0 + 1)
            if load:
                dve.wait_ge(loaded.sem, l0 + 16 * len(load))
            kit.dve(nc.vector.reciprocal(ss[:, 6:6 + NT], ss[:, 4:4 + NT]))
            for T in range(NT):
                ins = nc.vector.scalar_tensor_tensor(out=out[:, T], in0=x[:, T], scalar=ss[:, 6 + T:7 + T],
                                                     in1=gain, op0=ALU.mult, op1=ALU.mult)
                if shift is not None:
                    kit.dve(ins)
                    nc.vector.tensor_tensor(out[:, T], out[:, T], shift, ALU.add)


def norm_modulated(kit, x, g_row, scale, shift, out):
    nc = kit.nc
    loaded = kit.count("loaded")
    l0 = loaded.n
    with kit.sb("gain", [P, D]) as gain:
        with nc.Block() as block:
            @block.sync
            def _(sp):
                kit.load(sp, gain[:], bcast(g_row, D))

            @block.vector
            def _(dve):
                dve.wait_ge(loaded.sem, l0 + 16)
                nc.vector.scalar_tensor_tensor(out=gain[:], in0=scale, scalar=1.0, in1=gain[:],
                                               op0=ALU.add, op1=ALU.mult)
        norm(kit, x, gain[:], shift, out)


def norm_plain(kit, x, g_row, out):
    with kit.sb("gain", [P, D]) as gain:
        norm(kit, x, gain[:], None, out, load=[(gain[:], bcast(g_row, D))])


def norm_split(kit, x, g_row, scale, shift, out, hi, lo):
    nc = kit.nc
    loaded, squares, normed, turned, high, low = (kit.count(n) for n in (
        "loaded", "squares_summed", "tile_normed", "turned", "turned_high", "turned_out_dve"))
    l0, s0, n0, t0, h0 = loaded.n, squares.n, normed.n, turned.n, high.n
    jobs = [(T, k) for T in range(NT) for k in (0, 4)]
    place = lambda a, T, k: a[:, k:k + 4, T * P:(T + 1) * P]
    bank = lambda j: kit.bank[j][:, :].rearrange("p (n t) -> p n t", n=4)
    with kit.sb("gain", [P, D]) as gain, kit.sb("ss", [P, 3, NT]) as ss, kit.sb("junk", [P, D]) as junk, nc.Block() as block:
        @block.sync
        def _(sp):
            kit.load(sp, gain[:], bcast(g_row, D))

        @block.scalar
        def _(act):
            for T in range(NT):
                kit.act(nc.scalar.activation(junk[:], x[:, T], ACT.Square, accum_out=ss[:, 0, T:T + 1]))
                squares.up(nc.scalar.activation(ss[:, 1, T:T + 1], ss[:, 0, T:T + 1], ACT.Sqrt, scale=1.0 / D, bias=kit.eps))
            for j, (T, k) in enumerate(jobs):
                act.wait_ge(turned.sem, t0 + j + 1)
                high.up(nc.scalar.copy(place(hi, T, k), bank(j)))

        @block.vector
        def _(dve):
            dve.wait_ge(loaded.sem, l0 + 16)
            if scale is not None:
                kit.dve(nc.vector.scalar_tensor_tensor(out=gain[:], in0=scale, scalar=1.0, in1=gain[:],
                                                       op0=ALU.add, op1=ALU.mult))
            for T in range(NT):
                dve.wait_ge(squares.sem, s0 + T + 1)
                kit.dve(nc.vector.reciprocal(ss[:, 2, T:T + 1], ss[:, 1, T:T + 1]))
                ins = nc.vector.scalar_tensor_tensor(out=out[:, T], in0=x[:, T], scalar=ss[:, 2, T:T + 1],
                                                     in1=gain[:], op0=ALU.mult, op1=ALU.mult)
                if shift is not None:
                    kit.dve(ins)
                    ins = nc.vector.tensor_tensor(out[:, T], out[:, T], shift, ALU.add)
                normed.up(ins)
            for j, (T, k) in enumerate(jobs):
                dve.wait_ge(high.sem, h0 + j + 1)
                low.up(nc.vector.tensor_tensor(place(lo, T, k), bank(j), place(hi, T, k).bitcast(F32), ALU.subtract))

        @block.tensor
        def _(pe):
            for j, (T, k) in enumerate(jobs):
                pe.wait_ge(normed.sem, n0 + T + 1)
                for i in range(4):
                    mm = nc.tensor.transpose(kit.bank[j][:, i * P:(i + 1) * P], out[:, T, (k + i) * P:(k + i + 1) * P],
                                             kit.ident)
                turned.up(mm)


def linear_split(kit, src, nblocks, transposed, evacuate, on_dve=False, slots=2, extra=None, extra_evacuate=None,
                 then=None):
    nc, W = kit.nc, kit.weights
    b0 = W.used
    emptied, extra_done = kit.count("bank_emptied"), kit.count("extra_multiplied")
    high_made, split = kit.count("block_high_made"), kit.count("block_split")
    e0, x0, h0, p0 = emptied.n, extra_done.n, high_made.n, split.n
    with kit.sb("x_high", [P, KD, SEQ], F32R) as x_hi, kit.sb("x_low", [P, KD, SEQ], F32R) as x_lo, \
            kit.sb("high", [P, slots, 2048], F32R) as high, kit.sb("low", [P, slots, 2048], F32R) as low:
        if callable(src):
            src(x_hi, x_lo)
        else:
            transpose_tokens_split(kit, src, x_hi, x_lo)
        with nc.Block() as block:
            @block.sync
            def _(sp):
                W.issue(sp, b0 + nblocks + SLOTS)

            @block.tensor
            def _(pe):
                for b in range(nblocks):
                    pe.wait_ge(split.sem, p0 + b + 1)
                    if b >= 4:
                        pe.wait_ge(emptied.sem, e0 + b - 3)
                    if extra is not None and extra[0] == b:
                        W.wait(pe, b0 + b)
                        for T in range(NT):
                            for k in range(KD):
                                mm = nc.tensor.matmul(kit.bank[4][:, T * BLK:(T + 1) * BLK],
                                                      extra[1][:, k, T * P:(T + 1) * P], W.tile(b0 + b, KD)[:, k, :],
                                                      start=(k == 0), stop=(k == KD - 1))
                        extra_done.up(mm)
                    w_hi, w_lo = (a[:, b % slots, :].rearrange("p (k n) -> p k n", k=KD) for a in (high, low))
                    for half in range(2):
                        o = kit.bank[b % 4][:, half * BLK:(half + 1) * BLK]
                        cols = slice(half * P, (half + 1) * P)
                        for k in range(KD):
                            for n, (w, t) in enumerate([(w_lo, x_hi), (w_hi, x_lo), (w_hi, x_hi)]):
                                kw = dict(start=(k == 0 and n == 0), stop=(k == KD - 1 and n == 2))
                                if transposed:
                                    mm = nc.tensor.matmul(o, w[:, k, cols], t[:, k, :], **kw)
                                else:
                                    mm = nc.tensor.matmul(o, t[:, k, cols], w[:, k, :], **kw)
                    mm.then_inc(W.multiplied, 1)
                    if then and b >= 2:
                        then[0](pe, b - 2, e0)
                if then:
                    for b in range(nblocks - 2, nblocks):
                        then[0](pe, b, e0)

            def make_high(act, b):
                W.wait(act, b0 + b)
                if b >= slots:
                    act.wait_ge(W.multiplied, b0 + b - slots + 1)
                high_made.up(nc.scalar.copy(high[:, b % slots, :], W.ring[:, (b0 + b) % SLOTS, :]))

            def make_low(dve, b):
                dve.wait_ge(high_made.sem, h0 + b + 1)
                split.up(nc.vector.tensor_tensor(low[:, b % slots, :], W.ring[:, (b0 + b) % SLOTS, :],
                                                 high[:, b % slots, :].bitcast(F32), ALU.subtract))

            def empty(eng, b):
                eng.wait_ge(W.multiplied, b0 + b + 1)
                if on_dve and b:
                    eng.wait_ge(emptied.sem, e0 + b)
                emptied.up(evacuate(b, kit.bank[b % 4][:, :].rearrange("p (t n) -> p t n", t=2)))

            @block.scalar
            def _(act):
                for b in range(nblocks + (4 if then else slots)):
                    if b < nblocks:
                        make_high(act, b)
                    if slots <= b < nblocks + slots and not on_dve:
                        empty(act, b - slots)
                    if then and b >= 4:
                        then[1](act, b - 4)
                if extra is not None:
                    act.wait_ge(extra_done.sem, x0 + 1)
                    extra_evacuate(kit.bank[4][:, :].rearrange("p (t n) -> p t n", t=2))

            @block.vector
            def _(dve):
                for b in range(nblocks + (4 if then else slots)):
                    if b < nblocks:
                        make_low(dve, b)
                    if slots <= b < nblocks + slots and on_dve:
                        empty(dve, b - slots)
                    if then and b >= 4:
                        then[2](dve, b - 4)
    W.used += nblocks


def add_gated(kit, x, tmp, gate):
    nc = kit.nc

    def evacuate(b, bank):
        cols = slice(b * BLK, (b + 1) * BLK)
        g = gate[:, cols].unsqueeze(1).to_broadcast([P, NT, BLK])
        kit.dve(nc.vector.tensor_tensor(tmp[:], bank, g, ALU.mult))
        return nc.vector.tensor_tensor(x[:, :, cols], x[:, :, cols], tmp[:], ALU.add)
    return evacuate


def copy_out(kit, dst):
    def evacuate(b, bank):
        return kit.nc.scalar.copy(dst[:, :, b * BLK:(b + 1) * BLK], bank)
    return evacuate



def load_constants(kit, dram):
    nc = kit.nc
    loaded = kit.count("loaded")
    with nc.Block() as block:
        @block.sync
        def _(sp):
            kit.load(sp, kit.consts[:], dram["consts"])
            sp.wait_ge(loaded.sem, 16)

        @block.vector
        def _(dve):
            nc.vector.memset(kit.ones[:], 1.0)
            nc.vector.memset(kit.zeros[:], 0.0)
            nc.vector.memset(kit.eps, EPS)
            for s in range(GRING):
                kit.count("row_slots_freed").up(nc.vector.memset(kit.spare[:, s:s + 1], 0.0))
            dve.wait_ge(kit.count("row_slots_freed").sem, GRING)
            kit.count("dots_copied").up(nc.vector.memset(kit.spare[:, 0:1], 0.0))
            kit.count("hidden_ready").up(nc.vector.memset(kit.spare[:, 1:2], 0.0))


@contextmanager
def modulation_space(kit, vectors):
    with kit.sb("c_rows", [vectors * KD, P]) as rows, kit.sb("cwide", [P, vectors, KD, P]) as cwide, \
            kit.sb("mod_b_row", [1, N_MOD * D]) as brow:
        yield rows, cwide, brow


class Parts:

    def __init__(self, sync, tensor, scalar, vector):
        self.sync, self.tensor, self.scalar, self.vector = sync, tensor, scalar, vector


def modulation(kit, dram, layer, mod, mod_ctx):
    with modulation_space(kit, 2) as space, kit.nc.Block() as block:
        parts = modulation_parts(kit, dram, layer, mod, mod_ctx, space)
        block.sync(parts.sync)
        block.vector(parts.vector)
        block.tensor(parts.tensor)
        block.scalar(parts.scalar)


def modulation_parts(kit, dram, layer, mod, mod_ctx, space):
    nc, W = kit.nc, kit.weights
    b0 = W.used
    nb = N_MOD * D // BLK
    ctx_blocks = 2 * D // BLK if mod_ctx is not None else 0
    peeled = 2 * SLOTS if mod_ctx is not None else 0
    rounds = (nb - peeled) // SLOTS
    names = ("c", "c_ctx") if mod_ctx is not None else ("c",)
    nv, H = len(names), P // 2
    loaded, ready = kit.count("loaded"), kit.count("mod_input_ready")
    emptied, spread = kit.count("mod_emptied"), kit.count("mod_spread")
    l0, r0, e0, p0 = loaded.n, ready.n, emptied.n, spread.n
    rows, cwide, brow = space

    def sync(sp):
        for v, name in enumerate(names):
            src = dram[name] if name == "c" else dram[name].rearrange("(a d) -> a d", a=1)
            kit.load(sp, rows[v * KD:(v + 1) * KD], src.rearrange("a (k p) -> (a k) p", p=P))
        kit.load(sp, brow[:], dram["mod_b"][layer:layer + 1, :])
        W.issue(sp, b0 + max(peeled, SLOTS))
        done = max(peeled, SLOTS)
        n = (nb - done) // SLOTS
        v = dram["mod_w"][layer].rearrange("(k p) n -> p k n", p=P)
        with sp.Fori(0, n) as i:
            for u in range(SLOTS):
                b = b0 + done + u
                sp.wait_ge(W.multiplied, i * SLOTS + (b - SLOTS + 1))
                sp.dma_start(W.tile(b, KD), v[:, :, bass.ds(i * (SLOTS * BLK) + (done + u) * BLK, BLK)]) \
                    .then_inc(W.landed[b % SLOTS], 16)
        W.issued = b0 + nb
        W.issue(sp, b0 + nb + SLOTS)

    def vector(dve):
        dve.wait_ge(ready.sem, r0 + 2)
        c = [kit.bank[7][:, v * KD:(v + 1) * KD].unsqueeze(2) for v in range(nv)]
        nc.vector.tensor_copy(cwide[:, 0], c[0].to_broadcast([P, KD, P])).then_inc(ready.sem, 1)
        for v in range(nv if nv > 1 else 0):
            nc.vector.tensor_copy(cwide[:, 1, :, v * H:(v + 1) * H], c[v].to_broadcast([P, KD, H])).then_inc(ready.sem, 1)

    def tensor(pe):
        pe.wait_ge(ready.sem, r0 + 1)
        nc.tensor.transpose(kit.bank[7][:, 0:nv * KD], rows[:], kit.ident[0:nv * KD, 0:nv * KD]).then_inc(ready.sem, 1)
        pe.wait_ge(ready.sem, r0 + 3 + (2 if nv > 1 else 0))

        def one(u, slot, bias_cols, which=0):
            nc.tensor.matmul(kit.bank[u][:, 0:BLK], kit.ones[0:1, :], brow[0:1, bias_cols], start=True, stop=False)
            for k in range(KD):
                mm = nc.tensor.matmul(kit.bank[u][:, 0:BLK], cwide[:, which, k, :], W.tile(slot, KD)[:, k, :],
                                      start=False, stop=(k == KD - 1))
            return mm

        for b in range(peeled):
            W.wait(pe, b0 + b)
            if b >= SLOTS:
                pe.wait_ge(emptied.sem, e0 + b - SLOTS + 1)
            one(b % SLOTS, b0 + b, slice(b * BLK, (b + 1) * BLK), which=(1 if b < ctx_blocks else 0)) \
                .then_inc(W.multiplied, 1)
        with pe.Fori(0, rounds) as i:
            for u in range(SLOTS):
                b = b0 + peeled + u
                pe.wait_ge(W.landed[b % SLOTS], i * 16 + 16 * (b // SLOTS + 1))
                if peeled:
                    pe.wait_ge(emptied.sem, i * SLOTS + (e0 + peeled + u - SLOTS + 1))
                else:
                    pe.wait_ge(emptied.sem, i * SLOTS + e0)
                one(u, b, bass.ds(i * (SLOTS * BLK) + (peeled + u) * BLK, BLK)).then_inc(W.multiplied, 1)

    def scalar(act):
        act.wait_ge(loaded.sem, l0 + 16 * (nv + 1))
        nc.scalar.activation(rows[:], rows[:], ACT.Silu).then_inc(ready.sem, 1)
        for b in range(peeled):
            cols = slice(b * BLK, (b + 1) * BLK)
            act.wait_ge(W.multiplied, b0 + b + 1)
            if b < ctx_blocks:
                nc.scalar.copy(mod[0:H, cols], kit.bank[b % SLOTS][0:H, 0:BLK])
                nc.scalar.copy(mod_ctx[H:P, cols], kit.bank[b % SLOTS][H:P, 0:BLK]).then_inc(emptied.sem, 1)
            else:
                nc.scalar.copy(mod[:, cols], kit.bank[b % SLOTS][:, 0:BLK]).then_inc(emptied.sem, 1)
            if b == ctx_blocks:
                act.wait_ge(emptied.sem, e0 + ctx_blocks)
                cc = ctx_blocks * BLK
                spread.up(act.dma_start(mod[H:P, 0:cc], mod[0:H, 0:cc]), 16)
                spread.up(act.dma_start(mod_ctx[0:H, 0:cc], mod_ctx[H:P, 0:cc]), 16)
        with act.Fori(0, rounds) as i:
            for u in range(SLOTS):
                act.wait_ge(W.multiplied, i * SLOTS + (b0 + peeled + u + 1))
                nc.scalar.copy(mod[:, bass.ds(i * (SLOTS * BLK) + (peeled + u) * BLK, BLK)],
                               kit.bank[u][:, 0:BLK]).then_inc(emptied.sem, 1)
        if ctx_blocks:
            act.wait_ge(spread.sem, p0 + 32)

    W.used += nb
    emptied.n = e0 + nb
    ready.n = r0 + 3 + (2 if nv > 1 else 0)
    return Parts(sync, tensor, scalar, vector)



def attend(kit, units, PT, cat_bank, probs_of, values_of):
    nc = kit.nc
    turned, copied, mixed = kit.count("probs_turned"), kit.count("probs_copied"), kit.count("values_mixed")
    t0, c0, m0 = turned.n, copied.n, mixed.n
    jobs = []
    for u, chunks in enumerate(units):
        for a in range(0, len(chunks), 4):
            jobs.append((u, a, chunks[a:a + 4], a + 4 >= len(chunks)))

    def pe_side(pe, before_unit):
        def turn(j):
            u, a, cs, last = jobs[j]
            if a == 0:
                before_unit(pe, u)
            if j >= 4:
                pe.wait_ge(copied.sem, c0 + j - 3)
            for i, c in enumerate(cs):
                mm = nc.tensor.transpose(kit.bank[j % 4][:, i * P:(i + 1) * P], probs_of(u, c), kit.ident)
            turned.up(mm)

        def mix(j):
            u, a, cs, last = jobs[j]
            pe.wait_ge(copied.sem, c0 + j + 1)
            for i, c in enumerate(cs):
                mm = nc.tensor.matmul(cat_bank(u), PT[:, j % 4, i, :], values_of(u, c),
                                      start=(a == 0 and i == 0), stop=(last and i == len(cs) - 1))
            mixed.up(mm)

        for j in range(len(jobs)):
            turn(j)
            if j >= 2:
                mix(j - 2)
        for j in range(max(0, len(jobs) - 2), len(jobs)):
            mix(j)

    def act_side(act):
        for j, (u, a, cs, last) in enumerate(jobs):
            act.wait_ge(turned.sem, t0 + j + 1)
            if j >= 4:
                act.wait_ge(mixed.sem, m0 + j - 3)
            copied.up(nc.scalar.copy(PT[:, j % 4, 0:len(cs), :], kit.bank[j % 4][:, 0:len(cs) * P].rearrange(
                "p (n t) -> p n t", n=len(cs))))

    return pe_side, act_side, m0 + len(jobs)


def window_attention(kit, dram, proj, kvc, cat, gmlp_parts, load):
    nc = kit.nc
    nqk = (Q_W + KV_W) // HD
    loaded = kit.count("loaded")
    l0 = loaded.n
    gelu, norm_values, root = gmlp_parts
    with kit.sb("qT", [P, GQA, SEQ]) as qT, kit.sb("kT", [P, 2 * SEQ]) as kT, kit.sb("sink", [P, HEADS]) as sink:
        with kit.sb("rot", [P, NT, nqk * HD]) as rot, kit.sb("rot2", [P, NT, nqk * HD]) as rot2, \
                kit.sb("turned", [P, NT, nqk * HD]) as turned:
            with nc.Block() as block:
                @block.sync
                def _(sp):
                    kit.load(sp, sink[:], bcast(dram["attn_sink"], HEADS))
                    for dst, src in load:
                        kit.load(sp, dst, src, slow=True)

                @block.vector
                def _(dve):
                    for T in range(NT):
                        x = proj[:, T, 0:nqk * HD]
                        cos = kit.cos[:, T].unsqueeze(1).to_broadcast([P, nqk, HD])
                        nc.vector.tensor_tensor(rot[:, T].rearrange("p (h d) -> p h d", d=HD),
                                                x.rearrange("p (h d) -> p h d", d=HD), cos, ALU.mult)
                        xs = x.rearrange("p (h f s c) -> p h f s c", f=2, s=2, c=16)
                        o = rot2[:, T].rearrange("p (h f s c) -> p h f s c", f=2, s=2, c=16)
                        sn = kit.sin[:, T].rearrange("p (f s c) -> p f s c", f=2, s=2)
                        for s in range(2):
                            ins = nc.vector.tensor_tensor(o[:, :, :, s], xs[:, :, :, 1 - s],
                                                          sn[:, :, s].unsqueeze(1).to_broadcast([P, nqk, 2, 16]),
                                                          ALU.mult)
                        kit.dve(ins)
                        by_chunk = lambda a: a[:, T, 0:Q_W].rearrange("p (v c d) -> p c v d", v=2, d=HD)
                        nc.vector.tensor_tensor(turned[:, T, 0:Q_W].rearrange("p (c v d) -> p c v d", v=2, d=HD),
                                                by_chunk(rot), by_chunk(rot2), ALU.add)
                        nc.vector.tensor_tensor(turned[:, T, Q_W:], rot[:, T, Q_W:], rot2[:, T, Q_W:], ALU.add)
            jobs = []
            for T in range(NT):
                jobs.append(([turned[:, T, c * P:(c + 1) * P] for c in range(GQA)], qT[:, :, T * P:(T + 1) * P]))
            jobs.append(([turned[:, T, Q_W:Q_W + KV_W] for T in range(NT)] + [kvc[:, T, 0:KV_W] for T in range(NT)],
                         kT[:].rearrange("p (n t) -> p n t", t=P)))
            transposes(kit, jobs)

        units = [(T, h) for T in range(NT) for h in range(HEADS)]
        nu = len(units)
        with kit.sb("probs", [P, nu, 512]) as probs, kit.sb("PT", [P, 4, 4, P]) as PT, \
                kit.sb("rows", [P, 8, nu]) as rows:
            scored, masked = kit.count("scored"), kit.count("score_masked")
            s0, k0 = scored.n, masked.n
            negmax, exped, normed = kit.count("negmax_ready"), kit.count("exped"), kit.count("denominators")
            n0, x0, d0 = negmax.n, exped.n, normed.n
            cat_bank = lambda u: kit.bank[4 + u // HEADS][:, (u % HEADS) * HD:(u % HEADS + 1) * HD]
            values = lambda u, c: (proj[:, c, Q_W + KV_W:][:, (u % HEADS) // GQA * HD:((u % HEADS) // GQA + 1) * HD]
                                   if c < NT else
                                   kvc[:, c - NT, KV_W + (u % HEADS) // GQA * HD:KV_W + ((u % HEADS) // GQA + 1) * HD])
            pe_side, act_side, m_end = attend(kit, [range(4)] * nu, PT, cat_bank,
                                              lambda u, c: probs[:, u, c * P:(c + 1) * P], values)
            mixed = kit.count("values_mixed")
            with nc.Block() as block:
                @block.sync
                def _(sp):
                    sp.wait_ge(loaded.sem, l0 + 16 * (1 + len(load)))

                @block.tensor
                def _(pe):
                    for u, (T, h) in enumerate(units):
                        if u >= 4:
                            pe.wait_ge(masked.sem, k0 + u - 3)
                        v, c = h // GQA, h % GQA
                        scored.up(nc.tensor.matmul(kit.bank[u % 4][:, :], qT[v * HD:(v + 1) * HD, c, T * P:(T + 1) * P],
                                                   kT[v * HD:(v + 1) * HD, :], start=True, stop=True))
                    pe.wait_ge(masked.sem, k0 + nu)
                    pe_side(pe, lambda pe, u: pe.wait_ge(exped.sem, x0 + u + 1))

                @block.vector
                def _(dve):
                    for u, (T, h) in enumerate(units):
                        dve.wait_ge(scored.sem, s0 + u + 1)
                        masked.up(nc.vector.tensor_tensor_reduce(
                            out=probs[:, u], in0=kit.bank[u % 4][:, :], in1=kit.window[:, T], scale=SCALE,
                            scalar=NEG, op0=ALU.add, op1=ALU.max, accum_out=rows[:, 0, u:u + 1]))
                    dve.wait_ge(masked.sem, k0 + nu)
                    dve.wait_ge(loaded.sem, l0 + 16 * (1 + len(load)))
                    sk = sink[:].unsqueeze(1).to_broadcast([P, NT, HEADS])
                    r = lambda i: rows[:, i].rearrange("p (t h) -> p t h", t=NT)
                    kit.dve(nc.vector.tensor_tensor(r(1), r(0), sk, ALU.max))
                    nc.vector.tensor_tensor(r(3), sk, r(1), ALU.subtract).then_inc(negmax.sem, 1)
                    nc.vector.tensor_scalar(rows[:, 2], rows[:, 1], -1.0, None, ALU.mult).then_inc(negmax.sem, 1)
                    negmax.n += 2
                    norm_values(dve)
                    dve.wait_ge(exped.sem, x0 + nu + 1)
                    kit.dve(nc.vector.tensor_tensor(rows[:, 6], rows[:, 5], rows[:, 4], ALU.add))
                    kit.dve(nc.vector.reciprocal(rows[:, 7], rows[:, 6]))
                    dve.wait_ge(mixed.sem, m_end)
                    for T in range(NT):
                        nc.vector.tensor_tensor(
                            cat[:, T, 0:Q_W].rearrange("p (h d) -> p h d", d=HD),
                            kit.bank[4 + T][:, :].rearrange("p (h d) -> p h d", d=HD),
                            rows[:, 7, T * HEADS:(T + 1) * HEADS].unsqueeze(2).to_broadcast([P, HEADS, HD]), ALU.mult)

                @block.scalar
                def _(act):
                    gelu(act)
                    act.wait_ge(negmax.sem, n0 + 2)
                    for u in range(nu):
                        exped.up(nc.scalar.activation(probs[:, u], probs[:, u], ACT.Exp, bias=rows[:, 2, u:u + 1],
                                                      accum_out=rows[:, 4, u:u + 1]))
                    exped.up(nc.scalar.activation(rows[:, 5], rows[:, 3], ACT.Exp))
                    root(act)
                    act_side(act)


def mix_branches(kit, dram, proj, kvc, cat):
    nc = kit.nc
    u0 = Q_W + 2 * KV_W
    gelued = kit.count("gelued")
    g0 = gelued.n
    with kit.sb("ws", [P, GROUPS, P]) as ws, kit.sb("wsT", [P, GROUPS, P]) as wsT, kit.sb("bs", [P, GROUPS]) as bs:
        with kit.sb("stat", [P, 4, NT * GROUPS]) as stat, kit.sb("sq", [P, NT, A_W]) as sq:
            def gelu(act):
                gelued.up(nc.scalar.activation(proj[:, :, u0:u0 + 2 * A_W], proj[:, :, u0:u0 + 2 * A_W],
                                               ACT.Gelu_apprx_tanh))

            def norm_values(dve):
                dve.wait_ge(gelued.sem, g0 + 1)
                v = proj[:, :, u0 + A_W:u0 + 2 * A_W].rearrange("p t (g d) -> p t g d", d=HD)
                s = sq[:].rearrange("p t (g d) -> p t g d", d=HD)
                st = lambda i: stat[:, i].rearrange("p (t g) -> p t g", t=NT)
                wide = lambda i, T: st(i)[:, T].unsqueeze(2).to_broadcast([P, GROUPS, HD])
                kit.dve(nc.vector.tensor_reduce(st(0), v, AX, ALU.add))
                kit.dve(nc.vector.tensor_scalar(stat[:, 0], stat[:, 0], 1.0 / HD, None, ALU.mult))
                for T in range(NT):
                    ins = nc.vector.tensor_tensor(v[:, T], v[:, T], wide(0, T), ALU.subtract)
                kit.dve(ins)
                kit.dve(nc.vector.tensor_tensor(s, v, v, ALU.mult))
                kit.dve(nc.vector.tensor_reduce(st(1), s, AX, ALU.add))
                kit.rsqrt(dve, nc.vector.tensor_scalar(stat[:, 2], stat[:, 1], 1.0 / HD, EPS, ALU.mult, ALU.add),
                          stat[:, 3], stat[:, 3])
                for T in range(NT):
                    nc.vector.tensor_tensor(v[:, T], v[:, T], wide(3, T), ALU.mult)

            window_attention(kit, dram, proj, kvc, cat, (gelu, norm_values, lambda act: kit.roots(
                act, [(stat[:, 3], stat[:, 2])])), [(ws[:], dram["gmlp_w_s"].rearrange("e g p q -> p (e g) q")),
                                                    (bs[:], dram["gmlp_b_s"].rearrange("e g p -> p (e g)"))])
        transposes(kit, [([ws[:, g + i, :] for i in range(4)], wsT[:, g:g + 4, :]) for g in (0, 4)])
        spread = kit.count("tokens_mixed")
        s0 = spread.n
        with nc.Block() as block:
            @block.tensor
            def _(pe):
                for g in range(GROUPS):
                    spread.up(nc.tensor.matmul(kit.bank[g // 4][:, g % 4 * P:(g % 4 + 1) * P], wsT[:, g, :],
                                               proj[:, :, u0 + A_W + g * HD:u0 + A_W + (g + 1) * HD],
                                               start=True, stop=True))

            @block.vector
            def _(dve):
                dve.wait_ge(spread.sem, s0 + GROUPS)
                for g in range(GROUPS):
                    nc.vector.scalar_tensor_tensor(
                        out=cat[:, :, Q_W + g * HD:Q_W + (g + 1) * HD],
                        in0=kit.bank[g // 4][:, g % 4 * P:(g % 4 + 1) * P].rearrange("p (t d) -> p t d", t=NT),
                        scalar=bs[:, g:g + 1], in1=proj[:, :, u0 + g * HD:u0 + (g + 1) * HD],
                        op0=ALU.add, op1=ALU.mult)


def mixer(kit, dram, mod, mod_ctx):
    x, h = kit.x, kit.h
    nc = kit.nc
    with kit.sb("cat", [P, NT, D]) as cat:
        with kit.sb("proj", [P, NT, Q_W + 2 * KV_W + 2 * A_W]) as proj, kit.sb("kvc", [P, NT, 2 * KV_W]) as kvc:
            with kit.sb("hcT", [P, KD, SEQ]) as hcT:
                with kit.sb("xc", [P, NT, D]) as xc:
                    loaded = kit.count("loaded")
                    l0 = loaded.n
                    with nc.Block() as block:
                        @block.sync
                        def _(sp):
                            kit.load(sp, xc[:], dram["ctx"].rearrange("a (t p) d -> p (a t) d", p=P))
                            kit.load(sp, x[:], dram["x"].rearrange("a (t p) d -> p (a t) d", p=P))
                            sp.wait_ge(loaded.sem, l0 + 32)
                    norm_modulated(kit, xc, dram["norm1_g"][0:1, :], mod_ctx[:, D:2 * D], mod_ctx[:, 0:D], h)
                transpose_tokens(kit, h, hcT)
                linear_split(kit, lambda hi, lo: norm_split(kit, x, dram["norm1_g"][0:1, :], mod[:, D:2 * D],
                                                            mod[:, 0:D], h, hi, lo), 7, False, copy_out(kit, proj), extra=(Q_W // BLK, hcT),
                             extra_evacuate=lambda bank: nc.scalar.copy(kvc[:], bank))
            mix_branches(kit, dram, proj, kvc, cat)
        with kit.sb("tmp", [P, NT, BLK]) as tmp:
            linear_split(kit, cat, 4, False, add_gated(kit, x, tmp, mod[:, 2 * D:3 * D]), on_dve=True)


def pooling(kit, dram, mod):
    nc, W = kit.nc, kit.weights
    x, h = kit.x, kit.h
    norm_modulated(kit, x, dram["norm1_g"][1:2, :], mod[:, D:2 * D], mod[:, 0:D], h)
    b0 = W.used
    loaded, pooled, copied, done = kit.count("loaded"), kit.count("pooled"), kit.count("pooled_copied"), kit.count("pool_projected")
    l0, p0, c0, d0 = loaded.n, pooled.n, copied.n, done.n
    G = len(POOL_WINDOWS)
    with kit.sb("bands", [P, G, NT, SEQ]) as bands, kit.sb("pooledT", [P, KD, SEQ]) as pT, \
            kit.sb("gs", [P, D]) as gs, kit.sb("tmp", [P, D]) as tmp, nc.Block() as block:
        @block.sync
        def _(sp):
            kit.load(sp, bands[:], dram["bands"].rearrange("g (t p) n -> p g t n", p=P))
            kit.load(sp, gs[:], bcast(dram["pool_scale"], D))
            W.issue(sp, b0 + 1 + SLOTS)

        @block.tensor
        def _(pe):
            pe.wait_ge(loaded.sem, l0 + 32)
            for k in range(KD):
                for t in range(NT):
                    mm = nc.tensor.matmul(kit.bank[k // 2][:, k % 2 * SEQ:(k % 2 + 1) * SEQ], h[:, t, k * P:(k + 1) * P],
                                          bands[:, k // 2, t, :], start=(t == 0), stop=(t == NT - 1))
                pooled.up(mm)
            W.wait(pe, b0)
            w = W.tile(b0, KD)
            for T in range(NT):
                for g in range(G):
                    pe.wait_ge(copied.sem, c0 + g + 1)
                    for cc in range(2):
                        mm = nc.tensor.matmul(kit.bank[4 + 2 * T + g // 2][:, g % 2 * BLK:(g % 2 + 1) * BLK],
                                              pT[:, 2 * g + cc, T * P:(T + 1) * P], w[:, 2 * g + cc, :],
                                              start=(cc == 0), stop=(cc == 1))
                if T == NT - 1:
                    mm.then_inc(W.multiplied, 1)
                else:
                    done.up(mm)

        @block.scalar
        def _(act):
            for g in range(G):
                act.wait_ge(pooled.sem, p0 + 2 * g + 2)
                copied.up(nc.scalar.copy(pT[:, 2 * g:2 * g + 2, :], kit.bank[g][:, :].rearrange("p (a n) -> p a n", a=2)))

        @block.vector
        def _(dve):
            dve.wait_ge(loaded.sem, l0 + 32)
            kit.dve(nc.vector.tensor_tensor(gs[:], gs[:], mod[:, 2 * D:3 * D], ALU.mult))
            for T in range(NT):
                if T == NT - 1:
                    dve.wait_ge(W.multiplied, b0 + 1)
                else:
                    dve.wait_ge(done.sem, d0 + 1)
                for i in range(2):
                    kit.dve(nc.vector.tensor_tensor(tmp[:, i * 512:(i + 1) * 512], kit.bank[4 + 2 * T + i][:, :],
                                                    gs[:, i * 512:(i + 1) * 512], ALU.mult))
                kit.dve(nc.vector.tensor_tensor(x[:, T], x[:, T], tmp[:], ALU.add))
    W.used += 1



def peer(kit, dram, layer, mod, next_modulation):
    nc = kit.nc
    x, h = kit.x, kit.h
    fill = lambda hi, lo: norm_split(kit, x, dram["norm2_g"][layer:layer + 1, :], mod[:, 4 * D:5 * D],
                                     mod[:, 3 * D:4 * D], h, hi, lo)
    with kit.sb("scores", [P, NT, 2 * PH, NKEYS]) as scores, kit.sb("top", [P, PH, 2, TOPK]) as top, \
            kit.sb("itop", [P, PH, 2, TOPK], U32) as itop:
        with kit.sb("peer_q", [P, PH, 2, SEQ]) as qT, kit.sb("keys", [P, 2, P]) as keys, kit.sb("keysT", [P, 2, P]) as keysT:
            load_keys(kit, dram, layer, keys)
            transposes(kit, [([keys[:, s, :] for s in range(2)], keysT[:])])
            linear_split(kit, fill, 8, True, lambda b, bank: nc.scalar.copy(qT[:, b], bank),
                         then=score_keys(kit, qT, keysT, scores, top, itop))
        experts(kit, dram, layer, scores, top, itop, mod, next_modulation)


def load_keys(kit, dram, layer, keys):
    with kit.nc.Block() as block:
        @block.sync
        def _(sp):
            kit.load(sp, keys[:], dram["peer_sub_keys"][layer].rearrange("s n k -> n s k"))
            sp.wait_ge(kit.count("loaded").sem, kit.count("loaded").n)


def score_keys(kit, qT, keysT, sc, top, itop):
    nc = kit.nc
    emptied, scored, copied = kit.count("bank_emptied"), kit.count("keys_scored"), kit.count("key_scores_copied")
    s0, c0 = scored.n, copied.n
    spare = kit.hT[:].rearrange("p k n -> p (k n)")[:, 0:2 * NKEYS].rearrange("p (j n) -> p j n", j=2)

    def tensor(pe, hh, e0):
        pe.wait_ge(emptied.sem, e0 + hh + 1)
        if hh >= 2:
            pe.wait_ge(copied.sem, c0 + hh - 1)
        for i in range(4):
            T, s = i // 2, i % 2
            mm = nc.tensor.matmul(kit.bank[5 + hh % 2][:, i * P:(i + 1) * P], qT[:, hh, s, T * P:(T + 1) * P],
                                  keysT[:, s, :], start=True, stop=True)
        scored.up(mm)

    def scalar(act, hh):
        act.wait_ge(scored.sem, s0 + hh + 1)
        copied.up(nc.scalar.copy(sc[:, :, 2 * hh:2 * hh + 2, :], kit.bank[5 + hh % 2][:, :].rearrange(
            "p (t a n) -> p t a n", t=NT, a=2)))

    def vector(dve, hh):
        dve.wait_ge(copied.sem, c0 + hh + 1)
        top16s(kit, dve, [(top[:, hh, s], itop[:, hh, s], sc[:, 0, 2 * hh + s], spare[:, s], 0) for s in range(2)])
        dve.wait_ge(kit.step["dve"].sem, kit.step["dve"].n)

    return tensor, scalar, vector


def top16s(kit, dve, jobs):
    nc = kit.nc
    step = kit.step["dve"]
    last = [n for _, _, _, _, n in jobs]
    for stage in range(5):
        for j, (values, indices, data, spare, _) in enumerate(jobs):
            if last[j]:
                dve.wait_ge(step.sem, last[j])
            if stage == 0:
                ins = nc.vector.max(values[:, 0:8], data)
            elif stage == 1:
                ins = nc.vector.max_index(indices[:, 0:8], values[:, 0:8], data)
            elif stage == 2:
                ins = nc.vector.match_replace(spare, values[:, 0:8], data, -3e38)
            elif stage == 3:
                ins = nc.vector.max(values[:, 8:16], spare)
            else:
                ins = nc.vector.max_index(indices[:, 8:16], values[:, 8:16], spare)
            last[j] = step.up(ins)


def choose(kit, dve, layer, T, halves_done, sc, small, wide, idx, gate, shifted):
    nc = kit.nc
    nu = 2 * PH
    step = kit.step["dve"]
    top, itop, ftop, best, pos, part, fpart, row, fidx = small
    cand = wide[:, 0:4 * 256].rearrange("p (j n) -> p j n", j=4)
    spare = wide[:, 4 * 256:8 * 256].rearrange("p (j n) -> p j n", j=4)
    for q in range(nu if halves_done else 0, nu, 4):
        top16s(kit, dve, [(top[:, u // 2, u % 2], itop[:, u // 2, u % 2], sc[:, T, u], spare[:, u - q, 0:NKEYS], 0)
                          for u in range(q, q + 4)])
        dve.wait_ge(step.sem, step.n)
    for q in range(0, PH, 4):
        made = [step.up(nc.vector.tensor_tensor(
            cand[:, hh - q].rearrange("p (a b) -> p a b", a=16), top[:, hh, 0].unsqueeze(2).to_broadcast([P, 16, 16]),
            top[:, hh, 1].unsqueeze(1).to_broadcast([P, 16, 16]), ALU.add)) for hh in range(q, q + 4)]
        top16s(kit, dve, [(best[:, hh], pos[:, hh], cand[:, hh - q], spare[:, hh - q], made[hh - q])
                          for hh in range(q, q + 4)])
        dve.wait_ge(step.sem, step.n)
    g = gate[:, T].rearrange("p (h k) -> p h k", h=PH)
    shifted.up(nc.vector.tensor_tensor(g, best[:], best[:, :, 0:1].to_broadcast([P, PH, TOPK]), ALU.subtract))
    flat = pos[:].rearrange("p h k -> p (h k)")
    nc.vector.tensor_copy(ftop[:], itop[:])
    nc.vector.tensor_scalar(part[:, 0], flat, 4, None, ALU.logical_shift_right)
    kit.dve(nc.vector.tensor_scalar(part[:, 1], flat, 15, None, ALU.bitwise_and))
    kit.dve(nc.vector.tensor_copy(fpart[:], part[:]))
    for s in range(2):
        sel = wide.rearrange("p (k i) -> p k i", i=16)
        kit.dve(nc.vector.tensor_tensor(sel, fpart[:, s].unsqueeze(2).to_broadcast([P, PICKS, 16]),
                                        kit.iota16.unsqueeze(1).to_broadcast([P, PICKS, 16]), ALU.is_equal))
        sv = sel.rearrange("p (h k) i -> p h k i", h=PH)
        kit.dve(nc.vector.tensor_tensor(sv, sv, ftop[:, :, s].unsqueeze(2).to_broadcast([P, PH, TOPK, 16]), ALU.mult))
        kit.dve(nc.vector.tensor_reduce(row[:, s], sel, AX, ALU.add))
    kit.dve(nc.vector.scalar_tensor_tensor(out=fidx[:], in0=row[:, 0], scalar=float(NKEYS), in1=row[:, 1],
                                           op0=ALU.mult, op1=ALU.add))
    if layer:
        kit.dve(nc.vector.tensor_scalar(fidx[:], fidx[:], float(layer * NKEYS * NKEYS), None, ALU.add))
    return nc.vector.tensor_copy(idx[:, T], fidx[:])


def experts(kit, dram, layer, sc, top, itop, mod, next_modulation):
    nc = kit.nc
    x, h = kit.x, kit.h
    UN = 2 * GRING
    rounds = PICKS // UN
    row_landed = [kit.count(f"row_landed{i}") for i in range(GRING)]
    claimed = kit.count("row_slots_claimed")
    free, idx_ready, dots, gelued = (kit.count("row_slots_freed"), kit.count("slot_indices"), kit.count("dots_copied"),
                                     kit.count("gelu_done"))
    chosen, shifted, exped = kit.count("experts_chosen"), kit.count("best_shifted"), kit.count("best_exped")
    weighted, diag_made = kit.count("row_weights_ready"), kit.count("diagonal_made")
    phases = [(name, T) for T in range(NT) for name in ("peer_down", "peer_up")]
    tables = {n: dram[n].rearrange("l e d -> (l e) d") for n in ("peer_down", "peer_up")}
    u0, i0, d0, g0, c0 = free.n - GRING, idx_ready.n, dots.n, gelued.n, chosen.n
    h0, x0, w0, m0 = shifted.n, exped.n, weighted.n, diag_made.n
    L0 = row_landed[0].n
    with kit.sb("rows", [P, GRING, D]) as ring, kit.sb("slot_idx", [P, 2, GRING], U32) as slot_idx, \
            kit.sb("dot16", [P, UN]) as dot16, kit.sb("dot", [P, PICKS]) as dot, kit.sb("acc", [P, D]) as acc, \
            kit.sb("idx", [P, NT, PICKS], U32) as idx, kit.sb("gate", [P, NT, PICKS]) as gate, \
            kit.sb("ftop", [P, PH, 2, TOPK]) as ftop, kit.sb("best", [P, PH, TOPK]) as best, \
            kit.sb("pos", [P, PH, TOPK], U32) as pos, kit.sb("part", [P, 2, PICKS], U32) as part, \
            kit.sb("fpart", [P, 2, PICKS]) as fpart, kit.sb("row", [P, 2, PICKS]) as row, \
            kit.sb("fidx", [P, PICKS]) as fidx, kit.sb("den", [P, 2, PH]) as den, \
            kit.sb("diag", [P, 4, P]) as diag, kit.sb("g2", [P, D]) as g2, \
            (modulation_space(kit, 1) if next_modulation else kit.sb("none", [1, 8])) as space, nc.Block() as block:
        small = (top, itop, ftop, best, pos, part, fpart, row, fidx)
        wide = kit.hT[:].rearrange("p k n -> p (k n)")
        also = modulation_parts(kit, dram, layer + 1, mod, None, space) if next_modulation else None

        if also:
            @block.sync
            def _(sp):
                also.sync(sp)

        @block.gpsimd
        def _(pool):
            for ph, (name, T) in enumerate(phases):
                if name == "peer_down":
                    pool.wait_ge(chosen.sem, c0 + T + 1)
                p0 = ph * PICKS
                with pool.Fori(0, rounds) as i:
                    for half in range(2):
                        j = p0 + half * GRING
                        pool.wait_ge(free.sem, i * UN + (u0 + j + 1))
                        nc.gpsimd.tensor_copy(slot_idx[:, half], idx[:, T, bass.ds(i * UN + half * GRING, GRING)]) \
                            .then_inc(idx_ready.sem, 1)
                        pool.wait_ge(idx_ready.sem, i * 2 + (i0 + ph * 2 * rounds + half + 1))
                        for s in range(GRING):
                            pool.wait_ge(free.sem, i * UN + (u0 + j + s + 1))
                            pool.sem_inc(claimed.sem, 1)
                            nc.gpsimd.indirect_dma_start(
                                ring[:, s], None, tables[name],
                                bass.IndirectOffsetOnAxis(ap=slot_idx[:, half, s:s + 1], axis=0)) \
                                .then_inc(row_landed[s].sem, 16)

        def wait_row(eng, i, ph, n):
            eng.wait_ge(row_landed[n % GRING].sem, i * 32 + (L0 + 16 * (ph * PICKS // GRING + n // GRING + 1)))

        @block.tensor
        def _(pe):
            if also:
                also.tensor(pe)
            for half in range(2):
                nc.tensor.matmul(kit.bank[6 + half][:, :], kit.zeros[0:1, 0:P], kit.zeros[0:1, :], start=True, stop=False,
                                 skip_group_check=True)
            with pe.Fori(0, PE_ROWS // UN) as i:
                for n in range(UN):
                    wait_row(pe, i, 1, n)
                    pe.wait_ge(diag_made.sem, i * UN + (m0 + n + 1))
                    for half in range(2):
                        mm = nc.tensor.matmul(kit.bank[6 + half][:, :], diag[:, n % 4], ring[:, n % GRING, half * 512:(half + 1) * 512],
                                              start=False, stop=False, skip_group_check=True)
                    mm.then_inc(free.sem, 1)

        @block.scalar
        def _(act):
            g2_kept = nc.scalar.copy(g2[:], mod[:, 5 * D:6 * D])
            if also:
                kit.act(g2_kept)
                also.scalar(act)
            for T in range(NT):
                act.wait_ge(shifted.sem, h0 + T + 1)
                exped.up(nc.scalar.activation(gate[:, T], gate[:, T], ACT.Exp))
                act.wait_ge(dots.sem, d0 + (T + 1) * rounds)
                gelued.up(nc.scalar.activation(dot[:], dot[:], ACT.Gelu_apprx_tanh))
                if T == 0:
                    act.wait_ge(weighted.sem, w0 + 1)
                    with act.Fori(0, PE_ROWS // UN) as i:
                        for n in range(UN):
                            act.wait_ge(free.sem, i * UN + (u0 + GRING + PICKS + n - 3))
                            nc.scalar.activation(diag[:, n % 4], kit.ident, ACT.Copy,
                                                 scale=gate[:, 0, bass.ds(i * UN + n, 1)]).then_inc(diag_made.sem, 1)

        @block.vector
        def _(dve):
            def down(ph, T):
                with dve.Fori(0, rounds) as i:
                    for n in range(UN):
                        s = n % GRING
                        wait_row(dve, i, ph, n)
                        if n == 0:
                            dve.wait_ge(dots.sem, i + (d0 + T * rounds))
                        nc.vector.tensor_tensor_reduce(out=ring[:, s], in0=ring[:, s], in1=h[:, T], scale=1.0, scalar=0.0,
                                                       op0=ALU.mult, op1=ALU.add, accum_out=dot16[:, n:n + 1]) \
                            .then_inc(free.sem, 1)
                    dve.wait_ge(free.sem, i * UN + (u0 + GRING + ph * PICKS + UN))
                    nc.vector.tensor_copy(dot[:, bass.ds(i * UN, UN)], dot16[:]).then_inc(dots.sem, 1)

            def weigh(T):
                dve.wait_ge(exped.sem, x0 + T + 1)
                g = gate[:, T].rearrange("p (h k) -> p h k", h=PH)
                kit.dve(nc.vector.tensor_reduce(den[:, 0], g, AX, ALU.add))
                kit.dve(nc.vector.reciprocal(den[:, 1], den[:, 0]))
                kit.dve(nc.vector.tensor_tensor(g, g, den[:, 1].unsqueeze(2).to_broadcast([P, PH, TOPK]), ALU.mult))
                dve.wait_ge(gelued.sem, g0 + T + 1)
                kit.dve(nc.vector.tensor_tensor(gate[:, T], gate[:, T], dot[:], ALU.mult))
                weighted.up(nc.vector.memset(kit.spare[:, 0:1], 0.0))

            def up(ph, T, first):
                with dve.Fori(0, rounds - first // UN) as i:
                    for n in range(UN):
                        g = ph * PICKS + first + n
                        wait_row(dve, i, ph, first + n)
                        dve.wait_ge(free.sem, i * UN + (u0 + GRING + g))
                        nc.vector.scalar_tensor_tensor(out=acc[:], in0=ring[:, n % GRING],
                                                       scalar=gate[:, T, bass.ds(i * UN + first + n, 1)], in1=acc[:],
                                                       op0=ALU.mult, op1=ALU.add).then_inc(free.sem, 1)
                dve.wait_ge(free.sem, u0 + GRING + (ph + 1) * PICKS)
                kit.dve(nc.vector.tensor_tensor(acc[:], acc[:], g2[:], ALU.mult))
                kit.dve(nc.vector.tensor_tensor(x[:, T], x[:, T], acc[:], ALU.add))

            if also:
                also.vector(dve)
            chosen.up(choose(kit, dve, layer, 0, True, sc, small, wide, idx, gate, shifted))
            down(0, 0)
            weigh(0)
            chosen.up(choose(kit, dve, layer, 1, False, sc, small, wide, idx, gate, shifted))
            dve.wait_ge(free.sem, u0 + GRING + PICKS + PE_ROWS)
            nc.vector.tensor_copy(acc[:, 0:512], kit.bank[6][:, :])
            kit.dve(nc.vector.tensor_copy(acc[:, 512:D], kit.bank[7][:, :]))
            up(1, 0, PE_ROWS)
            down(2, 1)
            weigh(1)
            kit.dve(nc.vector.memset(acc[:], 0.0))
            up(3, 1, 0)
    free.n += len(phases) * PICKS
    idx_ready.n += len(phases) * 2 * rounds
    dots.n += NT * rounds
    diag_made.n += PE_ROWS
    for c in row_landed:
        c.n += len(phases) * PICKS // GRING * 16



def ffn_blocks(dram, layer, which):
    g = columns(dram["ffn_w_gate_2"][layer, which])
    u = columns(dram["ffn_w_up_2"][layer, which])
    d = dram["ffn_w_down_2"][layer, which].rearrange("(f s p) n -> f p s n", s=2, p=P)
    out = [g[0], u[0]]
    for f in range(1, FF_BLOCKS):
        out += [g[f], u[f], d[f - 1]]
    return out + [d[FF_BLOCKS - 1]]


def swiglu(kit, dram, layer, which):
    nc, W = kit.nc, kit.weights
    x, h = kit.x, kit.h
    b0 = W.used
    nb = 3 * FF_BLOCKS
    loops = (FF_BLOCKS - 1) // 2
    silued, ready = kit.count("gate_silued"), kit.count("hidden_ready")
    high_made, split = kit.count("block_high_made"), kit.count("block_split")
    s0, r0, h0, p0 = silued.n, ready.n, high_made.n, split.n
    gate_w = dram["ffn_w_gate_2"][layer, which].rearrange("(k p) n -> p k n", p=P)
    up_w = dram["ffn_w_up_2"][layer, which].rearrange("(k p) n -> p k n", p=P)
    down_w = dram["ffn_w_down_2"][layer, which]

    def up_block(f, v):
        return v if f == 0 else 3 * f - 1 + v

    def wait(eng, sem, value, reg, per_round):
        eng.wait_ge(sem, value if reg is None else reg * per_round + value)

    with kit.sb("hT_high", [P, KD, SEQ], F32R) as hT, kit.sb("hT_low", [P, KD, SEQ], F32R) as hT_low, \
            kit.sb("high", [P, SPLIT_SLOTS, 2048], F32R) as high, kit.sb("low", [P, SPLIT_SLOTS, 2048], F32R) as low, \
            kit.sb("act_gate", [P, 2, 2 * SEQ]) as ag, kit.sb("hidden", [P, 2, 2, SEQ], F32R) as hid, \
            kit.sb("hidden_low", [P, 2, 2, SEQ], F32R) as hid_low:
        norm_split(kit, x, dram["ffn_norm_2"][layer, which:which + 1, :], None, None, h, hT, hT_low)

        def parts(b):
            return W.ring[:, (b0 + b) % SLOTS, :], high[:, b % SPLIT_SLOTS, :], low[:, b % SPLIT_SLOTS, :]

        def shaped(b, k):
            return [a.rearrange("p (k n) -> p k n", k=k) for a in parts(b)[1:]]

        with nc.Block() as block:
            @block.sync
            def _(sp):
                W.issue(sp, b0 + 2 + 6)
                with sp.Fori(0, loops - 1) as i:
                    for v in range(6):
                        b, f = b0 + 8 + v, 3 + v // 3
                        sp.wait_ge(W.multiplied, i * 6 + (b - SLOTS + 1))
                        if v % 3 < 2:
                            src = (gate_w, up_w)[v % 3][:, :, bass.ds(i * (2 * BLK) + f * BLK, BLK)]
                        else:
                            src = down_w[bass.ds(i * (2 * BLK) + (f - 1) * BLK, BLK), :].rearrange("(s p) n -> p s n", p=P)
                        sp.dma_start(W.tile(b, KD if v % 3 < 2 else 2), src).then_inc(W.landed[b % SLOTS], 16)
                W.issued = b0 + nb - 1
                W.issue(sp, b0 + nb + SLOTS)

            def up_products(pe, f, reg=None):
                for v in range(2):
                    b = up_block(f, v)
                    wait(pe, split.sem, p0 + b + 1, reg, 6)
                    if v == 0 and reg is not None:
                        wait(pe, ready.sem, r0 + f - 1, reg, 2)
                    w_hi, w_lo = shaped(b, KD)
                    for s in range(2):
                        o = kit.bank[2 * (f % 2) + v][:, s * SEQ:(s + 1) * SEQ]
                        for k in range(KD):
                            terms = [(w_lo, hT), (w_hi, hT_low), (w_hi, hT)]
                            for n, (w, t) in enumerate(terms):
                                mm = nc.tensor.matmul(o, w[:, k, s * P:(s + 1) * P], t[:, k, :],
                                                      start=(k == 0 and n == 0), stop=(k == KD - 1 and n == 2))
                    mm.then_inc(W.multiplied, 1)

            def down_products(pe, f, reg=None, last=False):
                b = 3 * f + 4 if not last else nb - 1
                wait(pe, split.sem, p0 + b + 1, reg, 6)
                wait(pe, ready.sem, r0 + f + 1, reg, 2)
                w_hi, w_lo = shaped(b, 2)
                for T in range(NT):
                    for half in range(2):
                        for s in range(2):
                            for n, (hidden, w) in enumerate([(hid, w_lo), (hid_low, w_hi), (hid, w_hi)]):
                                mm = nc.tensor.matmul(kit.bank[4 + 2 * T + half][:, :],
                                                      hidden[:, f % 2, s, T * P:(T + 1) * P],
                                                      w[:, s, half * 512:(half + 1) * 512], start=False,
                                                      stop=(last and s == 1 and n == 2), skip_group_check=True)
                mm.then_inc(W.multiplied, 1)

            @block.tensor
            def _(pe):
                for bnk in range(4, 8):
                    nc.tensor.matmul(kit.bank[bnk][:, :], kit.zeros[0:1, 0:P], kit.zeros[0:1, :], start=True, stop=False,
                                     skip_group_check=True)
                up_products(pe, 0)
                with pe.Fori(0, loops) as i:
                    for f in (1, 2):
                        up_products(pe, f, reg=i)
                        down_products(pe, f - 1, reg=i)
                down_products(pe, FF_BLOCKS - 1, last=True)

            @block.scalar
            def _(act):
                def make_high(b, reg=None):
                    wait(act, W.landed[(b0 + b) % SLOTS], 16 * ((b0 + b) // SLOTS + 1), reg, 16)
                    if reg is not None:
                        wait(act, W.multiplied, b0 + b - SPLIT_SLOTS + 1, reg, 6)
                    w, hi, _ = parts(b)
                    nc.scalar.copy(hi, w).then_inc(high_made.sem, 1)

                def gate(f, reg=None):
                    wait(act, W.multiplied, b0 + up_block(f, 0) + 1, reg, 6)
                    if reg is not None:
                        wait(act, ready.sem, r0 + f - 1, reg, 2)
                    nc.scalar.activation(ag[:, f % 2], kit.bank[2 * (f % 2)][:, :], ACT.Silu).then_inc(silued.sem, 1)

                for b in range(3):
                    make_high(b)
                gate(0)
                with act.Fori(0, loops) as i:
                    for b, f in ((3, None), (4, 1), (5, None), (6, None), (7, 2), (8, None)):
                        make_high(b, reg=i)
                        if f:
                            gate(f, reg=i)

            @block.vector
            def _(dve):
                def make_low(b, reg=None):
                    wait(dve, high_made.sem, h0 + b + 1, reg, 6)
                    w, hi, lo = parts(b)
                    nc.vector.tensor_tensor(lo, w, hi.bitcast(F32), ALU.subtract).then_inc(split.sem, 1)

                def make_hidden(f, reg=None):
                    wait(dve, W.multiplied, b0 + up_block(f, 1) + 1, reg, 6)
                    wait(dve, silued.sem, s0 + f + 1, reg, 2)
                    flat = lambda a: a[:, f % 2].rearrange("p s t -> p (s t)")
                    nc.vector.tensor_tensor(ag[:, f % 2], ag[:, f % 2], kit.bank[2 * (f % 2) + 1][:, :],
                                            ALU.mult).then_inc(made.sem, 1)
                    wait(dve, made.sem, m0 + 2 * f + 1, reg, 4)
                    nc.vector.tensor_copy(flat(hid), ag[:, f % 2]).then_inc(made.sem, 1)
                    wait(dve, made.sem, m0 + 2 * f + 2, reg, 4)
                    nc.vector.tensor_tensor(flat(hid_low), ag[:, f % 2], flat(hid).bitcast(F32), ALU.subtract) \
                        .then_inc(ready.sem, 1)

                made = kit.count("hidden_steps")
                m0 = made.n
                for b in range(3):
                    make_low(b)
                make_hidden(0)
                with dve.Fori(0, loops) as i:
                    for b, f in ((3, None), (4, None), (5, 1), (6, None), (7, None), (8, 2)):
                        make_low(b, reg=i)
                        if f:
                            make_hidden(f, reg=i)
                made.n += 2 * FF_BLOCKS
                dve.wait_ge(W.multiplied, b0 + nb)
                for T in range(NT):
                    for half in range(2):
                        xs = x[:, T, half * 512:(half + 1) * 512]
                        nc.vector.scalar_tensor_tensor(out=xs, in0=kit.bank[4 + 2 * T + half][:, :], scalar=0.5, in1=xs,
                                                       op0=ALU.mult, op1=ALU.add)
    silued.n += FF_BLOCKS
    ready.n += FF_BLOCKS
    high_made.n += nb
    split.n += nb
    W.used += nb



def parallel_attention(kit, dram):
    nc, W = kit.nc, kit.weights
    x, h, hT = kit.x, kit.h, kit.hT
    QK0, NQK = 3 * SB_HEADS * HD, 2 * DIL_HEADS * HD
    V0 = QK0 + NQK
    width = (SB_HEADS + GROUP_HEADS) * HD
    with kit.sb("cat2", [P, NT, width]) as cat:
        with kit.sb("proj2", [P, NT, 3 * D]) as proj, kit.sb("tT", [P, 16, SEQ]) as tT:
            linear_split(kit, lambda hi, lo: norm_split(kit, x, dram["mix_norm_2"][0:1, :], None, None, h, hi, lo),
                         12, False, copy_out(kit, proj))
            head_norms(kit, dram, proj, QK0)
            cols = [i * P for i in range(4)] + [QK0 + i * P for i in range(12)]
            jobs = []
            for T in range(NT):
                for c in range(0, 16, 4):
                    jobs.append(([proj[:, T, cols[c + i]:cols[c + i] + P] for i in range(4)],
                                 tT[:, c:c + 4, T * P:(T + 1) * P]))
            transposes(kit, jobs)
            stick_breaking(kit, proj, tT, cat)
            dilated(kit, dram, proj, tT, cat, V0)
        transpose_tokens(kit, cat, hT, kc=4)
        b0 = W.used
        done = kit.count("attention_projected")
        d0 = done.n
        with nc.Block() as block:
            @block.sync
            def _(sp):
                W.issue(sp, b0 + 2 + SLOTS)

            @block.tensor
            def _(pe):
                for b in range(2):
                    W.wait(pe, b0 + b)
                    w = W.tile(b0 + b, 4)
                    for T in range(NT):
                        for k in range(4):
                            mm = nc.tensor.matmul(kit.bank[2 * b + T][:, :], hT[:, k, T * P:(T + 1) * P], w[:, k, :],
                                                  start=(k == 0), stop=(k == 3))
                    mm.then_inc(W.multiplied, 1)

            @block.vector
            def _(dve):
                for b in range(2):
                    dve.wait_ge(W.multiplied, b0 + b + 1)
                    for T in range(NT):
                        xs = x[:, T, b * 512:(b + 1) * 512]
                        nc.vector.tensor_tensor(xs, xs, kit.bank[2 * b + T][:, :], ALU.add)
        W.used += 2


def head_norms(kit, dram, proj, c0):
    nc = kit.nc
    n = DIL_HEADS
    loaded = kit.count("loaded")
    l0 = loaded.n
    with kit.sb("qkg", [P, 2, HD]) as qkg, kit.sb("sq", [P, 2 * n, HD]) as sq, kit.sb("st", [P, 3, 2 * n]) as st, \
            nc.Block() as block:
        @block.sync
        def _(sp):
            kit.load(sp, qkg[:, 0], bcast(dram["attn_q_norm_2"], HD))
            kit.load(sp, qkg[:, 1], bcast(dram["attn_k_norm_2"], HD))

        @block.scalar
        def _(act):
            kit.roots(act, [(st[:, 2], st[:, 1])] * NT)

        @block.vector
        def _(dve):
            for T in range(NT):
                v = proj[:, T, c0:c0 + 2 * n * HD].rearrange("p (g d) -> p g d", d=HD)
                kit.dve(nc.vector.tensor_tensor(sq[:], v, v, ALU.mult))
                kit.dve(nc.vector.tensor_reduce(st[:, 0], sq[:], AX, ALU.add))
                kit.rsqrt(dve, nc.vector.tensor_scalar(st[:, 1], st[:, 0], 1.0 / HD, EPS, ALU.mult, ALU.add), st[:, 2], st[:, 2])
                kit.dve(nc.vector.tensor_tensor(v, v, st[:, 2].unsqueeze(2).to_broadcast([P, 2 * n, HD]), ALU.mult))
                if T == 0:
                    dve.wait_ge(loaded.sem, l0 + 32)
                for s in range(2):
                    vs = v[:, s * n:(s + 1) * n]
                    kit.dve(nc.vector.tensor_tensor(vs, vs, qkg[:, s].unsqueeze(1).to_broadcast([P, n, HD]), ALU.mult))


def stick_breaking(kit, proj, tT, cat):
    nc = kit.nc
    H = SB_HEADS
    scored, zed, logged, kept, summed, logw, weighed, ready, mixed = (
        kit.count(n) for n in ("sb_scored", "sb_z", "sb_log", "sb_kept", "sb_after", "sb_logw", "sb_exped", "sb_ready",
                               "sb_mixed"))
    base = {c: c.n for c in (scored, zed, logged, kept, summed, logw, weighed, ready, mixed)}
    with kit.sb("z", [P, H, NT, SEQ]) as z, kit.sb("lg", [P, H, NT, SEQ]) as lg, kit.sb("lk", [P, H, NT, SEQ]) as lk, \
            nc.Block() as block:
        @block.tensor
        def _(pe):
            for hh in range(H):
                b, c = hh % 2 * HD, hh // 2
                for kt in range(NT):
                    mm = nc.tensor.matmul(kit.bank[hh][:, kt * SEQ:(kt + 1) * SEQ],
                                          tT[b:b + HD, 2 + c, kt * P:(kt + 1) * P], tT[b:b + HD, c, :],
                                          start=True, stop=True)
                scored.up(mm)
            for hh in range(H):
                pe.wait_ge(kept.sem, base[kept] + hh + 1)
                bank = kit.bank[4 + hh % 4]
                nc.tensor.matmul(bank[:, 0:SEQ], kit.after, lk[:, hh, 0, :], start=True, stop=False)
                nc.tensor.matmul(bank[:, 0:SEQ], kit.ones[:, 0:P], lk[:, hh, 1, :], start=False, stop=True)
                summed.up(nc.tensor.matmul(bank[:, SEQ:2 * SEQ], kit.after, lk[:, hh, 1, :], start=True, stop=True))
            for hh in range(H):
                pe.wait_ge(ready.sem, base[ready] + hh + 1)
                for T in range(NT):
                    for kt in range(T + 1):
                        mm = nc.tensor.matmul(kit.bank[0][:, (T * H + hh) * HD:(T * H + hh + 1) * HD],
                                              z[:, hh, kt, T * P:(T + 1) * P],
                                              proj[:, kt, (2 * H + hh) * HD:(2 * H + hh + 1) * HD],
                                              start=(kt == 0), stop=(kt == T))
                mixed.up(mm)

        @block.scalar
        def _(act):
            for hh in range(H):
                act.wait_ge(scored.sem, base[scored] + hh + 1)
                zv = z[:, hh].rearrange("p k q -> p (k q)")
                lv = lg[:, hh].rearrange("p k q -> p (k q)")
                zed.up(nc.scalar.activation(zv, kit.bank[hh][:, :], ACT.Copy, scale=SCALE))
                kit.act(nc.scalar.activation(lv, kit.bank[hh][:, :], ACT.Abs, scale=SCALE))
                kit.act(nc.scalar.activation(lv, lv, ACT.Exp, scale=-1.0))
                logged.up(nc.scalar.activation(lv, lv, ACT.Ln, bias=1.0))
            for hh in range(H):
                act.wait_ge(logw.sem, base[logw] + hh + 1)
                zv = z[:, hh].rearrange("p k q -> p (k q)")
                weighed.up(nc.scalar.activation(zv, zv, ACT.Exp))
            act.wait_ge(mixed.sem, base[mixed] + H)
            nc.scalar.copy(cat[:, :, 0:H * HD], kit.bank[0][:, :].rearrange("p (t n) -> p t n", t=NT))

        @block.vector
        def _(dve):
            for hh in range(H):
                dve.wait_ge(zed.sem, base[zed] + hh + 1)
                dve.wait_ge(logged.sem, base[logged] + hh + 1)
                kit.dve(nc.vector.scalar_tensor_tensor(out=lg[:, hh], in0=z[:, hh], scalar=0.0, in1=lg[:, hh],
                                                       op0=ALU.max, op1=ALU.add))
                kept.up(nc.vector.scalar_tensor_tensor(out=lk[:, hh], in0=lg[:, hh], scalar=-1.0, in1=kit.strict,
                                                       op0=ALU.mult, op1=ALU.mult))
                kit.dve(nc.vector.tensor_tensor(z[:, hh], z[:, hh], lg[:, hh], ALU.subtract))
            for hh in range(H):
                dve.wait_ge(summed.sem, base[summed] + hh + 1)
                logw.up(nc.vector.tensor_tensor(z[:, hh], z[:, hh], kit.bank[4 + hh % 4][:, :].rearrange(
                    "p (k q) -> p k q", k=NT), ALU.add))
            for hh in range(H):
                dve.wait_ge(weighed.sem, base[weighed] + hh + 1)
                ready.up(nc.vector.tensor_tensor(z[:, hh], z[:, hh], kit.strict, ALU.mult))


def dilated(kit, dram, proj, tT, cat, v0):
    nc = kit.nc
    G, J = DIL_GROUPS, GROUP_HEADS
    loaded, rowed, copied, stored = (kit.count(n) for n in ("loaded", "bias_rows", "bias_copied", "bias_stored"))
    l0, r0, c0, t0 = loaded.n, rowed.n, copied.n, stored.n
    scratch = dram["bias_scratch"]
    with kit.sb("bias", [P, NT, DIL_HEADS, SEQ]) as bias:
        with kit.sb("onehot", [N_BUCKETS + 1, G, 512]) as onehot, kit.sb("table", [N_BUCKETS + 1, DIL_HEADS]) as table, \
                kit.sb("bias_rows", [J, G, 512]) as rows, nc.Block() as block:
            @block.vector
            def _(dve):
                nc.vector.memset(table[N_BUCKETS:N_BUCKETS + 1, :], NEG).then_inc(rowed.sem, 1)
                rowed.n += 1

            @block.sync
            def _(sp):
                kit.load(sp, onehot[:], dram["onehot"])
                kit.load(sp, table[0:N_BUCKETS, :], dram["rel_bias_2"])
                sp.wait_ge(copied.sem, c0 + G)
                stored.up(sp.dma_start(scratch.rearrange("(g j) n -> j g n", g=G), rows[:]), 16)
                sp.wait_ge(stored.sem, t0 + 16)
                for T in range(NT):
                    src = bass.AP(scratch.tensor, scratch.offset + T * P, [[1, P], [512, DIL_HEADS], [1, SEQ]])
                    kit.load(sp, bias[:, T], src)
                sp.wait_ge(loaded.sem, l0 + 64)

            @block.tensor
            def _(pe):
                pe.wait_ge(loaded.sem, l0 + 32)
                pe.wait_ge(rowed.sem, r0 + 1)
                for g in range(G):
                    rowed.up(nc.tensor.matmul(kit.bank[g][0:J, :], table[:, g * J:(g + 1) * J], onehot[:, g, :],
                                              start=True, stop=True))

            @block.scalar
            def _(act):
                for g in range(G):
                    act.wait_ge(rowed.sem, r0 + 2 + g)
                    copied.up(nc.scalar.copy(rows[:, g, :], kit.bank[g][0:J, :]))

        units = [(T, j) for T in range(NT) for j in range(J)]
        nu = len(units)
        scored, masked = kit.count("scored"), kit.count("score_masked")
        negmax, exped = kit.count("negmax_ready"), kit.count("exped")
        s0, k0, n0, x0 = scored.n, masked.n, negmax.n, exped.n
        with kit.sb("probs", [P, nu, G * SEQ]) as probs, kit.sb("PT", [P, 4, 4, P]) as PT, \
                kit.sb("gmax", [P, nu, G]) as gmax, kit.sb("rows", [P, 4, nu]) as rows:
            chunks = [[c for c in range(2 * G) if c % 2 <= T] for T, _ in units]
            pe_side, act_side, m_end = attend(
                kit, chunks, PT, lambda u: kit.bank[4][:, u * HD:(u + 1) * HD],
                lambda u, c: probs[:, u, c * P:(c + 1) * P],
                lambda u, c: proj[:, c % 2, v0 + (c // 2 * J + units[u][1]) * HD:v0 + (c // 2 * J + units[u][1] + 1) * HD])
            mixed = kit.count("values_mixed")
            with nc.Block() as block:
                @block.tensor
                def _(pe):
                    for u, (T, j) in enumerate(units):
                        for g in range(G):
                            n = u * G + g
                            if n >= 4:
                                pe.wait_ge(masked.sem, k0 + n - 3)
                            hh = g * J + j
                            b = hh % 2 * HD
                            scored.up(nc.tensor.matmul(kit.bank[n % 4][:, 0:SEQ], tT[b:b + HD, 4 + hh // 2, T * P:(T + 1) * P],
                                                       tT[b:b + HD, 10 + hh // 2, :], start=True, stop=True))
                    pe.wait_ge(masked.sem, k0 + nu * G)
                    pe_side(pe, lambda pe, u: pe.wait_ge(exped.sem, x0 + u + 1))

                @block.vector
                def _(dve):
                    for u, (T, j) in enumerate(units):
                        for g in range(G):
                            n = u * G + g
                            dve.wait_ge(scored.sem, s0 + n + 1)
                            masked.up(nc.vector.tensor_tensor_reduce(
                                out=probs[:, u, g * SEQ:(g + 1) * SEQ], in0=kit.bank[n % 4][:, 0:SEQ],
                                in1=bias[:, T, g * J + j, ::-1], scale=SCALE, scalar=NEG, op0=ALU.add, op1=ALU.max,
                                accum_out=gmax[:, u, g:g + 1]))
                    dve.wait_ge(masked.sem, k0 + nu * G)
                    kit.dve(nc.vector.tensor_reduce(rows[:, 0], gmax[:], AX, ALU.max))
                    negmax.up(nc.vector.tensor_scalar(rows[:, 1], rows[:, 0], -1.0, None, ALU.mult))
                    dve.wait_ge(exped.sem, x0 + nu)
                    kit.dve(nc.vector.reciprocal(rows[:, 3], rows[:, 2]))
                    dve.wait_ge(mixed.sem, m_end)
                    for T in range(NT):
                        nc.vector.tensor_tensor(
                            cat[:, T, SB_HEADS * HD:].rearrange("p (j d) -> p j d", d=HD),
                            kit.bank[4][:, T * J * HD:(T + 1) * J * HD].rearrange("p (j d) -> p j d", d=HD),
                            rows[:, 3, T * J:(T + 1) * J].unsqueeze(2).to_broadcast([P, J, HD]), ALU.mult)

                @block.scalar
                def _(act):
                    act.wait_ge(negmax.sem, n0 + 1)
                    for u in range(nu):
                        exped.up(nc.scalar.activation(probs[:, u], probs[:, u], ACT.Exp, bias=rows[:, 1, u:u + 1],
                                                      accum_out=rows[:, 2, u:u + 1]))
                    act_side(act)



def load_only(kit, pairs):
    loaded = kit.count("loaded")
    l0 = loaded.n
    with kit.nc.Block() as block:
        @block.sync
        def _(sp):
            for dst, src in pairs:
                kit.load(sp, dst, src)
            sp.wait_ge(loaded.sem, l0 + 16 * len(pairs))


def vector_only(kit, body, roots=(), load=()):
    loaded = kit.count("loaded")
    l0 = loaded.n
    with kit.nc.Block() as block:
        @block.sync
        def _(sp):
            for dst, src in load:
                kit.load(sp, dst, src)
            if load:
                sp.wait_ge(loaded.sem, l0 + 16 * len(load))

        @block.scalar
        def _(act):
            kit.roots(act, roots)

        @block.vector
        def _(dve):
            body(dve)


def time_mix(kit, dram):
    x, h, hT = kit.x, kit.h, kit.hT
    norm_plain(kit, x, dram["mix_norm_2"][1:2, :], h)
    transpose_tokens(kit, h, hT)
    sb = kit.sb
    with sb("R", [P, NT, D]) as R, sb("K", [P, NT, D]) as K, sb("V", [P, NT, D]) as V, sb("A", [P, NT, D]) as A, \
            sb("KK", [P, NT, D]) as KK, sb("G", [P, NT, D]) as G, sb("bonus", [P, NT, RH]) as bonus, \
            sb("chunk_decay", [P, KD, NT, CH]) as PC:
        with sb("L", [P, NT, D]) as L:
            projections(kit, dram, R, K, V, A, L, G)
            prepare_keys(kit, dram, R, K, A, KK, L, bonus, PC)
        with sb("inverseT", [P, NT * RH, P]) as inv:
            invert(kit, dram, A, KK, inv)
            with sb("states", [P, CH + 1, KD, HD]) as S:
                vector_only(kit, lambda dve: kit.nc.vector.memset(S[:, CH], 0.0))
                for T in range(NT):
                    recur(kit, T, R, K, V, A, KK, PC, inv, S)
        finish_mix(kit, dram, R, V, G, bonus)


def project_mixes(kit, shift, mix, scratch, out):
    nc, W = kit.nc, kit.weights
    b0, slots, nb, per = W.used, 2, 12, 4
    emptied, high_made, split = kit.count("bank_emptied"), kit.count("block_high_made"), kit.count("block_split")
    mixed, mix_high, mix_split = kit.count("mix_made"), kit.count("mix_high_made"), kit.count("mix_split")
    e0, h0, p0, m0, g0, s0 = emptied.n, high_made.n, split.n, mixed.n, mix_high.n, mix_split.n
    tmp = [a[:].rearrange("p t (a n) -> p (t a) n", n=SEQ) for a in scratch]
    split_before = {0: 0, 2: 1, 6: 2}
    with kit.sb("mix_high", [P, 2, KD, SEQ], F32R) as x_hi, kit.sb("mix_low", [P, 2, KD, SEQ], F32R) as x_lo, \
            kit.sb("high", [P, slots, 2048], F32R) as high, kit.sb("low", [P, slots, 2048], F32R) as low, \
            nc.Block() as block:
        @block.sync
        def _(sp):
            W.issue(sp, b0 + nb + SLOTS)

        @block.tensor
        def _(pe):
            for b in range(nb):
                pe.wait_ge(split.sem, p0 + b + 1)
                pe.wait_ge(mix_split.sem, s0 + b // per + 1)
                if b >= 4:
                    pe.wait_ge(emptied.sem, e0 + b - 3)
                w_hi, w_lo = (a[:, b % slots, :].rearrange("p (k n) -> p k n", k=KD) for a in (high, low))
                t_hi, t_lo = x_hi[:, b // per % 2], x_lo[:, b // per % 2]
                for T in range(NT):
                    for k in range(KD):
                        for n, (w, t) in enumerate([(w_lo, t_hi), (w_hi, t_lo), (w_hi, t_hi)]):
                            mm = nc.tensor.matmul(kit.bank[b % 4][:, T * BLK:(T + 1) * BLK], t[:, k, T * P:(T + 1) * P],
                                                  w[:, k, :], start=(k == 0 and n == 0), stop=(k == KD - 1 and n == 2))
                mm.then_inc(W.multiplied, 1)

        @block.scalar
        def _(act):
            for b in range(nb + slots):
                if b in split_before:
                    m = split_before[b]
                    act.wait_ge(mixed.sem, m0 + m + 1)
                    if m >= 2:
                        act.wait_ge(W.multiplied, b0 + (m - 1) * per)
                    mix_high.up(nc.scalar.copy(x_hi[:, m % 2], tmp[m % 2]))
                if b < nb:
                    W.wait(act, b0 + b)
                    if b >= slots:
                        act.wait_ge(W.multiplied, b0 + b - slots + 1)
                    high_made.up(nc.scalar.copy(high[:, b % slots, :], W.ring[:, (b0 + b) % SLOTS, :]))
                if b >= slots:
                    e = b - slots
                    act.wait_ge(W.multiplied, b0 + e + 1)
                    emptied.up(nc.scalar.copy(out[e // per][:, :, e % per * BLK:(e % per + 1) * BLK],
                                              kit.bank[e % 4][:, :].rearrange("p (t n) -> p t n", t=2)))

        @block.vector
        def _(dve):
            shift()
            for b in range(nb):
                if b in split_before:
                    m = split_before[b]
                    mixed.up(mix((0, 2, 3)[m], tmp[m % 2]))
                    dve.wait_ge(mix_high.sem, g0 + m + 1)
                    mix_split.up(nc.vector.tensor_tensor(x_lo[:, m % 2], tmp[m % 2], x_hi[:, m % 2].bitcast(F32), ALU.subtract))
                dve.wait_ge(high_made.sem, h0 + b + 1)
                split.up(nc.vector.tensor_tensor(low[:, b % slots, :], W.ring[:, (b0 + b) % SLOTS, :],
                                                 high[:, b % slots, :].bitcast(F32), ALU.subtract))
    W.used += nb


def projections(kit, dram, R, K, V, A, L, G):
    nc, W = kit.nc, kit.weights
    hT = kit.hT
    xx = kit.h[:].rearrange("p t (a n) -> p (t a) n", n=SEQ)
    with kit.sb("mix_rows", [6 * KD, P]) as mix_rows, kit.sb("mixT", [P, 6 * KD]) as mixT:
        load_only(kit, [(mix_rows[:], dram["rw_mix_2"].rearrange("e i (k p) -> (e i k) p", p=P))])
        transposes(kit, [([mix_rows[:]], mixT[:].unsqueeze(1))])

        def shift():
            nc.vector.tensor_scalar(xx[:, :, 0:1], hT[:, :, 0:1], -1.0, None, ALU.mult)
            kit.dve(nc.vector.tensor_tensor(xx[:, :, 1:], hT[:, :, 0:SEQ - 1], hT[:, :, 1:], ALU.subtract))

        def mix(i, dst):
            for k in range(KD):
                ins = nc.vector.scalar_tensor_tensor(out=dst[:, k], in0=xx[:, k], scalar=mixT[:, i * KD + k:i * KD + k + 1],
                                                     in1=hT[:, k], op0=ALU.mult, op1=ALU.add)
            return ins

        project_mixes(kit, shift, mix, (L, A), (R, K, V))
        with kit.sb("mixed", [P, 3, KD, SEQ]) as xm:
            with kit.sb("w1", [P, KD, 64]) as w1, kit.sb("a1", [P, KD, 64]) as a1, kit.sb("g1", [P, KD, 160]) as g1, \
                    kit.sb("w2", [64, D]) as w2, kit.sb("a2", [64, D]) as a2, kit.sb("g2", [P, D]) as g2, \
                    kit.sb("g2b", [32, D]) as g2b, kit.sb("w0", [P, D]) as w0, kit.sb("a0", [P, D]) as a0, \
                    kit.sb("tw", [64, SEQ]) as tw, kit.sb("ta", [64, SEQ]) as ta, kit.sb("tg", [P, SEQ]) as tg, \
                    kit.sb("tgb", [32, SEQ]) as tgb:
                vector_only(kit, lambda dve: [mix(i, xm[:, n]) for n, i in enumerate((1, 4, 5))],
                            load=[(t[:], dram[n][0].rearrange("(k p) n -> p k n", p=P)) for t, n in
                                ((w1, "rw_w1_2"), (a1, "rw_a1_2"), (g1, "rw_g1_2"))] +
                          [(w2[:], dram["rw_w2_2"][0]), (a2[:], dram["rw_a2_2"][0]), (g2[:], dram["rw_g2_2"][0, 0:P]),
                           (g2b[:], dram["rw_g2_2"][0, P:160]), (w0[:], bcast(dram["rw_w0_2"], D)),
                           (a0[:], bcast(dram["rw_a0_2"], D))])
                inner, innered, outer, biased = (kit.count(n) for n in ("lora_in", "lora_in_copied", "lora_out", "lora_biased"))
                i0, c0, o0, z0 = inner.n, innered.n, outer.n, biased.n
                with nc.Block() as block:
                    @block.tensor
                    def _(pe):
                        for n, (w, lo, hi) in enumerate(((w1, 0, 64), (a1, 0, 64), (g1, 0, P), (g1, P, 160))):
                            for k in range(KD):
                                mm = nc.tensor.matmul(kit.bank[n][0:hi - lo, 0:SEQ], w[:, k, lo:hi], xm[:, min(n, 2), k],
                                                      start=(k == 0), stop=(k == KD - 1))
                            inner.up(mm)
                        for n, parts in enumerate((((tw, w2),), ((ta, a2),), ((tg, g2), (tgb, g2b)))):
                            pe.wait_ge(innered.sem, c0 + (1 if n == 0 else 4))
                            for q in range(4):
                                T, half = q // 2, q % 2
                                if n == 2:
                                    pe.wait_ge(biased.sem, z0 + q + 1)
                                for i, (t, w) in enumerate(parts):
                                    mm = nc.tensor.matmul(kit.bank[(4 if n != 1 else 0) + q][:, :], t[:, T * P:(T + 1) * P],
                                                          w[:, half * 512:(half + 1) * 512],
                                                          start=(i == 0), stop=(i == len(parts) - 1))
                                outer.up(mm)

                    @block.scalar
                    def _(act):
                        for n, (t, rows, func) in enumerate(((tw, 64, ACT.Tanh), (ta, 64, ACT.Copy), (tg, P, ACT.Sigmoid),
                                                             (tgb, 32, ACT.Sigmoid))):
                            act.wait_ge(inner.sem, i0 + n + 1)
                            innered.up(nc.scalar.activation(t[:], kit.bank[n][0:rows, 0:SEQ], func))
                        for n, dst in enumerate((L, A)):
                            act.wait_ge(biased.sem, z0 + 4 * n + 4)
                            nc.scalar.activation(dst[:], dst[:], ACT.Sigmoid)
                        for q in range(4):
                            act.wait_ge(outer.sem, o0 + 8 + q + 1)
                            nc.scalar.copy(G[:, q // 2, q % 2 * 512:(q % 2 + 1) * 512], kit.bank[4 + q][:, :])

                    @block.vector
                    def _(dve):
                        for n, (dst, row) in enumerate(((L, w0), (A, a0))):
                            for q in range(4):
                                T, cols = q // 2, slice(q % 2 * 512, (q % 2 + 1) * 512)
                                dve.wait_ge(outer.sem, o0 + 4 * n + q + 1)
                                biased.up(nc.vector.tensor_tensor(dst[:, T, cols], kit.bank[(4 if n == 0 else 0) + q][:, :],
                                                                  row[:, cols], ALU.add))


def heads(a):
    return a.rearrange("p (h d) -> p h d", d=HD)


def wide(row, n=HD):
    return row.unsqueeze(2).to_broadcast([P, row.shape[1], n])


def prepare_keys(kit, dram, R, K, A, KK, L, bonus, PC):
    nc = kit.nc
    ready, summed, exped, tmp_free, shifted = (kit.count(n) for n in ("log_decay_ready", "log_decay_summed", "decay_exped",
                                                                     "tmp_free", "log_decay_shifted"))
    r0, s0, x0, t0, h0 = ready.n, summed.n, exped.n, tmp_free.n, shifted.n
    with kit.sb("kk_w", [P, 3, D]) as rows, kit.sb("decay", [P, NT, D]) as up, kit.sb("rsum", [P, 4, RH]) as rs:
        down = kit.h
        loaded = kit.count("loaded")
        l0 = loaded.n
        with nc.Block() as block:
            @block.sync
            def _(sp):
                kit.load(sp, rows[:, 0], bcast(dram["rw_kk_2"], D))
                kit.load(sp, rows[:, 1], bcast(dram["rw_ka_2"], D))
                kit.load(sp, rows[:, 2], bcast(dram["rw_rk_2"].rearrange("e h d -> e (h d)"), D))

            @block.vector
            def _(dve):
                ready.up(nc.vector.tensor_scalar(L[:], L[:], -float(np.exp(-0.5)), None, ALU.mult))
                dve.wait_ge(loaded.sem, l0 + 48)
                for T in range(NT):
                    t = down[:, T]
                    kit.dve(nc.vector.tensor_tensor(KK[:, T], K[:, T], rows[:, 0], ALU.mult))
                    kit.dve(nc.vector.tensor_tensor(t, KK[:, T], KK[:, T], ALU.mult))
                    kit.dve(nc.vector.tensor_reduce(rs[:, 0], heads(t), AX, ALU.add))
                    kit.rsqrt(dve, nc.vector.tensor_scalar(rs[:, 1], rs[:, 0], 1e-24, None, ALU.max), rs[:, 2], rs[:, 2])
                    kit.dve(nc.vector.tensor_tensor(heads(KK[:, T]), heads(KK[:, T]), wide(rs[:, 2]), ALU.mult))
                    kit.dve(nc.vector.scalar_tensor_tensor(out=t, in0=A[:, T], scalar=-1.0, in1=rows[:, 1],
                                                           op0=ALU.add, op1=ALU.mult))
                    kit.dve(nc.vector.scalar_tensor_tensor(out=K[:, T], in0=t, scalar=1.0, in1=K[:, T],
                                                           op0=ALU.add, op1=ALU.mult))
                    kit.dve(nc.vector.tensor_tensor(t, R[:, T], K[:, T], ALU.mult))
                    kit.dve(nc.vector.tensor_tensor(t, t, rows[:, 2], ALU.mult))
                    kit.dve(nc.vector.tensor_reduce(bonus[:, T], heads(t), AX, ALU.add))
                    kit.dve(nc.vector.tensor_tensor(A[:, T], A[:, T], KK[:, T], ALU.mult))
                tmp_free.up(nc.vector.memset(kit.spare[:, 0:1], 0.0))
                dve.wait_ge(summed.sem, s0 + 2)
                for q in range(4):
                    T, cols = q // 2, slice(q % 2 * 512, (q % 2 + 1) * 512)
                    shifted.up(nc.vector.tensor_tensor(L[:, T, cols], kit.bank[q][:, :], L[:, T, cols], ALU.subtract))
                dve.wait_ge(exped.sem, x0 + 4)
                nc.vector.tensor_tensor(R[:], R[:], up[:], ALU.mult)
                dve.wait_ge(exped.sem, x0 + 8)
                nc.vector.tensor_tensor(K[:], K[:], down[:], ALU.mult)
                nc.vector.tensor_tensor(A[:], A[:], down[:], ALU.mult)
                dve.wait_ge(exped.sem, x0 + 9)
                nc.vector.scalar_tensor_tensor(out=KK[:], in0=KK[:], scalar=-1.0, in1=L[:], op0=ALU.mult, op1=ALU.mult)

            @block.tensor
            def _(pe):
                pe.wait_ge(ready.sem, r0 + 1)
                for q in range(4):
                    mm = nc.tensor.matmul(kit.bank[q][:, :], kit.le, L[:, q // 2, q % 2 * 512:(q % 2 + 1) * 512],
                                          start=True, stop=True)
                summed.up(mm)
                for k in range(KD):
                    for T in range(NT):
                        n = (k * NT + T) * CH
                        mm = nc.tensor.matmul(kit.bank[4][:, n:n + CH], L[:, T, k * P:(k + 1) * P], kit.ends,
                                              start=True, stop=True)
                summed.up(mm)

            @block.scalar
            def _(act):
                kit.roots(act, [(rs[:, 2], rs[:, 1])] * NT)
                act.wait_ge(summed.sem, s0 + 2)
                nc.scalar.activation(PC[:].rearrange("p k t c -> p (k t c)"), kit.bank[4][:, 0:KD * NT * CH], ACT.Exp)
                for q in range(4):
                    act.wait_ge(shifted.sem, h0 + q + 1)
                    exped.up(nc.scalar.activation(up[:, q // 2, q % 2 * 512:(q % 2 + 1) * 512], kit.bank[q][:, :], ACT.Exp))
                act.wait_ge(tmp_free.sem, t0 + 1)
                for q in range(4):
                    exped.up(nc.scalar.activation(down[:, q // 2, q % 2 * 512:(q % 2 + 1) * 512], kit.bank[q][:, :],
                                                  ACT.Exp, scale=-1.0))
                act.wait_ge(shifted.sem, h0 + 4)
                exped.up(nc.scalar.activation(L[:], L[:], ACT.Exp))


def invert(kit, dram, A, KK, inv):
    nc = kit.nc
    NS = NT * RH
    grams, masked, stored, loaded, solved = (kit.count(n) for n in ("grams", "grams_masked", "systems_stored", "loaded",
                                                                    "solved"))
    g0, m0, t0, l0, v0 = grams.n, masked.n, stored.n, loaded.n, solved.n
    tri, out = (dram[n].rearrange("(u c) (j t) -> c j u t", c=CH, j=C) for n in ("systems", "inverses"))
    with kit.sb("sysd", [P, NS, C]) as sysd, kit.sb("sys", [P, C, C]) as sy, kit.sb("XT", [P, C, C]) as XT, \
            kit.sb("terms", [P, C, C]) as terms:
        with kit.sb("aT", [P, NT * KD, P]) as aT, kit.sb("bT", [P, NT * KD, P]) as bT:
            transposes(kit, [([src[:, T, (k + i) * P:(k + i + 1) * P] for i in range(4)],
                              dst[:, T * KD + k:T * KD + k + 4, :])
                             for src, dst in ((KK, aT), (A, bT)) for T in range(NT) for k in (0, 4)])
            with nc.Block() as block:
                @block.tensor
                def _(pe):
                    for n in range(NS // 4):
                        if n >= 4:
                            pe.wait_ge(masked.sem, m0 + (n - 3) * CH)
                        for i in range(4):
                            b, p = n % 2 * HD, n // 2 * 4 + i
                            mm = nc.tensor.matmul(kit.bank[n % 4][:, i * P:(i + 1) * P], bT[b:b + HD, p, :],
                                                  aT[b:b + HD, p, :], start=True, stop=True)
                        grams.up(mm)

                @block.vector
                def _(dve):
                    for n in range(NS // 4):
                        dve.wait_ge(grams.sem, g0 + n + 1)
                        for c in range(CH):
                            r = slice(c * C, (c + 1) * C)
                            bank = kit.bank[n % 4][:, :].rearrange("p (u t) -> p u t", u=4)
                            u = n // 2 * 8 + n % 2
                            masked.up(nc.vector.tensor_tensor(sysd[r, u:u + 7:2, :], bank[r, :, r],
                                                              kit.lt[r, r].unsqueeze(1).to_broadcast([C, 4, C]), ALU.mult))

        with nc.Block() as block:
            @block.sync
            def _(sp):
                for c in range(CH):
                    stored.up(sp.dma_start(tri[c], sysd[c * C:(c + 1) * C]), 16)
                sp.wait_ge(stored.sem, t0 + 16 * CH)
                kit.load(sp, sy[:], dram["systems"].rearrange("s (j t) -> s j t", j=C))
                sp.wait_ge(solved.sem, v0 + 1)
                stored.up(sp.dma_start(dram["inverses"].rearrange("s (j t) -> s j t", j=C), XT[:]), 16)
                sp.wait_ge(stored.sem, t0 + 16 * (CH + 1))
                for c in range(CH):
                    r = slice(c * C, (c + 1) * C)
                    kit.load(sp, inv[r, :, r], out[c])
                sp.wait_ge(loaded.sem, l0 + 16 * (CH + 1))

            @block.vector
            def _(dve):
                kit.dve(nc.vector.memset(XT[:], 0.0))
                kit.dve(nc.vector.memset(XT[:].rearrange("p j t -> p (j t)")[:, 0::C + 1], 1.0))
                nc.vector.memset(inv[:], 0.0)
                dve.wait_ge(loaded.sem, l0 + 16)
                for t in range(1, C):
                    kit.dve(nc.vector.tensor_tensor(terms[:, 0:t, 0:t], XT[:, 0:t, 0:t],
                                                    sy[:, 0:t, t].unsqueeze(1).to_broadcast([P, t, t]), ALU.mult))
                    ins = nc.vector.tensor_reduce(XT[:, 0:t, t], terms[:, 0:t, 0:t], AX, ALU.add)
                    if t < C - 1:
                        kit.dve(ins)
                    else:
                        solved.up(ins)


def recur(kit, T, R, K, V, A, KK, PC, inv, S):
    nc = kit.nc
    KT = kit.hT[:].rearrange("p a n -> p (a n)")[:, 0:KD * P].rearrange("p (a n) -> p a n", n=P)
    BT = kit.hT[:].rearrange("p a n -> p (a n)")[:, KD * P:].rearrange("p (a n) -> p a n", n=P)
    Q, U = kit.h[:, 0], kit.h[:, 1]
    with kit.sb("arT", [P, KD, 2, P]) as arT, kit.sb("GK", [P, RH, 2 * P]) as GK, kit.sb("GB", [P, RH, P]) as GB, \
            kit.sb("W1T", [P, KD, P]) as W1T, kit.sb("W2", [P, D]) as W2:
        flat = arT[:].rearrange("p k s t -> p (k s) t")
        jobs = []
        for k in range(0, KD, 2):
            jobs.append(([s[:, T, (k + i) * P:(k + i + 1) * P] for i in range(2) for s in (KK, R)], flat[:, 2 * k:2 * k + 4]))
        for src, dst in ((K, KT), (A, BT)):
            for k in (0, 4):
                jobs.append(([src[:, T, (k + i) * P:(k + i + 1) * P] for i in range(4)], dst[:, k:k + 4]))
        transposes(kit, jobs)
        place = lambda hh: (slice(hh % 2 * HD, (hh % 2 + 1) * HD), hh // 2)
        cols = lambda hh: slice(hh * HD, (hh + 1) * HD)
        parity = lambda a, i: a.rearrange("p (a b d) -> p a b d", b=2, d=HD)[:, :, i]

        grams, masked = kit.count("grams"), kit.count("grams_masked")
        g0, m0 = grams.n, masked.n
        with nc.Block() as block:
            @block.tensor
            def _(pe):
                for n in range(KD):
                    if n >= 4:
                        pe.wait_ge(masked.sem, m0 + n - 3)
                    r, _ = place(n % 2)
                    for i in range(2):
                        p = n // 2 * 2 + i
                        mm = nc.tensor.matmul(kit.bank[n % 4][:, i * BLK:(i + 1) * BLK], KT[r, p, :],
                                              arT[r, p].rearrange("p s t -> p (s t)"), start=True, stop=True)
                    grams.up(mm)
                for n in range(4):
                    r, _ = place(n % 2)
                    for i in range(4):
                        p = n // 2 * 4 + i
                        mm = nc.tensor.matmul(kit.bank[4 + n][:, i * P:(i + 1) * P], BT[r, p, :], arT[r, p, 1, :],
                                              start=True, stop=True)
                    grams.up(mm)

            @block.vector
            def _(dve):
                for p in range(KD):
                    dve.wait_ge(grams.sem, g0 + p + 1)
                    u = p // 2 * 4 + p % 2
                    masked.up(nc.vector.tensor_tensor(GK[:, u:u + 3:2], kit.bank[p % 4][:, :].rearrange(
                        "p (a t) -> p a t", a=2), kit.ltle.unsqueeze(1).to_broadcast([P, 2, 2 * P]), ALU.mult))
                for n in range(4):
                    dve.wait_ge(grams.sem, g0 + KD + n + 1)
                    u = n // 2 * 8 + n % 2
                    nc.vector.tensor_tensor(GB[:, u:u + 7:2], kit.bank[4 + n][:, :].rearrange(
                        "p (a t) -> p a t", a=4), kit.le.unsqueeze(1).to_broadcast([P, 4, P]), ALU.mult)

        made, copied = kit.count("within_made"), kit.count("within_copied")
        d0, c0 = made.n, copied.n
        with nc.Block() as block:
            @block.tensor
            def _(pe):
                for hh in range(RH):
                    mm = nc.tensor.matmul(kit.bank[hh // 8][:, hh % 8 * HD:(hh % 8 + 1) * HD], GK[:, hh, 0:P],
                                          V[:, T, cols(hh)], start=True, stop=True)
                made.up(mm)
                for hh in range(RH):
                    r, p = place(hh)
                    mm = nc.tensor.matmul(kit.bank[2 + p // 4][r, p % 4 * P:(p % 4 + 1) * P], KK[:, T, cols(hh)],
                                          inv[:, T * RH + hh, :], start=True, stop=True)
                made.up(mm)
                pe.wait_ge(copied.sem, c0 + 2)
                for hh in range(RH):
                    mm = nc.tensor.matmul(kit.bank[4 + hh // 8][:, hh % 8 * HD:(hh % 8 + 1) * HD],
                                          inv[:, T * RH + hh, :], Q[:, cols(hh)], start=True, stop=True)
                made.up(mm)

            @block.scalar
            def _(act):
                act.wait_ge(made.sem, d0 + 1)
                for i in range(2):
                    copied.up(nc.scalar.copy(Q[:, i * 512:(i + 1) * 512], kit.bank[i][:, :]))
                act.wait_ge(made.sem, d0 + 2)
                for i in range(2):
                    nc.scalar.copy(W1T[:, 4 * i:4 * i + 4], kit.bank[2 + i][:, :].rearrange("p (a t) -> p a t", a=4))

            @block.vector
            def _(dve):
                nc.vector.tensor_copy(S[:, 0], S[:, CH])
                dve.wait_ge(made.sem, d0 + 3)
                for i in range(2):
                    nc.vector.tensor_copy(W2[:, i * 512:(i + 1) * 512], kit.bank[4 + i][:, :])

        read, filled, keyed, written, grown, shown = (kit.count(n) for n in (
            "state_read", "u_filled", "key_products", "state_products", "state_grown", "state_shown"))
        e0, f0, k0, w0, n0, o0, y0 = read.n, filled.n, keyed.n, written.n, grown.n, shown.n, made.n
        with nc.Block() as block:
            @block.tensor
            def _(pe):
                for c in range(CH):
                    t = slice(c * C, (c + 1) * C)
                    if c:
                        pe.wait_ge(grown.sem, n0 + c)
                    for hh in range(RH):
                        r, p = place(hh)
                        mm = nc.tensor.matmul(kit.bank[hh % 2][t, cols(p)], W1T[r, p, t],
                                              S[r, c, p, :], start=True, stop=True)
                    read.up(mm)
                    for hh in range(RH):
                        r, p = place(hh)
                        mm = nc.tensor.matmul(kit.bank[3][r, p * HD:(p + 1) * HD], K[t, T, cols(hh)], V[t, T, cols(hh)],
                                              start=True, stop=True, tile_position=(c * C, hh % 2 * HD))
                    keyed.up(mm)
                    pe.wait_ge(filled.sem, f0 + 2 * c + 2)
                    for hh in range(RH):
                        r, p = place(hh)
                        mm = nc.tensor.matmul(kit.bank[2][r, p * HD:(p + 1) * HD], A[t, T, cols(hh)], U[t, cols(hh)],
                                              start=True, stop=True, tile_position=(c * C, hh % 2 * HD))
                    written.up(mm)
                    for hh in range(RH):
                        r, p = place(hh)
                        mm = nc.tensor.matmul(kit.bank[4 + hh % 2][t, cols(p)], arT[r, p, 1, t], S[r, c, p, :],
                                              start=True, stop=True)
                shown.up(mm)
                for hh in range(RH):
                    o = kit.bank[6 + hh // 8][:, hh % 8 * HD:(hh % 8 + 1) * HD]
                    nc.tensor.matmul(o, GK[:, hh, P:2 * P], V[:, T, cols(hh)], start=True, stop=False)
                    mm = nc.tensor.matmul(o, GB[:, hh, :], U[:, cols(hh)], start=False, stop=True)
                    if hh % 8 == 7:
                        made.up(mm)

            @block.vector
            def _(dve):
                for c in range(CH):
                    t = slice(c * C, (c + 1) * C)
                    dve.wait_ge(read.sem, e0 + c + 1)
                    for i in range(2):
                        filled.up(nc.vector.tensor_tensor(parity(U, i)[t], heads(kit.bank[i][:, :])[t],
                                                          parity(W2[:], i)[t], ALU.add))
                    by_head = lambda b: kit.bank[b][:, :].rearrange("p (a v) -> p a v", v=HD)
                    dve.wait_ge(keyed.sem, k0 + c + 1)
                    kit.dve(nc.vector.tensor_tensor(S[:, c + 1], by_head(3), S[:, c], ALU.add))
                    dve.wait_ge(written.sem, w0 + c + 1)
                    kit.dve(nc.vector.tensor_tensor(S[:, c + 1], by_head(2), S[:, c + 1], ALU.add))
                    grown.up(nc.vector.tensor_tensor(S[:, c + 1], S[:, c + 1], wide(PC[:, :, T, c]), ALU.mult))
                dve.wait_ge(shown.sem, o0 + 1)
                for i in range(2):
                    ins = nc.vector.tensor_copy(parity(R[:, T], i), heads(kit.bank[4 + i][:, :]))
                kit.dve(ins)
                for i in range(2):
                    dve.wait_ge(made.sem, y0 + i + 1)
                    v = R[:, T, i * 512:(i + 1) * 512]
                    nc.vector.tensor_tensor(v, v, kit.bank[6 + i][:, :], ALU.add)


def finish_mix(kit, dram, R, V, G, bonus):
    nc = kit.nc
    with kit.sb("ln", [P, 2, D]) as ln, kit.sb("sq", [P, D]) as sq, kit.sb("st", [P, 4, RH]) as st:
        loaded = kit.count("loaded")
        l0 = loaded.n

        def body(dve):
            for T in range(NT):
                y, v = R[:, T], V[:, T]
                kit.dve(nc.vector.tensor_reduce(st[:, 0], heads(y), AX, ALU.add))
                kit.dve(nc.vector.tensor_scalar(st[:, 0], st[:, 0], 1.0 / HD, None, ALU.mult))
                kit.dve(nc.vector.tensor_tensor(heads(y), heads(y), wide(st[:, 0]), ALU.subtract))
                kit.dve(nc.vector.tensor_tensor(sq[:], y, y, ALU.mult))
                kit.dve(nc.vector.tensor_reduce(st[:, 1], heads(sq[:]), AX, ALU.add))
                kit.rsqrt(dve, nc.vector.tensor_scalar(st[:, 2], st[:, 1], 1.0 / HD, GN_EPS, ALU.mult, ALU.add), st[:, 3], st[:, 3])
                kit.dve(nc.vector.tensor_tensor(heads(y), heads(y), wide(st[:, 3]), ALU.mult))
                if T == 0:
                    dve.wait_ge(loaded.sem, l0 + 32)
                kit.dve(nc.vector.tensor_tensor(y, y, ln[:, 0], ALU.mult))
                kit.dve(nc.vector.tensor_tensor(y, y, ln[:, 1], ALU.add))
                kit.dve(nc.vector.tensor_tensor(heads(v), heads(v), wide(bonus[:, T]), ALU.mult))
                kit.dve(nc.vector.tensor_tensor(y, y, v, ALU.add))
                kit.dve(nc.vector.tensor_tensor(y, y, G[:, T], ALU.mult))
        vector_only(kit, body, roots=[(st[:, 3], st[:, 2])] * NT,
                    load=[(ln[:, 0], bcast(dram["rw_lnx_g_2"], D)), (ln[:, 1], bcast(dram["rw_lnx_b_2"], D))])

    def add(b, bank):
        c = slice(b * BLK, (b + 1) * BLK)
        return nc.vector.tensor_tensor(kit.x[:, :, c], kit.x[:, :, c], bank, ALU.add)
    linear_split(kit, R, 4, False, add, on_dve=True)



def plan_weights(W, dram):
    W.add(columns(dram["mod_w"][0]))
    W.add(columns(dram["attn_in_w"][0]))
    W.add(columns(dram["attn_out_w"][0]))
    W.add(columns(dram["peer_w_q"][0]))
    W.add(columns(dram["mod_w"][1]))
    W.add([dram["pool_w"].rearrange("e g (k p) n -> p (e g k) n", p=P)])
    W.add(columns(dram["peer_w_q"][1]))
    W.add(ffn_blocks(dram, 0, 0))
    W.add(columns(dram["attn_w_in_2"][0]))
    wo = dram["attn_w_out_2"][0].rearrange("(k p) n -> p k n", p=P)
    W.add([wo[:, :, 0:512], wo[:, :, 512:1024]])
    W.add(ffn_blocks(dram, 0, 1))
    W.add(ffn_blocks(dram, 1, 0))
    for n in ("rw_wr_2", "rw_wk_2", "rw_wv_2"):
        W.add(columns(dram[n][0]))
    W.add(columns(dram["rw_wo_2"][0]))
    W.add(ffn_blocks(dram, 1, 1))


def build(nc, dram, out):
    kit = Kit(nc, dram)
    kit.x = nc.alloc_sbuf_tensor("x_res", [P, NT, D], F32)
    kit.h = nc.alloc_sbuf_tensor("h", [P, NT, D], F32)
    kit.hT = nc.alloc_sbuf_tensor("hT", [P, KD, SEQ], F32)
    kit.ones = nc.alloc_sbuf_tensor("ones", [P, P], F32)
    kit.zeros = nc.alloc_sbuf_tensor("zeros", [1, 512], F32)
    kit.eps = nc.alloc_sbuf_tensor("eps", [P, 1], F32)[:]
    kit.spare = nc.alloc_sbuf_tensor("spare8", [P, GRING], F32)
    kit.consts = nc.alloc_sbuf_tensor("const_table", [P, sum(n for _, n in CONST_PARTS)], F32)
    at = {}
    o = 0
    for name, n in CONST_PARTS:
        at[name] = kit.consts[:, o:o + n]
        if name == "lt":
            kit.ltle = kit.consts[:, o:o + 2 * P]
        o += n
    kit.ident, kit.after, kit.lt, kit.le, kit.ends, kit.iota16 = (at[n] for n in ("ident", "after", "lt", "le", "ends", "iota16"))
    kit.strict = at["strict"].rearrange("p (t n) -> p t n", t=NT)
    kit.window = at["window"].rearrange("p (t n) -> p t n", t=NT)
    kit.cos = at["cos"].rearrange("p (t n) -> p t n", t=NT)
    kit.sin = at["sin"].rearrange("p (t n) -> p t n", t=NT)
    kit.weights = Weights(kit)
    plan_weights(kit.weights, dram)

    load_constants(kit, dram)
    with kit.sb("mod", [P, N_MOD * D]) as mod:
        with kit.sb("mod_ctx", [P, 2 * D]) as mod_ctx:
            modulation(kit, dram, 0, mod, mod_ctx)
            mixer(kit, dram, mod, mod_ctx)
        peer(kit, dram, 0, mod, True)
        pooling(kit, dram, mod)
        peer(kit, dram, 1, mod, False)
    norm_plain(kit, kit.x, dram["final_g"].rearrange("(a d) -> a d", a=1), kit.x)
    swiglu(kit, dram, 0, 0)
    parallel_attention(kit, dram)
    swiglu(kit, dram, 0, 1)
    swiglu(kit, dram, 1, 0)
    time_mix(kit, dram)
    swiglu(kit, dram, 1, 1)
    stored = kit.count("stored")
    with nc.Block() as block:
        @block.sync
        def _(sp):
            stored.up(sp.dma_start(out.rearrange("a (t p) d -> p (a t) d", p=P), kit.x[:]), 16)
            sp.wait_ge(stored.sem, 16)


INPUTS = ["x", "c", "ctx", "c_ctx", "mod_w", "mod_b", "norm1_g", "norm2_g", "attn_in_w", "attn_out_w", "attn_sink",
          "gmlp_w_s", "gmlp_b_s", "pool_w", "pool_scale", "peer_w_q", "peer_sub_keys", "peer_down", "peer_up", "final_g",
          "ffn_norm_2", "ffn_w_gate_2", "ffn_w_up_2", "ffn_w_down_2", "mix_norm_2", "rel_bias_2", "attn_w_in_2",
          "attn_q_norm_2", "attn_k_norm_2", "attn_w_out_2", "rw_mix_2", "rw_w0_2", "rw_w1_2", "rw_w2_2", "rw_a0_2",
          "rw_a1_2", "rw_a2_2", "rw_g1_2", "rw_g2_2", "rw_kk_2", "rw_ka_2", "rw_rk_2", "rw_wr_2", "rw_wk_2", "rw_wv_2",
          "rw_wo_2", "rw_lnx_g_2", "rw_lnx_b_2"]


def kernel(**inputs):
    import numpy as _np
    import concourse.bacc as _bacc
    from concourse.bass_utils import run_bass_kernel_spmd as _run

    nc = _bacc.Bacc("TRN2", target_bir_lowering=False, num_devices=1)
    arrays, dram = {}, {}
    for name in INPUTS:
        a = _np.ascontiguousarray(inputs[name])
        arrays[f"in_{name}"] = a
        dram[name] = nc.dram_tensor(f"in_{name}", a.shape, mybir.dt.from_np(a.dtype), kind="ExternalInput").ap()
    for name, a in layout_constants().items():
        arrays[f"in_{name}"] = a
        dram[name] = nc.dram_tensor(f"in_{name}", a.shape, F32, kind="ExternalInput").ap()
    for name, shape in (("bias_scratch", (DIL_HEADS, 512)), ("systems", (P, C * C)), ("inverses", (P, C * C))):
        dram[name] = nc.dram_tensor(name, shape, F32, kind="Internal").ap()
    out = nc.dram_tensor("out_0", (1, SEQ, D), F32, kind="ExternalOutput").ap()
    build(nc, dram, out)
    r = _run(nc, [arrays], core_ids=[0])
    return r.results[0]["out_0"]
```
